# Optimizing a Trainium2 kernel written in Bass

```python
import math
import jax, jax.numpy as jnp
from jax import lax
import numpy as np

D_MODEL = 2048
BATCH = 1
SEQ = 256
DEPTH = 1
DEC_BATCH = 8
DEC_SEQ = 1
PAST_LEN = 2048
PAGE_SIZE = 128

HEAD_DIM = 64
ATTN_WIDTH = D_MODEL // 2
N_HEADS = ATTN_WIDTH // HEAD_DIM
N_KV_HEADS = N_HEADS // 4
GROUP = N_HEADS // N_KV_HEADS
Q_DIM = N_HEADS * HEAD_DIM
KV_DIM = N_KV_HEADS * HEAD_DIM
CONV_DIM = D_MODEL - ATTN_WIDTH
CONV_WIDTH = 3
MIX_DIM = Q_DIM + CONV_DIM
IN_DIM = Q_DIM + 2 * KV_DIM + 3 * CONV_DIM
WINDOW = 128
BLOCK = 128
NUM_BUCKETS = 32
MAX_DISTANCE = 128
N_META = 16
D_FF = ((8 * D_MODEL // 3 + 255) // 256) * 256
RMS_EPS = 1e-6
SCALE = HEAD_DIM ** -0.5

kernel_name = "hymba_swa_shortconv_step"

def rms_norm(x, g):
    xf = x.astype(jnp.float32)
    y = xf * lax.rsqrt(jnp.mean(xf * xf, axis=-1, keepdims=True) + RMS_EPS)
    return (y * g.astype(jnp.float32)).astype(x.dtype)

def t5_bucket(d):
    max_exact = NUM_BUCKETS // 2
    df = jnp.maximum(d, 1).astype(jnp.float32)
    large = max_exact + (jnp.log(df / max_exact) / math.log(MAX_DISTANCE / max_exact)
                         * (NUM_BUCKETS - max_exact)).astype(jnp.int32)
    large = jnp.minimum(large, NUM_BUCKETS - 1)
    return jnp.where(d < max_exact, d, large)

def rel_bias_lookup(table, d):
    b = table[t5_bucket(jnp.maximum(d, 0))]
    return jnp.transpose(b, (2, 0, 1)).reshape(N_KV_HEADS, GROUP, *d.shape).astype(jnp.float32)

def sink_softmax(s, sink):
    sk = sink.astype(jnp.float32).reshape(N_KV_HEADS, GROUP)[:, :, None, None]
    m = jnp.maximum(jnp.max(s, axis=-1, keepdims=True), sk)
    e = jnp.exp(s - m)
    return e / (jnp.sum(e, axis=-1, keepdims=True) + jnp.exp(sk - m))

def split_proj(z):
    o1 = Q_DIM
    o2 = o1 + KV_DIM
    o3 = o2 + KV_DIM
    o4 = o3 + CONV_DIM
    o5 = o4 + CONV_DIM
    return jnp.split(z, [o1, o2, o3, o4, o5], axis=-1)

def band_pattern(L):
    pad = (-L) % BLOCK
    nb = (L + pad) // BLOCK
    i = jnp.arange(BLOCK)[:, None]
    j = jnp.arange(2 * BLOCK)[None, :]
    d = BLOCK + i - j
    n = jnp.arange(nb)[:, None, None]
    k_abs = (n - 1) * BLOCK + j
    mask = (d >= 0) & (d <= WINDOW) & (k_abs >= pad)
    return d, mask

def swa_prompt(q, k, v, sink, bias, mask):
    B, L = q.shape[:2]
    pad = (-L) % BLOCK
    nb = (L + pad) // BLOCK
    qp = (jnp.pad(q, ((0, 0), (pad, 0), (0, 0))) * SCALE).reshape(
        B, nb, BLOCK, N_KV_HEADS, GROUP, HEAD_DIM)

    def band(t):
        tp = jnp.pad(t, ((0, 0), (pad, 0), (0, 0))).reshape(B, nb, BLOCK, N_KV_HEADS, HEAD_DIM)
        prev = jnp.pad(tp[:, :-1], ((0, 0), (1, 0), (0, 0), (0, 0), (0, 0)))
        return jnp.concatenate([prev, tp], axis=2)

    kk, vv = band(k), band(v)
    s = jnp.einsum('bnqkgd,bnskd->bnkgqs', qp, kk).astype(jnp.float32) + bias
    s = jnp.where(mask[None, :, None, None], s, -jnp.inf)
    p = sink_softmax(s, sink).astype(v.dtype)
    o = jnp.einsum('bnkgqs,bnskd->bnqkgd', p, vv).reshape(B, nb * BLOCK, Q_DIM)
    return o[:, pad:]

def swa_sample(q, k, v, kbuf, vbuf, sink, table):
    DB, T = q.shape[:2]
    WB = kbuf.shape[1]
    qs = (q * SCALE).reshape(DB, T, N_KV_HEADS, GROUP, HEAD_DIM)
    kk = jnp.concatenate([kbuf.astype(k.dtype), k.reshape(DB, T, N_KV_HEADS, HEAD_DIM)], axis=1)
    vv = jnp.concatenate([vbuf.astype(v.dtype), v.reshape(DB, T, N_KV_HEADS, HEAD_DIM)], axis=1)
    d = (WB + jnp.arange(T))[:, None] - jnp.arange(WB + T)[None, :]
    mask = (d >= 0) & (d <= WINDOW)
    s = jnp.einsum('btkgd,bskd->bkgts', qs, kk).astype(jnp.float32) + rel_bias_lookup(table, d)
    s = jnp.where(mask, s, -jnp.inf)
    p = sink_softmax(s, sink).astype(v.dtype)
    o = jnp.einsum('bkgts,bskd->btkgd', p, vv).reshape(DB, T, Q_DIM)
    return o, kk[:, -WB:], vv[:, -WB:]

def causal_conv(u_ext, w, T):
    return sum(w[i] * u_ext[:, i:i + T] for i in range(CONV_WIDTH))

def swiglu(x, wg, wu, wd):
    return (jax.nn.silu(x @ wg) * (x @ wu)) @ wd

def setup_inputs(seed: int = 0) -> dict:
    key = jax.random.key(seed)
    ks = jax.random.split(key, 20)
    W_BUF = min(WINDOW, PAST_LEN)
    nrm = jax.random.normal
    return {
        "x_prompt": nrm(ks[0], (BATCH, SEQ, D_MODEL), jnp.float32),
        "x_sample": nrm(ks[1], (DEC_BATCH, DEC_SEQ, D_MODEL), jnp.float32),
        "cache_k": nrm(ks[2], (DEPTH, DEC_BATCH, W_BUF, N_KV_HEADS, HEAD_DIM), jnp.float32),
        "cache_v": nrm(ks[3], (DEPTH, DEC_BATCH, W_BUF, N_KV_HEADS, HEAD_DIM), jnp.float32),
        "state_conv": nrm(ks[4], (DEPTH, DEC_BATCH, CONV_WIDTH - 1, CONV_DIM), jnp.float32),
        "meta_tokens": nrm(ks[5], (N_META, D_MODEL), jnp.float32),
        "rel_bias": 0.5 * nrm(ks[6], (NUM_BUCKETS, N_HEADS), jnp.float32),
        "w_in": nrm(ks[7], (DEPTH, D_MODEL, IN_DIM), jnp.float32) * D_MODEL ** -0.5,
        "conv_w": nrm(ks[8], (DEPTH, CONV_WIDTH, CONV_DIM), jnp.float32) * CONV_WIDTH ** -0.5,
        "attn_sinks": nrm(ks[9], (DEPTH, N_HEADS), jnp.float32),
        "w_out": nrm(ks[10], (DEPTH, MIX_DIM, D_MODEL), jnp.float32) * MIX_DIM ** -0.5,
        "norm_pre_mix": 1.0 + 0.05 * nrm(ks[11], (DEPTH, D_MODEL), jnp.float32),
        "norm_post_mix": 1.0 + 0.05 * nrm(ks[12], (DEPTH, D_MODEL), jnp.float32),
        "norm_pre_ffn": 1.0 + 0.05 * nrm(ks[13], (DEPTH, D_MODEL), jnp.float32),
        "norm_post_ffn": 1.0 + 0.05 * nrm(ks[14], (DEPTH, D_MODEL), jnp.float32),
        "w_gate": nrm(ks[15], (DEPTH, D_MODEL, D_FF), jnp.float32) * D_MODEL ** -0.5,
        "w_up": nrm(ks[16], (DEPTH, D_MODEL, D_FF), jnp.float32) * D_MODEL ** -0.5,
        "w_down": nrm(ks[17], (DEPTH, D_FF, D_MODEL), jnp.float32) * D_FF ** -0.5,
    }

def reference(x_prompt, x_sample, cache_k, cache_v, state_conv, meta_tokens, rel_bias,
              w_in, conv_w, attn_sinks, w_out, norm_pre_mix, norm_post_mix,
              norm_pre_ffn, norm_post_ffn, w_gate, w_up, w_down):
    B = x_prompt.shape[0]
    meta = jnp.broadcast_to(meta_tokens[None].astype(x_prompt.dtype), (B, N_META, D_MODEL))
    hp = jnp.concatenate([meta, x_prompt], axis=1)
    hs = x_sample
    L = hp.shape[1]
    T = hs.shape[1]
    d_band, mask_band = band_pattern(L)
    bias_band = rel_bias_lookup(rel_bias, d_band)

    kp_l, vp_l, cp_l, ks_l, vs_l, cs_l = [], [], [], [], [], []
    for l in range(DEPTH):
        xn = rms_norm(hp, norm_pre_mix[l])
        q, k, v, gb, gc, hc = split_proj(xn @ w_in[l])
        a = swa_prompt(q, k, v, attn_sinks[l], bias_band, mask_band)
        u = gc * hc
        u_ext = jnp.pad(u, ((0, 0), (CONV_WIDTH - 1, 0), (0, 0)))
        c = gb * causal_conv(u_ext, conv_w[l], L)
        mix = jnp.concatenate([a, c], axis=-1) @ w_out[l]
        hp = hp + rms_norm(mix, norm_post_mix[l])
        kp_l.append(k.reshape(B, L, N_KV_HEADS, HEAD_DIM)[:, -WINDOW:])
        vp_l.append(v.reshape(B, L, N_KV_HEADS, HEAD_DIM)[:, -WINDOW:])
        cp_l.append(u[:, -(CONV_WIDTH - 1):])
        hp = hp + rms_norm(swiglu(rms_norm(hp, norm_pre_ffn[l]), w_gate[l], w_up[l], w_down[l]),
                           norm_post_ffn[l])

        xn = rms_norm(hs, norm_pre_mix[l])
        q, k, v, gb, gc, hc = split_proj(xn @ w_in[l])
        a, kb_new, vb_new = swa_sample(q, k, v, cache_k[l], cache_v[l], attn_sinks[l], rel_bias)
        u = gc * hc
        u_ext = jnp.concatenate([state_conv[l].astype(u.dtype), u], axis=1)
        c = gb * causal_conv(u_ext, conv_w[l], T)
        mix = jnp.concatenate([a, c], axis=-1) @ w_out[l]
        hs = hs + rms_norm(mix, norm_post_mix[l])
        ks_l.append(kb_new)
        vs_l.append(vb_new)
        cs_l.append(u_ext[:, -(CONV_WIDTH - 1):])
        hs = hs + rms_norm(swiglu(rms_norm(hs, norm_pre_ffn[l]), w_gate[l], w_up[l], w_down[l]),
                           norm_post_ffn[l])

    y_prompt = hp[:, N_META:]
    y_sample = hs
    k_prompt = jnp.stack(kp_l)
    v_prompt = jnp.stack(vp_l)
    conv_prompt = jnp.stack(cp_l)
    k_sample = jnp.stack(ks_l)
    v_sample = jnp.stack(vs_l)
    conv_sample = jnp.stack(cs_l)
    return (y_prompt, y_sample, k_prompt, v_prompt, conv_prompt, k_sample, v_sample, conv_sample)


_drawn_inputs = setup_inputs


def setup_inputs(seed=0):
    import zlib

    import numpy as np

    out = dict(_drawn_inputs(seed))
    spreads = {}
    factors = {'attn_sinks': 8.0}
    for name, (base, spread) in spreads.items():
        noise = np.random.default_rng([zlib.crc32(name.encode()), seed]).standard_normal(out[name].shape)
        drawn = base * np.exp(spread * noise) if base else spread * noise
        out[name] = __import__('jax').numpy.asarray(drawn.astype(out[name].dtype))
    for name, factor in factors.items():
        out[name] = (out[name] * factor).astype(out[name].dtype)
    return out
```

```python
from contextlib import ExitStack

import concourse.bass as bass
from concourse import mybir

F32 = mybir.dt.float32
F32R = mybir.dt.float32r
ALU = mybir.AluOpType
ACT = mybir.ActivationFunctionType
AX = mybir.AxisListType
RADD = bass.bass_isa.ReduceOp.add

P = 128
D = 2048
SEQ = 256
N_META = 16
NP = SEQ + N_META
ND = 8
N = NP + ND
HEAD = 64
HEADS = 16
KVH = 4
GROUP = HEADS // KVH
WINDOW = 128
CONV = 1024
BUCKETS = 32
FF = 5632
IN = 4608
EPS = 1e-6
MASKED = -1e30

KT = D // P
FT = FF // P
CT = CONV // P
RING = 4
NA = 3
NB = 4
ORDER = [4, 5, 6, 0, 1, 2, 3, 7]
NC = len(ORDER)
DC = FT // 2
K_ORDER = [2 * c + j for c in ORDER for j in range(2)]
K_ORDER = [2 * c + j for c in ORDER for j in range(2)]
K_ORDER = [2 * c + j for c in ORDER for j in range(2)]
K_ORDER = [2 * c + j for c in ORDER for j in range(2)]
K_ORDER = [2 * c + j for c in ORDER for j in range(2)]
K_ORDER = [2 * c + j for c in ORDER for j in range(2)]
K_ORDER = [2 * c + j for c in ORDER for j in range(2)]
K_ORDER = [2 * c + j for c in ORDER for j in range(2)]
QKV_TURNS = 2
CONV_TURNS = 4
FF_TURNS = FT // NB
C_QKV = 0
C_CONV = C_QKV + QKV_TURNS * 2 * NC
C_OUT = C_CONV + CONV_TURNS * 2 * NC
C_FF = C_OUT + 4 * NC
C_DOWN = C_FF + FF_TURNS * 2 * NC
C_END = C_DOWN + 4 * DC
BLOCKS = [(0, 128), (128, 128), (256, N - 256)]
V_PRE_MIX, V_POST_MIX, V_PRE_FFN, V_POST_FFN, V_CONV = 0, KT, 2 * KT, 3 * KT, 4 * KT
NVEC = V_CONV + 3 * CT
EXT = NP + 2 + 3 * ND
BIAS_N = 384


def mixer_kernel(nc, x_prompt, x_sample, cache_k, cache_v, state_conv, meta_tokens, rel_bias, w_in,
                 conv_w, attn_sinks, w_out, norm_pre_mix, norm_post_mix, norm_pre_ffn,
                 norm_post_ffn, w_gate, w_up, w_down, squares, onehot, row_masks,
                 y_prompt, y_sample, k_prompt, v_prompt, conv_prompt, k_sample, v_sample,
                 conv_sample, bias_rows):
    with ExitStack() as ctx:
        def sem(name):
            return ctx.enter_context(nc.semaphore(name))

        def place(name, shape, start, dt=F32):
            size = 4
            for s in shape[1:]:
                size *= s
            end = start + -(-size // 32) * 32
            assert end <= nc.sbuf_usable_end, (name, end)
            return nc.alloc_sbuf_tensor_at(name, shape, dt, offset=start), end

        e = -(-nc.sbuf_base // 32) * 32
        ident, e = place("ident", [P, P], e)
        ones, e = place("ones", [P, P], e)
        vec, e = place("vec", [P, NVEC], e)
        rstd, e = place("rstd", [P, N], e)
        stat3, e = place("stat3", [P, 8], e)
        resid, operand = place("resid", [P, KT, N], e)
        op_hi, e = place("op_hi", [P, KT, N], operand, F32R)
        op_lo, e = place("op_lo", [P, KT, N], e, F32R)
        raw, e = place("raw", [P, RING, 2, 512], e)
        w_hi, e = place("w_hi", [P, RING, 1024], e, F32R)
        w_lo, area = place("w_lo", [P, RING, 1024], e, F32R)
        h_hi, e = place("h_hi", [P, FT, N], area, F32R)
        h_lo, e = place("h_lo", [P, FT, N], e, F32R)
        gate, e = place("gate", [P, NB, N], e)
        up, keep = place("up", [P, NB, N], e)
        kv_rows, e = place("kv_rows", [P, 4 * P], keep)
        kv_dec, e = place("kv_dec", [ND, 4 * P], e)
        conv_rows, e = place("conv_rows", [2 + ND, CONV], e)
        yT, yT_end = place("yT", [P, KT, N], operand)
        y_sq, e = place("y_sq", [P, NB, N], yT_end)
        y_acc, e = place("y_acc", [P, NB, N], e)
        y_diag, e = place("y_diag", [P, 3, P], e)
        y_tmp, e = place("y_tmp", [P, 2, N], e)
        rows_out, _ = place("rows_out", [P, 3, D], area)
        zT, conv_area = place("zT", [P, 12, N], area)
        convT, zb_area = place("convT", [P, CT, N], conv_area)
        zb, e = place("zb", [P, 2, NA, N], zb_area)
        after_zb = e
        bias, e = place("bias", [P, HEADS, 2 * P], e)
        bias_c, e = place("bias_c", [HEAD, KVH, 144], e)
        u_ext, e = place("u_ext", [P, EXT], e)
        tap, e = place("tap", [P, EXT - 2], e)
        acc, e = place("acc", [P, EXT - 2], e)
        cw, e = place("cw", [P, 3], e)
        state_t, e = place("state_t", [P, CT, 2 * ND], e)
        u_out, e = place("u_out", [P, CT, 2 + ND], e)
        kd, e = place("kd", [P, KVH, NP], e)
        vd, e = place("vd", [P, 3, 2 * P], e)
        sink, e = place("sink", [P, HEADS], e)
        nsink, e = place("nsink", [P, HEADS], e)
        sink_c, e = place("sink_c", [HEAD, 2 * KVH], e)
        masks, e = place("masks", [P, ND + HEADS + GROUP], e)
        vc, e = place("vc", [P, ND, 2 * P], e)
        kct, e = place("kct", [P, ND, 2, P], e)
        onehot_s, e = place("onehot_s", [BUCKETS + 1, BIAS_N], e)
        table, e = place("table", [BUCKETS + 1, HEADS], e)
        table_d, e = place("table_d", [BUCKETS + 1, ND, HEADS], e)
        flip, attn = place("flip", [P, P], e)
        rows_in, _ = place("rows_in", [P, 3, D], attn)
        hankel, e = place("hankel", [P, HEADS, 2 * P], attn)
        qs, e = place("qs", [P, GROUP, 2 * P], attn)
        qs_c, e = place("qs_c", [P, GROUP, 16], e)
        ks, e = place("ks", [P, NP], e)
        vs, e = place("vs", [P, 3, 2, HEAD], e)
        s_ab, e = place("s_ab", [P, 512 + 1024], e)
        s_c, e = place("s_c", [HEAD, 144], e)
        nmax, e = place("nmax", [P, 12], e)
        den, e = place("den", [P, 12], e)
        esk, e = place("esk", [P, 12], e)
        pt, e = place("pt", [P, 3, 512], e)
        pt_c, e = place("pt_c", [P, 2, HEAD], e)
        qd, e = place("qd", [P, 2, ND, 2 * GROUP], e)
        sd, e = place("sd", [P, P + 1], e)
        sd_own8, e = place("sd_own8", [P, ND], e)
        sdt, e = place("sdt", [P, P], e)
        sd_own, e = place("sd_own", [ND, P], e)
        pd, e = place("pd", [P, P], e)
        pd_own, e = place("pd_own", [ND, P], e)
        dstat, e = place("dstat", [P, 8], e)
        sinks_m, e = place("sinks_m", [P, HEADS], e)
        assert e <= keep
        kc, _ = place("kc", [P, ND, 2 * P], conv_area)
        vec_rows, e = place("vec_rows", [NVEC, P], zb_area)
        state_rows, e = place("state_rows", [2 * ND, CONV], e)
        bias_sb, e = place("bias_sb", [HEADS, BIAS_N], e)
        assert e <= after_zb
        mixT, e = place("mixT", [P, KT, N], after_zb)
        assert e <= after_zb + (HEADS * 2 * P + KVH * 144) * 4, "mixT lies over the bias"
        sq, e = place("sq", [P, NB, N], attn)
        acc4, e = place("acc4", [P, NB, N], e)
        diag, e = place("diag", [P, 3, P], e)
        tmp, e = place("tmp", [P, 2, N], e)
        x_diag, _ = place("x_diag", [P, 3, P], after_zb)

        ps = ctx.enter_context(nc.psum_tensor("ps", [P, 8, 512], F32))

        raw_landed = [sem(f"raw_landed{s}") for s in range(RING)]
        hi_ready = sem("hi_ready")
        lo_ready = sem("lo_ready")
        chunk_used = sem("chunk_used")
        x_in, const_in, vec_in, table_in = sem("x_in"), sem("const_in"), sem("vec_in"), sem("table_in")
        kcache_in, state_in, sink_in, vcache_in = sem("kcache_in"), sem("state_in"), sem("sink_in"), sem("vcache_in")
        filled = sem("filled")
        vec_done, vec_out, table_d_ready = sem("vec_done"), sem("vec_out"), sem("table_d_ready")
        rel_done, rel_out, rel_stored, hankel_in = sem("rel_done"), sem("rel_out"), sem("rel_stored"), sem("hankel_in")
        xt_done, xt_out, x_squared = sem("xt_done"), sem("xt_out"), sem("x_squared")
        op_hi_ready, op_lo_ready = sem("op_hi_ready"), sem("op_lo_ready")
        rms_ready, inv_ready, diag_ready, bcast_done = sem("rms_ready"), sem("inv_ready"), sem("diag_ready"), sem("bcast_done")
        rstd_ready = sem("rstd_ready")
        z_out = sem("z_out")
        bias_done, bias_out, bias_c_in = sem("bias_done"), sem("bias_out"), sem("bias_c_in")
        kct_done, kct_out = sem("kct_done"), sem("kct_out")
        kv_done, kv_out, kd_ready = sem("kv_done"), sem("kv_out"), sem("kd_ready")
        state_done, state_out = sem("state_done"), sem("state_out")
        zeroed, q_staged, k_staged, v_staged, qd_staged = (sem("zeroed"), sem("q_staged"), sem("k_staged"),
                                                           sem("v_staged"), sem("qd_staged"))
        scores_done, scores_out = sem("scores_done"), sem("scores_out")
        nmax_ready, exp_done, probs_ready = sem("nmax_ready"), sem("exp_done"), sem("probs_ready")
        probs_t = sem("probs_t")
        probs_t_act, probs_t_dve = sem("probs_t_act"), sem("probs_t_dve")
        pv_done, pv_act, pv_dve = sem("pv_done"), sem("pv_act"), sem("pv_dve")
        dec_scores, dec_scores_out, dec_rows, dec_rows_out = (sem("dec_scores"), sem("dec_scores_out"),
                                                              sem("dec_rows"), sem("dec_rows_out"))
        dec_nmax, dec_exp, dec_probs = sem("dec_nmax"), sem("dec_exp"), sem("dec_probs")
        dec_pt, dec_pt_out, dec_pv, dec_pv_out = sem("dec_pt"), sem("dec_pt_out"), sem("dec_pv"), sem("dec_pv_out")
        zb_ready, conv_done = sem("zb_ready"), sem("conv_done")
        mix_out, mix_acc, sq_ready, stat_done = sem("mix_out"), sem("mix_acc"), sem("sq_ready"), sem("stat_done")
        scaled, resid_ready, rsq_ready, rsum = sem("scaled"), sem("resid_ready"), sem("rsq_ready"), sem("rsum")
        tot_ready, mean_ready, root_ready, ffn_rstd = sem("tot_ready"), sem("mean_ready"), sem("root_ready"), sem("ffn_rstd")
        crow_done, crow_out = sem("crow_done"), sem("crow_out")
        gate_ready, sig_ready, swish_ready = sem("gate_ready"), sem("sig_ready"), sem("swish_ready")
        up_ready, hid_ready, hid_hi, hid_lo = sem("up_ready"), sem("hid_ready"), sem("hid_hi"), sem("hid_lo")
        y_out, y_scaled, y_ready_pool, y_ready_dve = sem("y_out"), sem("y_scaled"), sem("y_ready_pool"), sem("y_ready_dve")
        yt_done, yt_act, yt_dve = sem("yt_done"), sem("yt_act"), sem("yt_dve")
        stored = sem("stored")
        dve_own, pool_own = sem("dve_own"), sem("pool_own")

        class Own:

            def __init__(self, engine, semaphore):
                self.engine, self.semaphore, self.n, self.turn = engine, semaphore, 0, 0

            def link(self, instruction):
                instruction.then_inc(self.semaphore, 1)
                self.n += 1
                self.engine.wait_ge(self.semaphore, self.n + self.turn)

            def begin(self, turn, per_turn):
                self.turn, self.mark, self.per = turn * per_turn, self.n, per_turn

            def end(self, turns):
                assert self.n - self.mark == self.per, (self.n - self.mark, self.per)
                self.turn, self.n = 0, self.mark + turns * self.per

        def each(ap, shape):
            return ap.unsqueeze(1).broadcast_to(shape)

        def heads4(ap):
            return ap.rearrange("p (h k) -> p h k", h=GROUP)

        def at(ap, i):
            return ap[:, bass.ds(i, 1)].rearrange("p a n -> p (a n)")

        block = ctx.enter_context(nc.Block())

        @block.sync
        def _(sp):
            sp.dma_start(rows_in[0:N_META, 0, :], meta_tokens).then_inc(x_in, 16)
            sp.dma_start(rows_in[N_META:P, 0, :], x_prompt[0, 0:P - N_META, :]).then_inc(x_in, 16)
            sp.dma_start(rows_in[:, 1, :], x_prompt[0, P - N_META:2 * P - N_META, :]).then_inc(x_in, 16)
            sp.dma_start(rows_in[0:N_META, 2, :], x_prompt[0, SEQ - N_META:SEQ, :]).then_inc(x_in, 16)
            sp.dma_start(rows_in[N_META:N_META + ND, 2, :], x_sample[:, 0, :]).then_inc(x_in, 16)

            def load(n, slot, src, dst, turn=0):
                sp.wait_ge(lo_ready, n + 1 + turn)
                sp.dma_start(dst, src).then_inc(raw_landed[slot], 16)

            def rows_of(w, chunk, col, width):
                return w[chunk * 2 * P:(chunk + 1) * 2 * P, bass.ds(col, width)].rearrange(
                    "(j p) n -> p j n", p=P)

            for c in range(QKV_TURNS * 2 * NC):
                if c == RING:
                    sp.wait_ge(rel_out, 1)
                    sp.dma_start(bias_rows, bias_sb[:]).then_inc(rel_stored, 16)
                    sp.wait_ge(rel_stored, 16)
                    sp.wait_ge(xt_done, KT)
                    sp.wait_ge(x_squared, 3)
                    sp.dma_start(hankel[:], bass.AP(bias_rows.tensor, 0, [[1, P], [BIAS_N, HEADS], [1, 2 * P]])).then_inc(hankel_in, 16)
                if c == 2 * NC + RING:
                    sp.wait_ge(bias_out, HEADS // 2)
                    for h in range(GROUP):
                        sp.dma_start(bias_c[16 * h:16 * h + 16, :, :],
                                     bias[0:16, h:HEADS:GROUP, 0:144]).then_inc(bias_c_in, 16)
                load(C_QKV + c, c % RING, rows_of(w_in[0], ORDER[c % NC], 1152 - 384 * (c // NC), 384),
                     raw[:, c % RING, :, 0:384])
            parts = w_in[0][:, IN - 3 * CONV:IN].rearrange("k (a n) -> k a n", a=3)
            with sp.Fori(0, CONV_TURNS) as turn:
                for c in range(2 * NC):
                    chunk = ORDER[c % NC]
                    sp.wait_ge(lo_ready, C_CONV + c + 1 + turn * (2 * NC))
                    for j in range(2):
                        k = 2 * chunk + j
                        sp.dma_start(raw[:, c % RING, j, 0:384].rearrange("p (a n) -> p a n", a=3),
                                     parts[k * P:k * P + P, :, bass.ds(turn * (2 * P) + c // NC * P, P)]
                                     ).then_inc(raw_landed[c % RING], 16)

            def column(turn, width, k):
                return (turn + turn) * (width // 2) if k == 0 else turn * width

            with sp.Fori(0, 2) as turn:
                for c in range(2 * NC):
                    load(C_OUT + c, c % RING, rows_of(w_out[0][:, c // NC * 512:], ORDER[c % NC], column(turn, 1024, ORDER[c % NC]), 512),
                         raw[:, c % RING], turn * (2 * NC))
            sp.wait_ge(kv_out, 4)
            flat = "t h d -> t (h d)"
            sp.dma_start(k_prompt[0, 0].rearrange(flat), kv_rows[:, 0:2 * P]).then_inc(stored, 16)
            sp.dma_start(v_prompt[0, 0].rearrange(flat), kv_rows[:, 2 * P:4 * P]).then_inc(stored, 16)
            sp.dma_start(k_sample[0, :, WINDOW - 1].rearrange(flat), kv_dec[:, 0:2 * P]).then_inc(stored, 16)
            sp.dma_start(v_sample[0, :, WINDOW - 1].rearrange(flat), kv_dec[:, 2 * P:4 * P]).then_inc(stored, 16)
            for cache, out in ((cache_k, k_sample), (cache_v, v_sample)):
                for b in range(ND):
                    sp.dma_start(out[0, b, 0:WINDOW - 1].rearrange(flat),
                                 cache[0, b, 1:WINDOW].rearrange(flat)).then_inc(stored, 16)
            sp.dma_start(conv_sample[0, :, 0, :], state_conv[0, :, 1, :]).then_inc(stored, 16)
            with sp.Fori(0, FF_TURNS) as turn:
                for c in range(2 * NC):
                    w = (w_gate, w_up)[c // NC][0]
                    load(C_FF + c, c % RING, rows_of(w, ORDER[c % NC], column(turn, 512, ORDER[c % NC]), 512),
                         raw[:, c % RING], turn * (2 * NC))
            sp.wait_ge(crow_out, 1)
            sp.dma_start(conv_prompt[0, 0], conv_rows[0:2, :]).then_inc(stored, 16)
            sp.dma_start(conv_sample[0, :, 1, :], conv_rows[2:2 + ND, :]).then_inc(stored, 16)
            with sp.Fori(0, 2) as turn:
                for c in range(2 * DC):
                    load(C_DOWN + c, c % RING, rows_of(w_down[0][:, c // DC * 512:], c % DC, column(turn, 1024, c % DC), 512),
                         raw[:, c % RING], turn * (2 * DC))
            sp.wait_ge(yt_act, 6)
            sp.wait_ge(yt_dve, 6)
            sp.dma_start(y_prompt[0, 0:P - N_META, :], rows_out[N_META:P, 0, :]).then_inc(stored, 16)
            sp.dma_start(y_prompt[0, P - N_META:2 * P - N_META, :], rows_out[:, 1, :]).then_inc(stored, 16)
            sp.dma_start(y_prompt[0, SEQ - N_META:SEQ, :], rows_out[0:N_META, 2, :]).then_inc(stored, 16)
            sp.dma_start(y_sample[:, 0, :], rows_out[N_META:N_META + ND, 2, :]).then_inc(stored, 16)
            sp.wait_ge(stored, 16 * (4 + 2 * ND + 1 + 2 + 4))

        @block.tensor
        def _(pe):
            def tr(out, in_):
                n = in_.shape[0]
                return nc.tensor.transpose(out, in_, ident[0:n, 0:n])

            def chunk(slot, tiles, bank, k0, moving_hi, moving_lo, first, last):
                for m in range(tiles):
                    for j in range(2):
                        col = (j * tiles + m) * P
                        hi, lo = w_hi[:, slot, col:col + P], w_lo[:, slot, col:col + P]
                        for i, (w, x) in enumerate(((hi, moving_hi), (hi, moving_lo), (lo, moving_hi))):
                            mm = nc.tensor.matmul(ps[:, bank + m, 0:N], w, x[:, k0 + j, :],
                                                  start=first and j == 0 and i == 0,
                                                  stop=last and j == 1 and i == 2)
                return mm

            def project(n, c, slot, tiles, bank, turn=0):
                pe.wait_ge(lo_ready, RING + n + 1 + turn)
                mm = chunk(slot, tiles, bank, 2 * ORDER[c], op_hi, op_lo, c == 0, c == NC - 1)
                mm.then_inc(chunk_used, 1)

            def spread(k, scratch, bank, cols):
                pe.wait_ge(diag_ready, k)
                nc.tensor.matmul(ps[:, bank, 0:2 * P], ones[:], scratch[:, 0:2, :], start=True, stop=True)
                nc.tensor.matmul(ps[:, bank, 2 * P:N], ones[:], scratch[:, 2, cols], start=True, stop=True).then_inc(bcast_done, 1)

            pe.wait_ge(const_in, 48)
            pe.wait_ge(vec_in, 80)
            tr(ps[:, 7, 0:NVEC], vec_rows[:]).then_inc(vec_done, 1)
            pe.wait_ge(table_in, 32)
            pe.wait_ge(filled, 4)
            nc.tensor.matmul(ps[0:HEADS, 6, 0:BIAS_N], table[:], onehot_s[:], start=True, stop=True).then_inc(rel_done, 1)
            pe.wait_ge(x_in, 80)
            for i, k in enumerate(K_ORDER):
                if i >= 6:
                    pe.wait_ge(xt_out, i - 5)
                for b, (t, size) in enumerate(BLOCKS):
                    mm = tr(ps[:, i % 6, t:t + size], rows_in[0:size, b, k * P:k * P + P])
                mm.then_inc(xt_done, 1)

            for c in range(QKV_TURNS * 2 * NC):
                if c < NC:
                    pe.wait_ge(op_lo_ready, 2 * c + 2)
                if c == 0:
                    pe.wait_ge(xt_out, KT)
                project(C_QKV + c, c % NC, c % RING, NA, NA * (c // NC % 2))
                if c == 2:
                    spread(1, x_diag, 6, slice(0, N - 2 * P))
                if 4 <= c < 4 + HEADS // 2:
                    i = c - 4
                    if i == 0:
                        pe.wait_ge(hankel_in, 16)
                        pe.wait_ge(rstd_ready, 1)
                    if i >= 2:
                        pe.wait_ge(bias_out, i - 1)
                    nc.tensor.matmul(ps[:, 6 + i % 2, :], flip[:], hankel[:, 2 * i:2 * i + 2, :],
                                     start=True, stop=True).then_inc(bias_done, 1)
                if 12 <= c < 16:
                    i = c - 12
                    if i == 0:
                        pe.wait_ge(kcache_in, 16)
                    if i < 2:
                        pe.wait_ge(bias_out, HEADS // 2 - 1 + i)
                    else:
                        pe.wait_ge(kct_out, i - 1)
                    for m in range(4):
                        b, r = 2 * i + m // 2, m % 2
                        mm = tr(ps[:, 6 + i % 2, m * P:m * P + P], kc[:, b, r * P:r * P + P])
                    mm.then_inc(kct_done, 1)
                if c == 17:
                    pe.wait_ge(z_out, 2)
                    pe.wait_ge(kct_out, 3)
                    for m in range(4):
                        b, r = m // 2, m % 2
                        mm = tr(ps[:, 6, m * P:m * P + P], zT[:, 10 + r, b * P:b * P + P])
                    mm.then_inc(kv_done, 1)
                if c == 18:
                    pe.wait_ge(kct_out, 4)
                    for r in range(2):
                        mm = tr(ps[0:N - 2 * P, 7, r * P:r * P + P], zT[:, 10 + r, 2 * P:N])
                    mm.then_inc(kv_done, 1)
                if c == 19:
                    pe.wait_ge(kv_out, 1)
                    for m in range(4):
                        mm = tr(ps[:, 6, m * P:m * P + P], zT[:, 8 + m, NP - WINDOW:NP])
                    mm.then_inc(kv_done, 1)
                if c == 20:
                    pe.wait_ge(kv_out, 2)
                    for m in range(4):
                        mm = tr(ps[0:ND, 7, m * P:m * P + P], zT[:, 8 + m, NP:N])
                    mm.then_inc(kv_done, 1)
                if c == 22:
                    pe.wait_ge(state_in, 16)
                    pe.wait_ge(kv_out, 3)
                    for j in range(CT):
                        mm = tr(ps[:, 6, j * 2 * ND:(j + 1) * 2 * ND], state_rows[:, j * P:j * P + P])
                    mm.then_inc(state_done, 1)

            def conv_turn(turn, last_turn):
                for c in range(2 * NC):
                    if c == 9:
                        pe.wait_ge(probs_ready, 3 * turn + 3)
                        pe.wait_ge(probs_t_dve, 2 * turn + 1)
                    project(C_CONV + c, c % NC, c % RING, NA, NA * (c // NC), turn * (2 * NC))
                    if c == 0:
                        pe.wait_ge(q_staged, 4 * turn + 4)
                        pe.wait_ge(k_staged, turn + 1)
                        for h in range(GROUP):
                            mm = nc.tensor.matmul(ps[:, 6, h * P:h * P + P], qs[:, h, 0:P], ks[:, 0:P],
                                                  start=True, stop=True)
                        mm.then_inc(scores_done, 1)
                    if c in (1, 2):
                        bank = 7 if c == 1 else 6
                        if c == 2:
                            pe.wait_ge(scores_out, 4 * turn + 1)
                        for i in range(2):
                            mm = nc.tensor.matmul(ps[:, bank, i * 256:i * 256 + 256], qs[:, 2 * (c - 1) + i, P:2 * P],
                                                  ks[:, 0:2 * P], start=True, stop=True)
                        mm.then_inc(scores_done, 1)
                    if c == 3:
                        pe.wait_ge(scores_out, 4 * turn + 2)
                        nc.tensor.matmul(ps[0:HEAD, 7, 0:144], qs_c[:].rearrange("p h q -> p (h q)"), ks[:, P:NP],
                                         start=True, stop=True).then_inc(scores_done, 1)
                    if last_turn and c == 4:
                        pe.wait_ge(scores_out, 4 * turn + 4)
                        pe.wait_ge(qd_staged, 8)
                        for b in range(ND):
                            for r in range(2):
                                mm = nc.tensor.matmul(ps[:, 6, b * HEADS + 8 * r:b * HEADS + 8 * r + 8],
                                                      kct[:, b, r, :], qd[:, r, b, :], start=True, stop=True)
                        own = ps[0:ND, 7, 0:P].rearrange("p (b r h) -> p r b h", r=2, h=8)
                        for r in range(2):
                            mm = nc.tensor.matmul(own[:, r], zT[:, 8 + r, NP:N], qd[:, r], start=True, stop=True)
                        mm.then_inc(dec_scores, 1)
                    if c == 5:
                        pe.wait_ge(probs_ready, 3 * turn + 1)
                        if last_turn:
                            pe.wait_ge(dec_scores_out, 2)
                        else:
                            pe.wait_ge(scores_out, 4 * turn + 3)
                        for h in range(GROUP):
                            mm = tr(ps[:, 6, h * P:h * P + P], s_ab[:, h * P:h * P + P])
                        mm.then_inc(probs_t, 1)
                    if c in (6, 7):
                        if c == 6:
                            pe.wait_ge(probs_ready, 3 * turn + 2)
                            pe.wait_ge(scores_out, 4 * turn + 4)
                        else:
                            pe.wait_ge(probs_t_act, 2 * turn + 1)
                        for h in range(GROUP):
                            col = 512 + h * 256 + (c - 6) * P
                            mm = tr(ps[:, 7 if c == 6 else 6, h * P:h * P + P], s_ab[:, col:col + P])
                        mm.then_inc(probs_t, 1)
                    if c == 9:
                        tr(ps[:, 7, 0:HEAD], s_c[:, 0:P])
                        tr(ps[0:16, 7, HEAD:2 * HEAD], s_c[:, P:144]).then_inc(probs_t, 1)
                    if last_turn and c == 9:
                        pe.wait_ge(probs_t_act, 2 * turn + 2)
                        nc.tensor.matmul(ps[:, 6, 0:P + 1], table_d[:].rearrange("p b h -> p (b h)"),
                                         onehot_s[:, P - 1:2 * P], start=True, stop=False)
                        nc.tensor.matmul(ps[:, 6, 0:P], sdt[:], ident[:], start=False, stop=True)
                        tr(ps[:, 6, 256:256 + ND], sd_own[:]).then_inc(dec_rows, 1)
                    if c == 10:
                        pe.wait_ge(v_staged, 4 * turn + 4)
                        pe.wait_ge(probs_t_act, 2 * turn + 1)
                        pe.wait_ge(probs_t_dve, 2 * turn + 2)
                        nc.tensor.matmul(ps[:, 7, :], vs[:, 0].rearrange("p a d -> p (a d)"), pt[:, 0, :],
                                         start=True, stop=True).then_inc(pv_done, 1)
                    if c == 11:
                        pe.wait_ge(probs_t_act, 2 * turn + 2)
                        if last_turn:
                            pe.wait_ge(dec_rows_out, 2)
                        nc.tensor.matmul(ps[:, 6, :], vs[:, 0].rearrange("p a d -> p (a d)"), pt[:, 1, :],
                                         start=True, stop=False)
                        nc.tensor.matmul(ps[:, 6, :], vs[:, 1].rearrange("p a d -> p (a d)"), pt[:, 2, :],
                                         start=False, stop=True).then_inc(pv_done, 1)
                    if c == 12:
                        pe.wait_ge(pv_act, 4 * turn + 2)
                        nc.tensor.matmul(ps[:, 7, 0:HEAD], vs[:, 1].rearrange("p a d -> p (a d)"), pt_c[:, 0, :],
                                         start=True, stop=False)
                        nc.tensor.matmul(ps[:, 7, 0:HEAD], vs[0:16, 2].rearrange("p a d -> p (a d)"), pt_c[0:16, 1, :],
                                         start=False, stop=True).then_inc(pv_done, 1)
                    if last_turn and c == 13:
                        pe.wait_ge(dec_probs, 2)
                        pe.wait_ge(pv_act, 4 * turn + 4)
                        tr(ps[:, 6, 0:P], sd[:, 0:P])
                        tr(ps[0:ND, 6, P:2 * P], sd_own8[:]).then_inc(dec_pt, 1)
                    if last_turn and c == 15:
                        pe.wait_ge(dec_pt_out, 2)
                        pe.wait_ge(pv_dve, 2 * turn + 2)
                        pe.wait_ge(vcache_in, 16)
                        pe.wait_ge(kv_out, 4)
                        own = pd_own[:].rearrange("p (b r h) -> p r b h", r=2, h=8)
                        for r in range(2):
                            out = ps[:, 7, HEAD * r:HEAD * r + HEAD]
                            nc.tensor.matmul(out.rearrange("p (b h) -> p b h", h=8), kv_dec[:, 2 * P + r * P:3 * P + r * P],
                                             own[:, r], start=True, stop=False)
                            for b in range(ND):
                                mm = nc.tensor.matmul(out[:, 8 * b:8 * b + 8], vc[:, b, r * P:r * P + P],
                                                      pd[:, b * HEADS + 8 * r:b * HEADS + 8 * r + 8],
                                                      start=False, stop=b == ND - 1)
                        mm.then_inc(dec_pv, 1)

            with pe.Fori(0, CONV_TURNS - 1) as turn:
                conv_turn(turn, False)
            conv_turn(CONV_TURNS - 1, True)

            pe.wait_ge(zb_ready, CT)
            pe.wait_ge(dec_pv_out, 4)
            with pe.Fori(0, 2) as turn:
                for c in range(2 * NC):
                    if c < NC:
                        pe.wait_ge(op_lo_ready, KT + (1 if c < 3 else 2 if c < 7 else 3))
                    project(C_OUT + c, c % NC, c % RING, NB, NB * (c // NC), turn * (2 * NC))
            pe.wait_ge(mix_out, 3)
            pe.wait_ge(conv_done, CT)
            for j in range(CT):
                mm = tr(ps[0:2 + ND, j // 4, j % 4 * P:j % 4 * P + P], u_out[:, j, :])
            mm.then_inc(crow_done, 1)

            def token_sums(first, second, bank, step):
                for part, (src, ready) in enumerate((first, second)):
                    pe.wait_ge(*ready)
                    for i, t in enumerate((0, P, N - P)):
                        for m in range(NB):
                            mm = nc.tensor.matmul(ps[:, bank, 4 * i:4 * i + 1], src[:, m, t:t + P], ones[:, 0:1],
                                                  start=part == 0 and i == 0 and m == 0, stop=False if (part == 0 or m < NB - 1) else True,
                                                  skip_group_check=True)
                mm.then_inc(stat_done, 1)

            token_sums((acc4, (mix_acc, 1)), (sq, (sq_ready, 1)), 2, 1)
            pe.wait_ge(mix_out, 4)
            spread(2, diag, 7, slice(P - (N - 2 * P), P))

            pe.wait_ge(crow_out, 1)
            pe.wait_ge(rms_ready, 2)
            with pe.Fori(0, FF_TURNS) as turn:
                for c in range(2 * NC):
                    if c < NC:
                        pe.wait_ge(op_lo_ready, KT + 3 + 2 * c + 2)
                    project(C_FF + c, c % NC, c % RING, NB, NB * (c // NC), turn * (2 * NC))

            with pe.Fori(0, 2) as turn:
                for c in range(2 * DC):
                    k = c % DC
                    pe.wait_ge(lo_ready, RING + C_DOWN + c + 1 + turn * (2 * DC))
                    if c < DC and k * 2 + 2 > FT - NB:
                        pe.wait_ge(hid_lo, FF_TURNS)
                    elif c == 0:
                        pe.wait_ge(hid_lo, FF_TURNS - 1)
                        pe.wait_ge(up_ready, FF_TURNS)
                    chunk(c % RING, NB, NB * (c // DC), 2 * k, h_hi, h_lo, k == 0, k == DC - 1).then_inc(chunk_used, 1)
            token_sums((y_acc, (mix_acc, 2)), (y_sq, (sq_ready, 2)), 0, 2)
            pe.wait_ge(y_out, 4)
            spread(3, y_diag, 7, slice(P - (N - 2 * P), P))
            for q in range(4):
                for b, (t, size) in enumerate(BLOCKS):
                    i = 3 * q + b
                    if b == 0:
                        pe.wait_ge(y_ready_pool, 2 * q + 2)
                        pe.wait_ge(y_ready_dve, 2 * q + 2)
                    if i == 0:
                        pe.wait_ge(rms_ready, 3)
                    if i >= 6:
                        pe.wait_ge((yt_act, yt_dve)[i % 2], (i - 6) // 2 + 1)
                    for m in range(NB):
                        mm = tr(ps[0:size, i % 6, m * P:m * P + P], yT[:, NB * q + m, t:t + size])
                    mm.then_inc(yt_done, 1)

        @block.gpsimd
        def _(pool):
            own = Own(pool, pool_own)
            nc.gpsimd.memset(stat3[:, 6:7], 0.0).then_inc(lo_ready, RING)
            nc.gpsimd.memset(cw[:], 0.0).then_inc(chunk_used, RING)
            nc.gpsimd.memset(stat3[:, 7:8], -0.5).then_inc(filled, 1)
            nc.gpsimd.memset(stat3[:, 0:3], 1.0).then_inc(filled, 1)
            pool.wait_ge(filled, 2)
            nc.gpsimd.memset(table[BUCKETS:BUCKETS + 1, :], 1.0).then_inc(filled, 1)
            pool.wait_ge(filled, 3)
            nc.gpsimd.memset(ones[:], 1.0).then_inc(filled, 1)
            own.link(nc.gpsimd.memset(u_ext[:, 0:2], 0.0))
            pool.wait_ge(filled, 4)

            def inverse_root(k):
                pool.wait_ge(rms_ready, k)
                nc.gpsimd.tensor_tensor(stat3[:, 3:6], stat3[:, 0:3], stat3[:, 7:8].broadcast_to([P, 3]),
                                        ALU.pow).then_inc(inv_ready, 1)

            inverse_root(1)

            def stage_k(g):
                nc.gpsimd.tensor_copy(ks[:], at(kd, g)).then_inc(k_staged, 1)

            def stage_v(g):
                for half in range(2):
                    nc.gpsimd.tensor_copy(vs[:, 0:2, half, :], vd[:, 0:2, bass.ds(g * HEAD, HEAD)]).then_inc(v_staged, 1)
                    nc.gpsimd.tensor_copy(vs[0:16, 2, half, :], vd[0:16, 2, bass.ds(g * HEAD, HEAD)]).then_inc(v_staged, 1)

            def tap_of(i):
                return cw[:, i:i + 1].broadcast_to([P, EXT - 2])

            def conv_tile(j, half):
                pool.wait_ge(zb_ready, j + 1)
                g, c, h = (zb[:, half, i, :] for i in range(3))
                dec = u_ext[:, NP + 2:EXT].rearrange("p (b t) -> p b t", t=3)
                keep, out = at(u_out, j), at(convT, j)
                taps = vec[:, V_CONV:NVEC].rearrange("p (i j) -> p i j", j=CT)[:, :, bass.ds(j, 1)]
                own.link(nc.gpsimd.tensor_copy(cw[:], taps.rearrange("p i j -> p (i j)")))
                own.link(nc.gpsimd.tensor_copy(dec[:, :, 0:2], at(state_t, j).rearrange("p (b t) -> p b t", t=2)))
                own.link(nc.gpsimd.tensor_tensor(u_ext[:, 2:NP + 2], c[:, 0:NP], h[:, 0:NP], ALU.mult))
                own.link(nc.gpsimd.tensor_tensor(dec[:, :, 2], c[:, NP:N], h[:, NP:N], ALU.mult))
                own.link(nc.gpsimd.tensor_tensor(acc[:], u_ext[:, 0:EXT - 2], tap_of(0), ALU.mult))
                own.link(nc.gpsimd.tensor_tensor(tap[:], u_ext[:, 1:EXT - 1], tap_of(1), ALU.mult))
                own.link(nc.gpsimd.tensor_tensor(acc[:], acc[:], tap[:], ALU.add))
                own.link(nc.gpsimd.tensor_tensor(tap[:], u_ext[:, 2:EXT], tap_of(2), ALU.mult))
                own.link(nc.gpsimd.tensor_tensor(acc[:], acc[:], tap[:], ALU.add))
                nc.gpsimd.tensor_copy(keep[:, 0:2], u_ext[:, NP:NP + 2])
                nc.gpsimd.tensor_copy(keep[:, 2:2 + ND], dec[:, :, 2])
                nc.gpsimd.tensor_tensor(out[:, 0:NP], acc[:, 0:NP], g[:, 0:NP], ALU.mult)
                nc.gpsimd.tensor_tensor(out[:, NP:N], acc[:, NP + 2:EXT - 2:3], g[:, NP:N], ALU.mult).then_inc(conv_done, 1)

            CONV_LINKS = 9

            pool.wait_ge(bias_done, HEADS // 2)
            nc.gpsimd.memset(qs[:], 0.0).then_inc(zeroed, 1)
            nc.gpsimd.memset(qs_c[:], 0.0).then_inc(zeroed, 1)
            nc.gpsimd.memset(qd[:], 0.0).then_inc(zeroed, 1)
            pool.wait_ge(zeroed, 3)
            pool.wait_ge(kd_ready, 4)
            stage_k(KVH - 1)
            pool.wait_ge(kv_out, 2)
            stage_v(KVH - 1)
            pool.wait_ge(z_out, 4)
            pool.wait_ge(v_staged, 4)
            for e in range(2):
                for a in range(2):
                    for r in range(2):
                        q = zT[HEAD * e:HEAD * e + HEAD, 4 * r + 2 * a:4 * r + 2 * a + 2, NP:N].rearrange("p i b -> p b i")
                        nc.gpsimd.tensor_scalar(qd[HEAD * a:HEAD * a + HEAD, r, :, 4 * a + e:4 * a + 4:2], q,
                                                HEAD ** -0.5, None, ALU.mult).then_inc(qd_staged, 1)
                        pool.wait_ge(qd_staged, 4 * e + 2 * a + r + 1)
            pool.wait_ge(state_out, 1)
            with pool.Fori(0, CONV_TURNS - 1) as turn:
                own.begin(turn, 2 * CONV_LINKS)
                conv_tile(turn * 2, 0)
                pool.wait_ge(scores_done, 4 * turn + 4)
                stage_k(turn * -1 + (KVH - 2))
                conv_tile(turn * 2 + 1, 1)
                pool.wait_ge(pv_done, 3 * turn + 3)
                stage_v(turn * -1 + (KVH - 2))
                own.end(CONV_TURNS - 1)
            conv_tile(CT - 2, 0)
            conv_tile(CT - 1, 1)

            def square_sums(total, scratch, src, ready, base):
                for i in range(3):
                    pool.wait_ge(ready, base + i + 1)
                    m = src[:, NB * i:NB * i + NB, :]
                    if i == 0:
                        own.link(nc.gpsimd.tensor_tensor(total[:], m, m, ALU.mult))
                        continue
                    own.link(nc.gpsimd.tensor_tensor(scratch[:], m, m, ALU.mult))
                    last = nc.gpsimd.tensor_tensor(total[:], total[:], scratch[:], ALU.add)
                    if i < 2:
                        own.link(last)
                last.then_inc(mix_acc, 1)

            square_sums(acc4, sq, mixT, mix_out, 0)
            inverse_root(2)
            for i, k in enumerate(K_ORDER):
                pool.wait_ge(scaled, i + 1)
                nc.gpsimd.tensor_tensor(resid[:, k, :], tmp[:, i % 2, :], resid[:, k, :], ALU.add).then_inc(resid_ready, 1)
                if i:
                    pool.wait_ge(rsq_ready, i)
                    if i == 1:
                        nc.gpsimd.tensor_copy(acc4[:, 0, :], sq[:, 0, :]).then_inc(rsum, 1)
                    else:
                        pool.wait_ge(rsum, i - 1)
                        nc.gpsimd.tensor_tensor(acc4[:, 0, :], acc4[:, 0, :], sq[:, (i - 1) % 2, :], ALU.add).then_inc(rsum, 1)
            pool.wait_ge(rsq_ready, KT)
            pool.wait_ge(rsum, KT - 1)
            nc.gpsimd.tensor_tensor(acc4[:, 0, :], acc4[:, 0, :], sq[:, (KT - 1) % 2, :], ALU.add).then_inc(rsum, 1)
            pool.wait_ge(rsum, KT)
            nc.gpsimd.partition_all_reduce(acc4[:, 1, :], acc4[:, 0, :], P, RADD).then_inc(tot_ready, 1)
            with pool.Fori(0, FF_TURNS) as turn:
                pool.wait_ge(sig_ready, turn + 1)
                nc.gpsimd.tensor_tensor(gate[:], gate[:], up[:], ALU.mult).then_inc(swish_ready, 1)
                pool.wait_ge(swish_ready, turn + 1)
                pool.wait_ge(up_ready, turn + 1)
                nc.gpsimd.tensor_tensor(up[:], up[:], gate[:], ALU.mult).then_inc(hid_ready, 1)
                pool.wait_ge(hid_ready, turn + 1)
                pool.wait_ge(hid_hi, turn + 1)
                nc.gpsimd.tensor_tensor(h_lo[:, bass.ds(turn * NB, NB), :], up[:],
                                        h_hi[:, bass.ds(turn * NB, NB), :].bitcast(F32), ALU.subtract).then_inc(hid_lo, 1)
            square_sums(y_acc, y_sq, yT, y_out, 0)
            inverse_root(3)
            for k in range(0, KT, 2):
                pool.wait_ge(y_scaled, k + 1)
                nc.gpsimd.tensor_tensor(yT[:, k, :], yT[:, k, :], resid[:, k, :], ALU.add).then_inc(y_ready_pool, 1)

        @block.scalar
        def _(act):
            act.dma_start(ident[:], squares[0]).then_inc(const_in, 16)
            act.dma_start(flip[:], squares[1]).then_inc(const_in, 16)
            act.dma_start(masks[:], row_masks).then_inc(const_in, 16)
            for i, gain in enumerate((norm_pre_mix, norm_post_mix, norm_pre_ffn, norm_post_ffn)):
                act.dma_start(vec_rows[KT * i:KT * i + KT, :], gain[0].rearrange("(t p) -> t p", p=P)).then_inc(vec_in, 16)
            act.dma_start(vec_rows[V_CONV:NVEC, :], conv_w[0].rearrange("i (j p) -> (i j) p", p=P)).then_inc(vec_in, 16)
            act.dma_start(onehot_s[:], onehot).then_inc(table_in, 16)
            act.dma_start(table[0:BUCKETS, :], rel_bias).then_inc(table_in, 16)
            act.dma_start(sink[:], attn_sinks[0:1, :].broadcast_to([P, HEADS])).then_inc(sink_in, 16)
            act.dma_start(kc[:], cache_k[0].rearrange("b t h d -> t b (h d)")).then_inc(kcache_in, 16)
            act.dma_start(state_rows[:], state_conv[0].rearrange("b t c -> (b t) c")).then_inc(state_in, 16)
            act.dma_start(vc[:], cache_v[0].rearrange("b t h d -> t b (h d)")).then_inc(vcache_in, 16)

            def split(n, slot, size, loads, turn=0, turn_loads=0):
                act.wait_ge(raw_landed[slot], 16 * loads + turn_loads)
                act.wait_ge(chunk_used, n + 1 + turn)
                nc.scalar.activation(w_hi[:, slot, 0:size].rearrange("p (j n) -> p j n", j=2),
                                     raw[:, slot, :, 0:size // 2], ACT.Copy).then_inc(hi_ready, 1)

            def loads_to(n):
                a, b = C_CONV // RING, C_OUT // RING
                done = n // RING + 1
                return done + min(max(done - a, 0), b - a)

            act.wait_ge(x_in, 80)
            act.wait_ge(filled, 4)
            for b, (_, size) in enumerate(BLOCKS):
                if b:
                    act.wait_ge(x_squared, b)
                nc.scalar.activation(w_hi[0:size, 0:2, :].rearrange("p a n -> p (a n)"), rows_in[0:size, b, :],
                                     ACT.Square, accum_out=stat3[0:size, b:b + 1]).then_inc(x_squared, 1)
            act.wait_ge(vec_out, 1)
            for i, k in enumerate(K_ORDER):
                act.wait_ge(xt_out, i + 1)
                nc.scalar.activation(op_hi[:, k, :], resid[:, k, :], ACT.Copy,
                                     scale=vec[:, V_PRE_MIX + k:V_PRE_MIX + k + 1]).then_inc(op_hi_ready, 1)
            act.wait_ge(x_squared, 3)
            for n in range(RING):
                split(n, n, 768, loads_to(n))

            def stage_q(g):
                for e in range(2):
                    part = slice(HEAD * e, HEAD * e + HEAD)
                    nc.scalar.activation(qs[part, e:GROUP:2, :], zT[part, bass.ds(g * 2, 2), 0:2 * P], ACT.Copy).then_inc(q_staged, 1)
                    nc.scalar.activation(qs_c[part, e:GROUP:2, :], zT[part, bass.ds(g * 2, 2), 2 * P:NP], ACT.Copy).then_inc(q_staged, 1)

            for c in range(QKV_TURNS * 2 * NC):
                split(c + RING, c % RING, 768, loads_to(c + RING))
                if 12 <= c < 16:
                    i = c - 12
                    act.wait_ge(kct_done, i + 1)
                    nc.scalar.activation(kct[:, 2 * i:2 * i + 2, :, :].rearrange("p b r k -> p (b r k)"),
                                         ps[:, 6 + i % 2, :], ACT.Copy).then_inc(kct_out, 1)
                if c == 18:
                    act.wait_ge(z_out, 2)
                    for a in range(2):
                        for half in range(2):
                            nc.scalar.activation(kd[HEAD * half:HEAD * half + HEAD, a:KVH:2, :],
                                                 zT[HEAD * a:HEAD * a + HEAD, 8:10, 0:NP], ACT.Copy,
                                                 scale=HEAD ** -0.5).then_inc(kd_ready, 1)
                if c == 24:
                    act.wait_ge(zeroed, 2)
                    stage_q(KVH - 1)

            def conv_turn(turn, g, last_turn):
                for c in range(2 * NC):
                    into_next = (c + RING) // (2 * NC)
                    if last_turn and into_next:
                        split(C_CONV + c + RING, c % RING, 1024, loads_to(C_CONV + 2 * NC * CONV_TURNS + c + RING - 2 * NC), turn * (2 * NC))
                    else:
                        loads = C_CONV // RING + 2 * ((c + RING) // RING + 1)
                        split(C_CONV + c + RING, c % RING, 768, loads, turn * (2 * NC), turn * (16 * 2 * 2 * NC // RING))
                    if c in (1, 3):
                        width, start, col = ((P, 0, 0), (2 * P, 512, 4))[c // 2]
                        act.wait_ge(nmax_ready, 3 * turn + 1 + c // 2)
                        for h in range(GROUP):
                            part = s_ab[:, start + h * width:start + (h + 1) * width]
                            nc.scalar.activation(part, part, ACT.Exp, bias=nmax[:, col + h:col + h + 1],
                                                 accum_out=den[:, col + h:col + h + 1])
                        nc.scalar.activation(esk[:, col:col + 4], esk[:, col:col + 4], ACT.Exp).then_inc(exp_done, 1)
                    if c == 4:
                        act.wait_ge(nmax_ready, 3 * turn + 3)
                        nc.scalar.activation(s_c[:], s_c[:], ACT.Exp, bias=nmax[0:HEAD, 8:9], accum_out=den[0:HEAD, 8:9])
                        nc.scalar.activation(esk[0:HEAD, 8:9], esk[0:HEAD, 8:9], ACT.Exp).then_inc(exp_done, 1)
                    if c in (5, 7):
                        act.wait_ge(probs_t, 4 * turn + (1 if c == 5 else 3))
                        nc.scalar.activation(pt[:, 0 if c == 5 else 2, :], ps[:, 6, :], ACT.Copy).then_inc(probs_t_act, 1)
                    if last_turn and c == 10:
                        act.wait_ge(dec_nmax, 1)
                        nc.scalar.activation(sd[:], sd[:], ACT.Exp, bias=dstat[:, 0:1], accum_out=dstat[:, 2:3])
                        nc.scalar.activation(dstat[:, 3:4], dstat[:, 1:2], ACT.Exp, bias=dstat[:, 0:1]).then_inc(dec_exp, 1)
                    if c in (10, 11):
                        block_i = c - 10
                        act.wait_ge(pv_done, 3 * turn + 1 + block_i)
                        src = ps[:, 7 - block_i, :].rearrange("p (i e q) -> p i e q", e=2, q=P)
                        for e in range(2):
                            part = slice(HEAD * e, HEAD * e + HEAD)
                            nc.scalar.activation(zT[part, bass.ds(g * 2, 2), block_i * P:block_i * P + P],
                                                 src[part, :, e, :], ACT.Copy).then_inc(pv_act, 1)
                    if c == 13 and not last_turn:
                        stage_q(g - 1)
                    if last_turn and c == 12:
                        act.wait_ge(conv_done, CT - 2)
                        act.wait_ge(chunk_used, RING + C_OUT - NC + 3)
                        nc.scalar.activation(op_hi[:, 8:14, :], convT[:, 0:6, :], ACT.Copy).then_inc(op_hi_ready, 1)

            with act.Fori(0, CONV_TURNS - 1) as turn:
                conv_turn(turn, turn * -1 + (KVH - 1), False)
            conv_turn(CONV_TURNS - 1, 0, True)
            act.wait_ge(dec_pv_out, 4)
            act.wait_ge(pv_dve, 2 * CONV_TURNS)
            act.wait_ge(chunk_used, RING + C_OUT - 1)
            nc.scalar.activation(op_hi[:, 0:8, :], zT[:, 0:8, :], ACT.Copy).then_inc(op_hi_ready, 1)
            act.wait_ge(conv_done, CT)
            act.wait_ge(chunk_used, RING + C_OUT)
            nc.scalar.activation(op_hi[:, 14:16, :], convT[:, 6:8, :], ACT.Copy).then_inc(op_hi_ready, 1)

            with act.Fori(0, 2) as turn:
                for c in range(2 * NC):
                    split(C_OUT + c + RING, c % RING, 1024, loads_to(C_OUT + c + RING), turn * (2 * NC),
                          turn * (16 * 2 * NC // RING))
                    if c % NC == NC - 1:
                        half = c // NC
                        act.wait_ge(chunk_used, RING + C_OUT + c + 1 + turn * (2 * NC))
                        nc.scalar.activation(mixT[:, bass.ds(turn * (2 * NB) + NB * half, NB), :],
                                             ps[:, NB * half:NB * half + NB, 0:N], ACT.Copy).then_inc(mix_out, 1)
            act.wait_ge(crow_done, 1)
            nc.scalar.activation(conv_rows[:], ps[0:2 + ND, 0:2, :].rearrange("p a n -> p (a n)"), ACT.Copy).then_inc(crow_out, 1)

            def input_step(i):
                k = K_ORDER[i]
                act.wait_ge(resid_ready, i + 1)
                nc.scalar.activation(op_hi[:, k, :], resid[:, k, :], ACT.Copy,
                                     scale=vec[:, V_PRE_FFN + k:V_PRE_FFN + k + 1]).then_inc(op_hi_ready, 1)
                if i == 0:
                    act.wait_ge(stat_done, 1)
                if i >= 2:
                    act.wait_ge(rsum, i - 1)
                nc.scalar.activation(sq[:, i % 2, :], resid[:, k, :], ACT.Square).then_inc(rsq_ready, 1)

            def ffn_turn(turn, first):
                for c in range(2 * NC):
                    if first and 2 * c + 3 < KT:
                        for i in range(2 * c + 3, min(2 * c + 5, KT)):
                            input_step(i)
                    split(C_FF + c + RING, c % RING, 1024, loads_to(C_FF + c + RING), turn * (2 * NC),
                          turn * (16 * 2 * NC // RING))
                    if first and c == NC - 1:
                        act.wait_ge(mean_ready, 1)
                        nc.scalar.activation(acc4[:, 2, :], acc4[:, 1, :], ACT.Sqrt).then_inc(root_ready, 1)
                    if c == NC:
                        act.wait_ge(gate_ready, turn + 1)
                        nc.scalar.activation(up[:], gate[:], ACT.Sigmoid).then_inc(sig_ready, 1)
                    if c == 2 * NC - 1:
                        act.wait_ge(hid_ready, turn + 1)
                        nc.scalar.activation(h_hi[:, bass.ds(turn * NB, NB), :], up[:], ACT.Copy).then_inc(hid_hi, 1)

            for i in range(3):
                input_step(i)
            ffn_turn(0, True)
            with act.Fori(1, FF_TURNS) as turn:
                ffn_turn(turn, False)

            def down_slots(first, count):
                for c in range(first, first + count):
                    split(C_DOWN + c + RING, c % RING, 1024, loads_to(C_DOWN + c + RING))

            def down_turns(first, turns):
                with act.Fori(0, turns) as turn:
                    for c in range(first, first + RING):
                        split(C_DOWN + c + RING, c % RING, 1024, loads_to(C_DOWN + c + RING), turn * RING, turn * 16)

            def down_out(group):
                act.wait_ge(chunk_used, RING + C_DOWN + DC * group + DC)
                bank = NB * (group % 2)
                nc.scalar.activation(yT[:, NB * group:NB * group + NB, :], ps[:, bank:bank + NB, 0:N], ACT.Copy).then_inc(y_out, 1)

            whole = DC // RING
            for half in range(2):
                start = 2 * DC * half
                down_turns(start, whole)
                down_slots(start + whole * RING, DC % RING)
                down_out(2 * half)
                down_slots(start + DC, RING - DC % RING)
                down_turns(start + DC + RING - DC % RING, whole - half)
                down_out(2 * half + 1)
            for i in range(0, 12, 2):
                b, q = i % 3, i // 3
                size = BLOCKS[b][1]
                act.wait_ge(yt_done, i + 1)
                nc.scalar.activation(rows_out[0:size, b, 512 * q:512 * q + 512], ps[0:size, i % 6, :], ACT.Copy).then_inc(yt_act, 1)

        @block.vector
        def _(dve):
            own = Own(dve, dve_own)

            def split(n, slot, size, turn=0):
                dve.wait_ge(hi_ready, n + 1 + turn)
                hi = w_hi[:, slot, 0:size].rearrange("p (j n) -> p j n", j=2)
                lo = w_lo[:, slot, 0:size].rearrange("p (j n) -> p j n", j=2)
                nc.vector.tensor_tensor(lo, raw[:, slot, :, 0:size // 2], hi.bitcast(F32), ALU.subtract).then_inc(lo_ready, 1)

            def low_half(i, k, gain, base):
                dve.wait_ge(op_hi_ready, base + i + 1)
                nc.vector.scalar_tensor_tensor(out=op_lo[:, k, :], in0=resid[:, k, :], scalar=vec[:, gain + k:gain + k + 1],
                                               in1=op_hi[:, k, :].bitcast(F32), op0=ALU.mult, op1=ALU.subtract).then_inc(op_lo_ready, 1)

            def diagonals(k, scratch):
                dve.wait_ge(inv_ready, k)
                nc.vector.tensor_tensor(scratch[:], each(ident[:], [P, 3, P]),
                                        stat3[:, 3:6].unsqueeze(2).broadcast_to([P, 3, P]), ALU.mult).then_inc(diag_ready, 1)

            dve.wait_ge(vec_done, 1)
            nc.vector.tensor_copy(vec[:], ps[:, 7, 0:NVEC]).then_inc(vec_out, 1)
            dve.wait_ge(rel_done, 1)
            nc.vector.tensor_copy(bias_sb[:], ps[0:HEADS, 6, 0:BIAS_N]).then_inc(rel_out, 1)
            dve.wait_ge(filled, 4)
            dve.wait_ge(table_in, 32)
            nc.vector.tensor_copy(table_d[:], each(table[:], [BUCKETS + 1, ND, HEADS])).then_inc(table_d_ready, 1)
            for i, k in enumerate(K_ORDER):
                dve.wait_ge(xt_done, i + 1)
                nc.vector.tensor_copy(resid[:, k, :], ps[:, i % 6, 0:N]).then_inc(xt_out, 1)
                if i == 2:
                    dve.wait_ge(x_squared, 3)
                    nc.vector.tensor_scalar(stat3[:, 0:3], stat3[:, 0:3], 1.0 / D, EPS, ALU.mult, ALU.add).then_inc(rms_ready, 1)
                if i:
                    dve.wait_ge(xt_out, i)
                    low_half(i - 1, K_ORDER[i - 1], V_PRE_MIX, 0)
            dve.wait_ge(xt_out, KT)
            low_half(KT - 1, K_ORDER[-1], V_PRE_MIX, 0)
            for n in range(RING):
                split(n, n, 768)
            dve.wait_ge(const_in, 48)
            diagonals(1, x_diag)
            dve.wait_ge(sink_in, 16)
            own.link(nc.vector.tensor_scalar(nsink[:], sink[:], -1.0, None, ALU.mult))

            for c in range(QKV_TURNS * 2 * NC):
                split(c + RING, c % RING, 768)
                if c == 2:
                    dve.wait_ge(bcast_done, 1)
                    nc.vector.tensor_copy(rstd[:], ps[:, 6, 0:N]).then_inc(rstd_ready, 1)
                    dve.wait_ge(rstd_ready, 1)
                if c % NC == NC - 1:
                    group = c // NC
                    dve.wait_ge(chunk_used, RING + c + 1)
                    bank = NA * (group % 2)
                    nc.vector.tensor_tensor(zT[:, 9 - 3 * group:12 - 3 * group, :], ps[:, bank:bank + NA, 0:N],
                                            each(rstd[:], [P, NA, N]), ALU.mult).then_inc(z_out, 1)
                if 4 <= c < 4 + HEADS // 2:
                    i = c - 4
                    dve.wait_ge(bias_done, i + 1)
                    nc.vector.tensor_copy(bias[:, 2 * i:2 * i + 2, :].rearrange("p a n -> p (a n)"),
                                          ps[:, 6 + i % 2, :]).then_inc(bias_out, 1)
                if c == 14:
                    own.link(nc.vector.tensor_tensor(sinks_m[:], sink[:], masks[:, ND:ND + HEADS], ALU.mult))
                    own.link(nc.vector.tensor_reduce(dstat[:, 1:2], sinks_m[:], AX.X, ALU.add))
                    own.link(nc.vector.tensor_scalar(dstat[:, 6:7], dstat[:, 1:2], -1.0, None, ALU.mult))
                    by_head = sinks_m[0:HEAD, :].rearrange("p (g h) -> p g h", g=KVH)
                    own.link(nc.vector.tensor_tensor(by_head, sink[0:HEAD, :].rearrange("p (g h) -> p g h", g=KVH),
                                                     each(masks[0:HEAD, ND + HEADS:ND + HEADS + GROUP], [HEAD, KVH, GROUP]), ALU.mult))
                    own.link(nc.vector.tensor_reduce(sink_c[:, 0:KVH], by_head, AX.X, ALU.add))
                    own.link(nc.vector.tensor_scalar(sink_c[:, KVH:2 * KVH], sink_c[:, 0:KVH], -1.0, None, ALU.mult))
                if c == 17:
                    dve.wait_ge(kv_done, 1)
                    nc.vector.tensor_copy(vd[:, 0:2, :].rearrange("p a n -> p (a n)"), ps[:, 6, :]).then_inc(kv_out, 1)
                if c == 18:
                    dve.wait_ge(kv_done, 2)
                    nc.vector.tensor_copy(vd[0:N - 2 * P, 2, :], ps[0:N - 2 * P, 7, 0:2 * P]).then_inc(kv_out, 1)
                if c == 19:
                    dve.wait_ge(kv_done, 3)
                    nc.vector.tensor_copy(kv_rows[:], ps[:, 6, :]).then_inc(kv_out, 1)
                if c == 20:
                    dve.wait_ge(kv_done, 4)
                    nc.vector.tensor_copy(kv_dec[:], ps[0:ND, 7, :]).then_inc(kv_out, 1)
                if c == 22:
                    dve.wait_ge(state_done, 1)
                    nc.vector.tensor_copy(state_t[:].rearrange("p j r -> p (j r)"), ps[:, 6, 0:P]).then_inc(state_out, 1)

            def minus_max(scores, rows, cols, negated, plain):
                own.link(nc.vector.tensor_reduce(nmax[rows, cols], scores, AX.X, ALU.max))
                own.link(nc.vector.scalar_tensor_tensor(out=nmax[rows, cols], in0=nmax[rows, cols], scalar=-1.0, in1=negated,
                                                        op0=ALU.mult, op1=ALU.min))
                nc.vector.tensor_tensor(esk[rows, cols], nmax[rows, cols], plain, ALU.add).then_inc(nmax_ready, 1)

            def normalise(probs, rows, cols, width):
                n = cols.stop - cols.start
                own.link(nc.vector.tensor_tensor(den[rows, cols], den[rows, cols], esk[rows, cols], ALU.add))
                own.link(nc.vector.reciprocal(den[rows, cols], den[rows, cols]))
                size = den[rows, cols].shape[0]
                nc.vector.tensor_tensor(probs, probs, den[rows, cols].unsqueeze(2).broadcast_to([size, n, width]),
                                        ALU.mult).then_inc(probs_ready, 1)

            dve.wait_ge(bias_c_in, 64)
            TURN_LINKS = 12
            every = slice(0, P)
            few = slice(0, HEAD)

            def conv_turn(turn, g, last_turn):
                heads = bass.ds(g * GROUP, GROUP)
                a_blk, b_blk = heads4(s_ab[:, 0:512]), heads4(s_ab[:, 512:1536])
                c_blk = s_c[:].unsqueeze(1)
                for c in range(2 * NC):
                    size = 1024 if last_turn and c + RING >= 2 * NC else 768
                    split(C_CONV + c + RING, c % RING, size, turn * (2 * NC))
                    if c % NC == NC - 1:
                        half = c // NC
                        dve.wait_ge(chunk_used, RING + C_CONV + c + 1 + turn * (2 * NC))
                        nc.vector.tensor_tensor(zb[:, half], ps[:, NA * half:NA * half + NA, 0:N],
                                                each(rstd[:], [P, NA, N]), ALU.mult).then_inc(zb_ready, 1)
                    if c == 0:
                        dve.wait_ge(scores_done, 4 * turn + 1)
                        nc.vector.tensor_tensor(a_blk, heads4(ps[:, 6, :]), bias[:, heads, P:2 * P], ALU.add).then_inc(scores_out, 1)
                        dve.wait_ge(scores_out, 4 * turn + 1)
                        minus_max(a_blk, every, slice(0, 4), nsink[:, heads], sink[:, heads])
                    if c in (1, 2):
                        bank, h = (7, 0) if c == 1 else (6, 2)
                        dve.wait_ge(scores_done, 4 * turn + 1 + c)
                        nc.vector.tensor_tensor(b_blk[:, h:h + 2], ps[:, bank, :].rearrange("p (h k) -> p h k", h=2),
                                                bias[:, bass.ds(g * GROUP + h, 2), :], ALU.add).then_inc(scores_out, 1)
                    if c == 2:
                        dve.wait_ge(scores_out, 4 * turn + 3)
                        minus_max(b_blk, every, slice(4, 8), nsink[:, heads], sink[:, heads])
                    if c == 3:
                        dve.wait_ge(scores_done, 4 * turn + 4)
                        nc.vector.tensor_tensor(s_c[:], ps[0:HEAD, 7, 0:144], at(bias_c, g), ALU.add).then_inc(scores_out, 1)
                        dve.wait_ge(scores_out, 4 * turn + 4)
                        minus_max(c_blk, few, slice(8, 9), sink_c[:, bass.ds(g + KVH, 1)], sink_c[:, bass.ds(g, 1)])
                    if c == 3:
                        dve.wait_ge(exp_done, 3 * turn + 1)
                        normalise(a_blk, every, slice(0, 4), P)
                    if last_turn and c == 4:
                        dve.wait_ge(dec_scores, 1)
                        nc.vector.tensor_copy(sdt[:], ps[:, 6, 0:P]).then_inc(dec_scores_out, 1)
                        nc.vector.tensor_copy(sd_own[:], ps[0:ND, 7, 0:P]).then_inc(dec_scores_out, 1)
                    if c == 5:
                        dve.wait_ge(exp_done, 3 * turn + 3)
                        normalise(b_blk, every, slice(4, 8), 2 * P)
                        normalise(c_blk, few, slice(8, 9), 144)
                    if c == 6:
                        dve.wait_ge(probs_t, 4 * turn + 2)
                        nc.vector.tensor_copy(pt[:, 1, :], ps[:, 7, :]).then_inc(probs_t_dve, 1)
                    if c == 9:
                        dve.wait_ge(probs_t, 4 * turn + 4)
                        nc.vector.tensor_copy(pt_c[:, 0, :], ps[:, 7, 0:HEAD])
                        nc.vector.tensor_copy(pt_c[0:16, 1, :], ps[0:16, 7, HEAD:2 * HEAD]).then_inc(probs_t_dve, 1)
                    if last_turn and c == 9:
                        dve.wait_ge(dec_rows, 1)
                        nc.vector.tensor_copy(sd[:], ps[:, 6, 0:P + 1]).then_inc(dec_rows_out, 1)
                        own.link(nc.vector.tensor_tensor(sd_own8[:], ps[:, 6, 256:256 + ND], masks[:, 0:ND], ALU.mult))
                        own.link(nc.vector.tensor_reduce(dstat[:, 5:6], sd_own8[:], AX.X, ALU.add))
                        nc.vector.tensor_tensor(sd[:, P:P + 1], sd[:, P:P + 1], dstat[:, 5:6], ALU.add).then_inc(dec_rows_out, 1)
                        dve.wait_ge(dec_rows_out, 2)
                        own.link(nc.vector.tensor_reduce(dstat[:, 0:1], sd[:], AX.X, ALU.max))
                        nc.vector.scalar_tensor_tensor(out=dstat[:, 0:1], in0=dstat[:, 0:1], scalar=-1.0, in1=dstat[:, 6:7],
                                                       op0=ALU.mult, op1=ALU.min).then_inc(dec_nmax, 1)
                    if last_turn and c == 11:
                        dve.wait_ge(dec_exp, 1)
                        own.link(nc.vector.tensor_tensor(dstat[:, 4:5], dstat[:, 2:3], dstat[:, 3:4], ALU.add))
                        own.link(nc.vector.reciprocal(dstat[:, 4:5], dstat[:, 4:5]))
                        nc.vector.tensor_scalar(sd[:], sd[:], dstat[:, 4:5], None, ALU.mult).then_inc(dec_probs, 1)
                        dve.wait_ge(dec_probs, 1)
                        nc.vector.tensor_scalar(sd_own8[:], masks[:, 0:ND], sd[:, P:P + 1], None, ALU.mult).then_inc(dec_probs, 1)
                    if c == 12:
                        dve.wait_ge(pv_done, 3 * turn + 3)
                        src = ps[:, 7, 0:HEAD].rearrange("p (i e q) -> p i e q", e=2, q=16)
                        for e in range(2):
                            part = slice(HEAD * e, HEAD * e + HEAD)
                            nc.vector.tensor_copy(zT[part, bass.ds(g * 2, 2), 2 * P:NP], src[part, :, e, :]).then_inc(pv_dve, 1)
                    if last_turn and c == 13:
                        dve.wait_ge(op_hi_ready, KT + 1)
                        nc.vector.tensor_tensor(op_lo[:, 8:14, :], convT[:, 0:6, :], op_hi[:, 8:14, :].bitcast(F32),
                                                ALU.subtract).then_inc(op_lo_ready, 1)
                        dve.wait_ge(dec_pt, 1)
                        nc.vector.tensor_copy(pd[:], ps[:, 6, 0:P]).then_inc(dec_pt_out, 1)
                        nc.vector.tensor_copy(pd_own[:], ps[0:ND, 6, P:2 * P]).then_inc(dec_pt_out, 1)

            with dve.Fori(0, CONV_TURNS - 1) as turn:
                own.begin(turn, TURN_LINKS)
                conv_turn(turn, turn * -1 + (KVH - 1), False)
                own.end(CONV_TURNS - 1)
            conv_turn(CONV_TURNS - 1, 0, True)
            dve.wait_ge(dec_pv, 1)
            for a in range(2):
                for e in range(2):
                    src = ps[HEAD * a:HEAD * a + HEAD, 7, 0:P].rearrange("p (r b h) -> p r h b", r=2, h=8)[:, :, 4 * a + e:4 * a + 4:2, :]
                    dst = zT[HEAD * e:HEAD * e + HEAD, 0:8, NP:N].rearrange("p (r a i) b -> p r a i b", r=2, a=2)[:, :, a]
                    nc.vector.tensor_copy(dst, src).then_inc(dec_pv_out, 1)
            dve.wait_ge(op_hi_ready, KT + 2)
            nc.vector.tensor_tensor(op_lo[:, 0:8, :], zT[:, 0:8, :], op_hi[:, 0:8, :].bitcast(F32), ALU.subtract).then_inc(op_lo_ready, 1)
            dve.wait_ge(op_hi_ready, KT + 3)
            nc.vector.tensor_tensor(op_lo[:, 14:16, :], convT[:, 6:8, :], op_hi[:, 14:16, :].bitcast(F32), ALU.subtract).then_inc(op_lo_ready, 1)

            with dve.Fori(0, 2) as turn:
                for c in range(2 * NC):
                    split(C_OUT + c + RING, c % RING, 1024, turn * (2 * NC))

            def norm_of(k, src, out_ready, scratch, stat_bank, diag_scratch):
                dve.wait_ge(out_ready, 4)
                m = src[:, KT - NB:KT, :]
                dve.wait_ge(mix_acc, k - 1)
                nc.vector.tensor_tensor(scratch[:], m, m, ALU.mult).then_inc(sq_ready, 1)
                dve.wait_ge(stat_done, k - 1)
                nc.vector.tensor_scalar(stat3[:, 0:3], ps[:, stat_bank, 0:12:4], 1.0 / D, EPS, ALU.mult, ALU.add).then_inc(rms_ready, 1)
                diagonals(k, diag_scratch)
                dve.wait_ge(bcast_done, k)

            norm_of(2, mixT, mix_out, sq, 2, diag)

            def input_step(i):
                if i < KT:
                    k = K_ORDER[i]
                    if i >= 2:
                        dve.wait_ge(resid_ready, i - 1)
                    nc.vector.scalar_tensor_tensor(out=tmp[:, i % 2, :], in0=mixT[:, k, :],
                                                   scalar=vec[:, V_POST_MIX + k:V_POST_MIX + k + 1],
                                                   in1=ps[:, 7, 0:N], op0=ALU.mult, op1=ALU.mult).then_inc(scaled, 1)
                if i:
                    low_half(i - 1, K_ORDER[i - 1], V_PRE_FFN, KT + 3)

            def scale_out(dst, bank, ready, c, turn):
                dve.wait_ge(chunk_used, RING + C_FF + c + 1 + turn * (2 * NC))
                nc.vector.tensor_tensor(dst[:], ps[:, bank:bank + NB, 0:N], each(rstd[:], [P, NB, N]), ALU.mult).then_inc(ready, 1)

            def ffn_turn(turn, first):
                for c in range(2 * NC):
                    if first and 2 * c + 4 <= KT:
                        input_step(2 * c + 3)
                        input_step(2 * c + 4)
                    split(C_FF + c + RING, c % RING, 1024, turn * (2 * NC))
                    if c == NC - 1:
                        if first:
                            dve.wait_ge(tot_ready, 1)
                            nc.vector.tensor_scalar(acc4[:, 1, :], acc4[:, 1, :], 1.0 / D, EPS, ALU.mult, ALU.add).then_inc(mean_ready, 1)
                            dve.wait_ge(root_ready, 1)
                            nc.vector.reciprocal(rstd[:], acc4[:, 2, :]).then_inc(ffn_rstd, 1)
                            dve.wait_ge(ffn_rstd, 1)
                        else:
                            dve.wait_ge(hid_lo, turn)
                        scale_out(gate, 0, gate_ready, c, turn)
                    if c == 2 * NC - 1:
                        dve.wait_ge(swish_ready, turn + 1)
                        scale_out(up, NB, up_ready, c, turn)

            for i in range(3):
                input_step(i)
            ffn_turn(0, True)
            with dve.Fori(1, FF_TURNS) as turn:
                ffn_turn(turn, False)

            with dve.Fori(0, (4 * DC - RING) // RING) as turn:
                for c in range(RING):
                    split(C_DOWN + c + RING, c, 1024, turn * RING)
            norm_of(3, yT, y_out, y_sq, 0, y_diag)

            def add_residual(k):
                dve.wait_ge(y_scaled, k + 1)
                nc.vector.tensor_tensor(yT[:, k, :], yT[:, k, :], resid[:, k, :], ALU.add).then_inc(y_ready_dve, 1)

            def rows(q):
                for i in range(3 * q, 3 * q + 3):
                    if i % 2:
                        b = i % 3
                        size = BLOCKS[b][1]
                        dve.wait_ge(yt_done, i + 1)
                        nc.vector.tensor_copy(rows_out[0:size, b, 512 * q:512 * q + 512], ps[0:size, i % 6, :]).then_inc(yt_dve, 1)

            for k in range(KT):
                nc.vector.scalar_tensor_tensor(out=yT[:, k, :], in0=yT[:, k, :], scalar=vec[:, V_POST_FFN + k:V_POST_FFN + k + 1],
                                               in1=ps[:, 7, 0:N], op0=ALU.mult, op1=ALU.mult).then_inc(y_scaled, 1)
                if k % 2 == 0 and k:
                    add_residual(k - 1)
                if k % NB == 2 and k > NB:
                    rows(k // NB - 1)
            add_residual(KT - 1)
            rows(3)


def shape_constants():
    import math
    import numpy as np
    squares = np.stack([np.eye(P), np.eye(P)[::-1]]).astype(np.float32)
    d = 255 - np.arange(BIAS_N)
    exact = BUCKETS // 2
    ratio = np.maximum(d, 1).astype(np.float32) / np.float32(exact)
    far = exact + (np.log(ratio) / np.float32(math.log(WINDOW / exact)) * np.float32(BUCKETS - exact)).astype(np.int32)
    bucket = np.where(d < exact, d, np.minimum(far, BUCKETS - 1))
    onehot = np.zeros((BUCKETS + 1, BIAS_N), np.float32)
    for n in range(BIAS_N):
        if 0 <= d[n] <= WINDOW:
            onehot[bucket[n], n] = 1.0
        else:
            onehot[BUCKETS, n] = MASKED
    row = np.arange(P)[:, None]
    row_masks = np.concatenate([row // HEADS == np.arange(ND), row % HEADS == np.arange(HEADS),
                                row // 16 == np.arange(GROUP)], axis=1).astype(np.float32)
    return dict(squares=squares, onehot=onehot, row_masks=row_masks)


def kernel(x_prompt, x_sample, cache_k, cache_v, state_conv, meta_tokens, rel_bias, w_in, conv_w,
           attn_sinks, w_out, norm_pre_mix, norm_post_mix, norm_pre_ffn, norm_post_ffn, w_gate,
           w_up, w_down):
    import numpy as np
    import concourse.bacc as _bacc
    from concourse.bass_utils import run_bass_kernel_spmd as _run

    inputs = dict(x_prompt=x_prompt, x_sample=x_sample, cache_k=cache_k, cache_v=cache_v,
                  state_conv=state_conv, meta_tokens=meta_tokens, rel_bias=rel_bias, w_in=w_in,
                  conv_w=conv_w, attn_sinks=attn_sinks, w_out=w_out, norm_pre_mix=norm_pre_mix,
                  norm_post_mix=norm_post_mix, norm_pre_ffn=norm_pre_ffn,
                  norm_post_ffn=norm_post_ffn, w_gate=w_gate, w_up=w_up, w_down=w_down)
    inputs.update(shape_constants())
    outputs = dict(y_prompt=(1, SEQ, D), y_sample=(ND, 1, D),
                   k_prompt=(1, 1, WINDOW, KVH, HEAD), v_prompt=(1, 1, WINDOW, KVH, HEAD),
                   conv_prompt=(1, 1, 2, CONV),
                   k_sample=(1, ND, WINDOW, KVH, HEAD), v_sample=(1, ND, WINDOW, KVH, HEAD),
                   conv_sample=(1, ND, 2, CONV))
    nc = _bacc.Bacc("TRN2", target_bir_lowering=False, num_devices=1, dynamic_dma_scratch_size=1024)
    arrays, args = {}, {}
    for name, value in inputs.items():
        arrays[f"in_{name}"] = np.ascontiguousarray(value)
        args[name] = nc.dram_tensor(f"in_{name}", arrays[f"in_{name}"].shape, F32, kind="ExternalInput").ap()
    for name, shape in outputs.items():
        args[name] = nc.dram_tensor(f"out_{name}", shape, F32, kind="ExternalOutput").ap()
    args["bias_rows"] = nc.dram_tensor("bias_rows", (HEADS, BIAS_N), F32, kind="Internal").ap()
    mixer_kernel(nc, **args)
    r = _run(nc, [arrays], core_ids=[0])
    return tuple(r.results[0][f"out_{name}"] for name in outputs)
```

```python
from contextlib import ExitStack

import concourse.bass as bass
from concourse import mybir

F32 = mybir.dt.float32
F32R = mybir.dt.float32r
ALU = mybir.AluOpType
ACT = mybir.ActivationFunctionType
AX = mybir.AxisListType
RADD = bass.bass_isa.ReduceOp.add

P = 128
D = 2048
SEQ = 256
N_META = 16
NP = SEQ + N_META
ND = 8
N = NP + ND
HEAD = 64
HEADS = 16
KVH = 4
GROUP = HEADS // KVH
WINDOW = 128
CONV = 1024
BUCKETS = 32
FF = 5632
IN = 4608
EPS = 1e-6
MASKED = -1e30

T0 = N_META
M = N - T0
U0 = T0 - 2
NU = N - U0
ALL, WANTED = slice(0, N), slice(T0, N)
KEYS_A = T0 + P
OUT_BLOCKS = [(0, P), (P, P), (2 * P, ND)]

KT = D // P
FT = FF // P
CT = CONV // P
RING = 4
NA = 3
NB = 4
ORDER = [4, 5, 6, 0, 1, 2, 3, 7]
NC = len(ORDER)
DC = FT // 2
K_ORDER = [2 * c + j for c in ORDER for j in range(2)]
K_ORDER = [2 * c + j for c in ORDER for j in range(2)]
K_ORDER = [2 * c + j for c in ORDER for j in range(2)]
K_ORDER = [2 * c + j for c in ORDER for j in range(2)]
K_ORDER = [2 * c + j for c in ORDER for j in range(2)]
K_ORDER = [2 * c + j for c in ORDER for j in range(2)]
K_ORDER = [2 * c + j for c in ORDER for j in range(2)]
K_ORDER = [2 * c + j for c in ORDER for j in range(2)]
QKV_TURNS = 2
CONV_TURNS = 4
FF_TURNS = FT // NB
C_QKV = 0
C_CONV = C_QKV + QKV_TURNS * 2 * NC
C_OUT = C_CONV + CONV_TURNS * 2 * NC
C_FF = C_OUT + 4 * NC
C_DOWN = C_FF + FF_TURNS * 2 * NC
C_END = C_DOWN + 4 * DC
BLOCKS = [(0, 128), (128, 128), (256, N - 256)]
V_PRE_MIX, V_POST_MIX, V_PRE_FFN, V_POST_FFN, V_CONV = 0, KT, 2 * KT, 3 * KT, 4 * KT
NVEC = V_CONV + 3 * CT
EXT = SEQ + 2 + 3 * ND
LEAD = 7
BIAS_N = 384


def mixer_kernel(nc, x_prompt, x_sample, cache_k, cache_v, state_conv, meta_tokens, rel_bias, w_in,
                 conv_w, attn_sinks, w_out, norm_pre_mix, norm_post_mix, norm_pre_ffn,
                 norm_post_ffn, w_gate, w_up, w_down, squares, onehot, row_masks,
                 y_prompt, y_sample, k_prompt, v_prompt, conv_prompt, k_sample, v_sample,
                 conv_sample, bias_rows):
    with ExitStack() as ctx:
        def sem(name):
            return ctx.enter_context(nc.semaphore(name))

        def place(name, shape, start, dt=F32):
            size = 4
            for s in shape[1:]:
                size *= s
            end = start + -(-size // 32) * 32
            assert end <= nc.sbuf_usable_end, (name, end)
            return nc.alloc_sbuf_tensor_at(name, shape, dt, offset=start), end

        e = -(-nc.sbuf_base // 32) * 32
        ident, e = place("ident", [P, P], e)
        ones, e = place("ones", [P, P], e)
        vec, e = place("vec", [P, NVEC], e)
        rstd, e = place("rstd", [P, N], e)
        eps, e = place("eps", [P, 1], e)
        stat3, e = place("stat3", [P, 8], e)
        resid, operand = place("resid", [P, KT, N], e)
        op_hi, e = place("op_hi", [P, KT, N], operand, F32R)
        op_lo, e = place("op_lo", [P, KT, N], e, F32R)
        raw, e = place("raw", [P, RING, 2, 512], e)
        w_hi, e = place("w_hi", [P, RING, 1024], e, F32R)
        w_lo, area = place("w_lo", [P, RING, 1024], e, F32R)
        h_hi, e = place("h_hi", [P, FT, M], area, F32R)
        h_lo, e = place("h_lo", [P, FT, M], e, F32R)
        gate, e = place("gate", [P, NB, M], e)
        up, keep = place("up", [P, NB, M], e)
        kv_rows, e = place("kv_rows", [P, 4 * P], keep)
        kv_dec, e = place("kv_dec", [ND, 4 * P], e)
        conv_rows, e = place("conv_rows", [2 + ND, CONV], e)
        yT, yT_end = place("yT", [P, KT, M], operand)
        y_sq, e = place("y_sq", [P, NB, M], yT_end)
        y_acc, e = place("y_acc", [P, NB, M], e)
        y_root, e = place("y_root", [P, M], e)
        rows_out, _ = place("rows_out", [P, 3, D], area)
        zT, conv_area = place("zT", [P, 12, N], area)
        convT, zb_area = place("convT", [P, CT, M], conv_area)
        zb, e = place("zb", [P, 2, NA, NU], zb_area)
        after_zb = e
        bias, e = place("bias", [P, HEADS, 2 * P], e)
        u_ext, e = place("u_ext", [P, EXT], e)
        tap, e = place("tap", [P, EXT - 2], e)
        acc, e = place("acc", [P, EXT - 2], e)
        cw, e = place("cw", [P, 3], e)
        state_t, e = place("state_t", [P, CT, 2 * ND], e)
        u_out, e = place("u_out", [P, CT, 2 + ND], e)
        kd, e = place("kd", [P, KVH, NP], e)
        vd, e = place("vd", [P, 3, 2 * P], e)
        sink, e = place("sink", [P, HEADS], e)
        nsink, e = place("nsink", [P, HEADS], e)
        masks, e = place("masks", [P, ND + HEADS], e)
        vc, e = place("vc", [P, ND, 2 * P], e)
        kct, e = place("kct", [P, ND, 2, P], e)
        onehot_s, e = place("onehot_s", [BUCKETS + 1, BIAS_N], e)
        table, e = place("table", [BUCKETS + 1, HEADS], e)
        table_d, e = place("table_d", [BUCKETS + 1, ND, HEADS], e)
        flip, attn = place("flip", [P, P], e)
        rows_in, _ = place("rows_in", [P, 3, D], attn)
        hankel, e = place("hankel", [P, HEADS, 2 * P], attn)
        qs, e = place("qs", [P, GROUP, 2 * P], attn)
        ks, e = place("ks", [P, NP], e)
        vs, e = place("vs", [P, 3, 2, HEAD], e)
        s_a, e = place("s_a", [P, GROUP, KEYS_A], e)
        s_b, e = place("s_b", [P, GROUP, 2 * P], e)
        nmax, e = place("nmax", [P, 12], e)
        den, e = place("den", [P, 12], e)
        esk, e = place("esk", [P, 12], e)
        pt, e = place("pt", [P, 3, 512], e)
        pt_m, e = place("pt_m", [N_META, 512], e)
        qd, e = place("qd", [P, 2, ND, 2 * GROUP], e)
        sd, e = place("sd", [P, P + 1], e)
        sd_own8, e = place("sd_own8", [P, ND], e)
        sdt, e = place("sdt", [P, P], e)
        sd_own, e = place("sd_own", [ND, P], e)
        pd, e = place("pd", [P, P], e)
        pd_own, e = place("pd_own", [ND, P], e)
        dstat, e = place("dstat", [P, 8], e)
        sinks_m, e = place("sinks_m", [P, HEADS], e)
        assert e <= keep
        kc, _ = place("kc", [P, ND, 2 * P], conv_area)
        vec_rows, e = place("vec_rows", [NVEC, P], zb_area)
        state_rows, e = place("state_rows", [2 * ND, CONV], e)
        bias_sb, e = place("bias_sb", [HEADS, BIAS_N], e)
        assert e <= after_zb
        mixT, e = place("mixT", [P, KT, M], after_zb)
        sq, e = place("sq", [P, NB, M], max(e, attn))
        acc4, e = place("acc4", [P, NB, M], e)
        root, e = place("root", [P, M], e)
        inv, e = place("inv", [P, M], e)
        tmp, e = place("tmp", [P, 2, M], e)
        assert e <= keep
        x_diag, _ = place("x_diag", [P, 3, P], after_zb)

        ps = ctx.enter_context(nc.psum_tensor("ps", [P, 8, 512], F32))

        raw_landed = [sem(f"raw_landed{s}") for s in range(RING)]
        hi_ready = sem("hi_ready")
        lo_ready = sem("lo_ready")
        chunk_used = sem("chunk_used")
        x_in, const_in, vec_in, table_in = sem("x_in"), sem("const_in"), sem("vec_in"), sem("table_in")
        kcache_in, state_in, sink_in, vcache_in = sem("kcache_in"), sem("state_in"), sem("sink_in"), sem("vcache_in")
        filled = sem("filled")
        vec_done, vec_out, table_d_ready = sem("vec_done"), sem("vec_out"), sem("table_d_ready")
        rel_done, rel_out, rel_stored, hankel_in = sem("rel_done"), sem("rel_out"), sem("rel_stored"), sem("hankel_in")
        xt_done, xt_out, x_squared = sem("xt_done"), sem("xt_out"), sem("x_squared")
        op_hi_ready, op_lo_ready = sem("op_hi_ready"), sem("op_lo_ready")
        rms_ready, inv_ready, diag_ready, bcast_done = sem("rms_ready"), sem("inv_ready"), sem("diag_ready"), sem("bcast_done")
        rstd_ready = sem("rstd_ready")
        z_out = sem("z_out")
        bias_done, bias_out = sem("bias_done"), sem("bias_out")
        kct_done, kct_out = sem("kct_done"), sem("kct_out")
        kv_done, kv_out, kd_ready = sem("kv_done"), sem("kv_out"), sem("kd_ready")
        state_done, state_out = sem("state_done"), sem("state_out")
        zeroed, q_staged, k_staged, v_staged, qd_staged = (sem("zeroed"), sem("q_staged"), sem("k_staged"),
                                                           sem("v_staged"), sem("qd_staged"))
        scores_done, scores_out = sem("scores_done"), sem("scores_out")
        nmax_ready, exp_done, probs_ready = sem("nmax_ready"), sem("exp_done"), sem("probs_ready")
        probs_t = sem("probs_t")
        probs_t_act, probs_t_dve = sem("probs_t_act"), sem("probs_t_dve")
        pv_done, pv_act = sem("pv_done"), sem("pv_act")
        dec_scores, dec_scores_out, dec_rows, dec_rows_out = (sem("dec_scores"), sem("dec_scores_out"),
                                                              sem("dec_rows"), sem("dec_rows_out"))
        dec_nmax, dec_exp, dec_probs = sem("dec_nmax"), sem("dec_exp"), sem("dec_probs")
        dec_pt, dec_pt_out, dec_pv, dec_pv_out = sem("dec_pt"), sem("dec_pt_out"), sem("dec_pv"), sem("dec_pv_out")
        zb_ready, conv_done = sem("zb_ready"), sem("conv_done")
        mix_out, sq_ready, acc_ready, sums_done = sem("mix_out"), sem("sq_ready"), sem("acc_ready"), sem("sums_done")
        pool_sums = sem("pool_sums")
        scaled, resid_ready, rsq_ready, rsum = sem("scaled"), sem("resid_ready"), sem("rsq_ready"), sem("rsum")
        tot_ready, root_ready, rms_inverse = sem("tot_ready"), sem("root_ready"), sem("rms_inverse")
        crow_done, crow_out = sem("crow_done"), sem("crow_out")
        gate_ready, sig_ready, swish_ready = sem("gate_ready"), sem("sig_ready"), sem("swish_ready")
        up_ready, hid_ready, hid_hi, hid_lo = sem("up_ready"), sem("hid_ready"), sem("hid_hi"), sem("hid_lo")
        y_out, y_scaled, y_ready_pool, y_ready_dve = sem("y_out"), sem("y_scaled"), sem("y_ready_pool"), sem("y_ready_dve")
        yt_done, yt_act, yt_dve = sem("yt_done"), sem("yt_act"), sem("yt_dve")
        stored = sem("stored")
        dve_own, pool_own = sem("dve_own"), sem("pool_own")

        class Own:

            def __init__(self, engine, semaphore):
                self.engine, self.semaphore, self.n, self.turn = engine, semaphore, 0, 0

            def link(self, instruction):
                instruction.then_inc(self.semaphore, 1)
                self.n += 1
                self.engine.wait_ge(self.semaphore, self.n + self.turn)

            def begin(self, turn, per_turn):
                self.turn, self.mark, self.per = turn * per_turn, self.n, per_turn

            def end(self, turns):
                assert self.n - self.mark == self.per, (self.n - self.mark, self.per)
                self.turn, self.n = 0, self.mark + turns * self.per

        def each(ap, shape):
            return ap.unsqueeze(1).broadcast_to(shape)

        def heads4(ap):
            return ap.rearrange("p (h k) -> p h k", h=GROUP)

        def at(ap, i):
            return ap[:, bass.ds(i, 1)].rearrange("p a n -> p (a n)")

        block = ctx.enter_context(nc.Block())

        @block.sync
        def _(sp):
            sp.dma_start(rows_in[0:N_META, 0, :], meta_tokens).then_inc(x_in, 16)
            sp.dma_start(rows_in[N_META:P, 0, :], x_prompt[0, 0:P - N_META, :]).then_inc(x_in, 16)
            sp.dma_start(rows_in[:, 1, :], x_prompt[0, P - N_META:2 * P - N_META, :]).then_inc(x_in, 16)
            sp.dma_start(rows_in[0:N_META, 2, :], x_prompt[0, SEQ - N_META:SEQ, :]).then_inc(x_in, 16)
            sp.dma_start(rows_in[N_META:N_META + ND, 2, :], x_sample[:, 0, :]).then_inc(x_in, 16)

            def load(n, slot, src, dst, turn=0):
                sp.wait_ge(lo_ready, n + 1 + turn)
                sp.dma_start(dst, src).then_inc(raw_landed[slot], 16)

            def rows_of(w, chunk, col, width):
                return w[chunk * 2 * P:(chunk + 1) * 2 * P, bass.ds(col, width)].rearrange(
                    "(j p) n -> p j n", p=P)

            for c in range(QKV_TURNS * 2 * NC):
                if c == RING:
                    sp.wait_ge(rel_out, 1)
                    sp.dma_start(bias_rows, bias_sb[:]).then_inc(rel_stored, 16)
                    sp.wait_ge(rel_stored, 16)
                    sp.wait_ge(xt_done, KT)
                    sp.wait_ge(x_squared, 3)
                    sp.dma_start(hankel[:], bass.AP(bias_rows.tensor, 0, [[1, P], [BIAS_N, HEADS], [1, 2 * P]])).then_inc(hankel_in, 16)
                load(C_QKV + c, c % RING, rows_of(w_in[0], ORDER[c % NC], 1152 - 384 * (c // NC), 384),
                     raw[:, c % RING, :, 0:384])
            parts = w_in[0][:, IN - 3 * CONV:IN].rearrange("k (a n) -> k a n", a=3)
            with sp.Fori(0, CONV_TURNS) as turn:
                for c in range(2 * NC):
                    chunk = ORDER[c % NC]
                    sp.wait_ge(lo_ready, C_CONV + c + 1 + turn * (2 * NC))
                    for j in range(2):
                        k = 2 * chunk + j
                        sp.dma_start(raw[:, c % RING, j, 0:384].rearrange("p (a n) -> p a n", a=3),
                                     parts[k * P:k * P + P, :, bass.ds(turn * (2 * P) + c // NC * P, P)]
                                     ).then_inc(raw_landed[c % RING], 16)

            def column(turn, width, k):
                return (turn + turn) * (width // 2) if k == 0 else turn * width

            with sp.Fori(0, 2) as turn:
                for c in range(2 * NC):
                    load(C_OUT + c, c % RING, rows_of(w_out[0][:, c // NC * 512:], ORDER[c % NC], column(turn, 1024, ORDER[c % NC]), 512),
                         raw[:, c % RING], turn * (2 * NC))
            sp.wait_ge(kv_out, 4)
            flat = "t h d -> t (h d)"
            sp.dma_start(k_prompt[0, 0].rearrange(flat), kv_rows[:, 0:2 * P]).then_inc(stored, 16)
            sp.dma_start(v_prompt[0, 0].rearrange(flat), kv_rows[:, 2 * P:4 * P]).then_inc(stored, 16)
            sp.dma_start(k_sample[0, :, WINDOW - 1].rearrange(flat), kv_dec[:, 0:2 * P]).then_inc(stored, 16)
            sp.dma_start(v_sample[0, :, WINDOW - 1].rearrange(flat), kv_dec[:, 2 * P:4 * P]).then_inc(stored, 16)
            for cache, out in ((cache_k, k_sample), (cache_v, v_sample)):
                for b in range(ND):
                    sp.dma_start(out[0, b, 0:WINDOW - 1].rearrange(flat),
                                 cache[0, b, 1:WINDOW].rearrange(flat)).then_inc(stored, 16)
            sp.dma_start(conv_sample[0, :, 0, :], state_conv[0, :, 1, :]).then_inc(stored, 16)
            with sp.Fori(0, FF_TURNS) as turn:
                for c in range(2 * NC):
                    w = (w_gate, w_up)[c // NC][0]
                    load(C_FF + c, c % RING, rows_of(w, ORDER[c % NC], column(turn, 512, ORDER[c % NC]), 512),
                         raw[:, c % RING], turn * (2 * NC))
            sp.wait_ge(crow_out, 1)
            sp.dma_start(conv_prompt[0, 0], conv_rows[0:2, :]).then_inc(stored, 16)
            sp.dma_start(conv_sample[0, :, 1, :], conv_rows[2:2 + ND, :]).then_inc(stored, 16)
            with sp.Fori(0, 2) as turn:
                for c in range(2 * DC):
                    load(C_DOWN + c, c % RING, rows_of(w_down[0][:, c // DC * 512:], c % DC, column(turn, 1024, c % DC), 512),
                         raw[:, c % RING], turn * (2 * DC))
            for q in range(4):
                cols = slice(512 * q, 512 * q + 512)
                for b, (t, size) in enumerate(OUT_BLOCKS):
                    i = 3 * q + b
                    sp.wait_ge((yt_act, yt_dve)[i % 2], i // 2 + 1)
                    dst = y_prompt[0, t:t + size, cols] if b < 2 else y_sample[:, 0, cols]
                    sp.dma_start(dst, rows_out[0:size, b, cols]).then_inc(stored, 16)
            sp.wait_ge(stored, 16 * (4 + 2 * ND + 1 + 2 + 12))

        @block.tensor
        def _(pe):
            def tr(out, in_):
                n = in_.shape[0]
                return nc.tensor.transpose(out, in_, ident[0:n, 0:n])

            def chunk(slot, tiles, bank, k0, moving_hi, moving_lo, first, last, out, cols):
                for m in range(tiles):
                    for j in range(2):
                        col = (j * tiles + m) * P
                        hi, lo = w_hi[:, slot, col:col + P], w_lo[:, slot, col:col + P]
                        for i, (w, x) in enumerate(((hi, moving_hi), (hi, moving_lo), (lo, moving_hi))):
                            mm = nc.tensor.matmul(ps[:, bank + m, out], w, x[:, k0 + j, cols],
                                                  start=first and j == 0 and i == 0,
                                                  stop=last and j == 1 and i == 2)
                return mm

            def project(n, c, slot, tiles, bank, out, cols, turn=0):
                pe.wait_ge(lo_ready, RING + n + 1 + turn)
                mm = chunk(slot, tiles, bank, 2 * ORDER[c], op_hi, op_lo, c == 0, c == NC - 1, out, cols)
                mm.then_inc(chunk_used, 1)

            def spread(scratch, bank):
                pe.wait_ge(diag_ready, 1)
                nc.tensor.matmul(ps[:, bank, 0:2 * P], ones[:], scratch[:, 0:2, :], start=True, stop=True)
                nc.tensor.matmul(ps[:, bank, 2 * P:N], ones[:], scratch[:, 2, 0:N - 2 * P], start=True, stop=True).then_inc(bcast_done, 1)

            pe.wait_ge(const_in, 48)
            pe.wait_ge(vec_in, 80)
            tr(ps[:, 7, 0:NVEC], vec_rows[:]).then_inc(vec_done, 1)
            pe.wait_ge(table_in, 32)
            pe.wait_ge(filled, 4)
            nc.tensor.matmul(ps[0:HEADS, 6, 0:BIAS_N], table[:], onehot_s[:], start=True, stop=True).then_inc(rel_done, 1)
            pe.wait_ge(x_in, 80)
            for i, k in enumerate(K_ORDER):
                if i >= 6:
                    pe.wait_ge(xt_out, i - 5)
                for b, (t, size) in enumerate(BLOCKS):
                    mm = tr(ps[:, i % 6, t:t + size], rows_in[0:size, b, k * P:k * P + P])
                mm.then_inc(xt_done, 1)

            for c in range(QKV_TURNS * 2 * NC):
                if c < NC:
                    pe.wait_ge(op_lo_ready, 2 * c + 2)
                if c == 0:
                    pe.wait_ge(xt_out, KT)
                wanted = ALL if c < 2 * NC else WANTED
                project(C_QKV + c, c % NC, c % RING, NA, NA * (c // NC % 2), wanted, wanted)
                if c == 2:
                    spread(x_diag, 6)
                if 4 <= c < 4 + HEADS // 2:
                    i = c - 4
                    if i == 0:
                        pe.wait_ge(hankel_in, 16)
                        pe.wait_ge(rstd_ready, 1)
                    if i >= 2:
                        pe.wait_ge(bias_out, i - 1)
                    nc.tensor.matmul(ps[:, 6 + i % 2, :], flip[:], hankel[:, 2 * i:2 * i + 2, :],
                                     start=True, stop=True).then_inc(bias_done, 1)
                if 12 <= c < 16:
                    i = c - 12
                    if i == 0:
                        pe.wait_ge(kcache_in, 16)
                    if i < 2:
                        pe.wait_ge(bias_out, HEADS // 2 - 1 + i)
                    else:
                        pe.wait_ge(kct_out, i - 1)
                    for m in range(4):
                        b, r = 2 * i + m // 2, m % 2
                        mm = tr(ps[:, 6 + i % 2, m * P:m * P + P], kc[:, b, r * P:r * P + P])
                    mm.then_inc(kct_done, 1)
                if c == 17:
                    pe.wait_ge(z_out, 2)
                    pe.wait_ge(kct_out, 3)
                    for m in range(4):
                        b, r = m // 2, m % 2
                        mm = tr(ps[:, 6, m * P:m * P + P], zT[:, 10 + r, T0 + b * P:T0 + b * P + P])
                    mm.then_inc(kv_done, 1)
                if c == 18:
                    pe.wait_ge(kct_out, 4)
                    for r in range(2):
                        mm = tr(ps[0:N_META, 7, r * P:r * P + P], zT[:, 10 + r, 0:N_META])
                    mm.then_inc(kv_done, 1)
                if c == 19:
                    pe.wait_ge(kv_out, 1)
                    for m in range(4):
                        mm = tr(ps[:, 6, m * P:m * P + P], zT[:, 8 + m, NP - WINDOW:NP])
                    mm.then_inc(kv_done, 1)
                if c == 20:
                    pe.wait_ge(kv_out, 2)
                    for m in range(4):
                        mm = tr(ps[0:ND, 7, m * P:m * P + P], zT[:, 8 + m, NP:N])
                    mm.then_inc(kv_done, 1)
                if c == 22:
                    pe.wait_ge(state_in, 16)
                    pe.wait_ge(kv_out, 3)
                    for j in range(CT):
                        mm = tr(ps[:, 6, j * 2 * ND:(j + 1) * 2 * ND], state_rows[:, j * P:j * P + P])
                    mm.then_inc(state_done, 1)

            def conv_turn(turn, last_turn):
                for c in range(2 * NC):
                    project(C_CONV + c, c % NC, c % RING, NA, NA * (c // NC), slice(0, NU), slice(U0, N), turn * (2 * NC))
                    if c == 0:
                        pe.wait_ge(q_staged, 2 * turn + 2)
                        pe.wait_ge(k_staged, turn + 1)
                        for h in range(GROUP):
                            mm = nc.tensor.matmul(ps[:, 6, h * P:h * P + P], qs[:, h, 0:P], ks[:, T0:KEYS_A],
                                                  start=True, stop=True)
                        mm.then_inc(scores_done, 1)
                        for h in range(GROUP):
                            mm = nc.tensor.matmul(ps[:, 7, h * N_META:(h + 1) * N_META], qs[:, h, 0:P], ks[:, 0:N_META],
                                                  start=True, stop=True)
                        mm.then_inc(scores_done, 1)
                    if c in (1, 2):
                        pe.wait_ge(scores_out, 4 * turn + c)
                        for i in range(2):
                            mm = nc.tensor.matmul(ps[:, 5 + c, i * 256:i * 256 + 256], qs[:, 2 * (c - 1) + i, P:2 * P],
                                                  ks[:, T0:NP], start=True, stop=True)
                        mm.then_inc(scores_done, 1)
                    if last_turn and c == 4:
                        pe.wait_ge(scores_out, 4 * turn + 4)
                        pe.wait_ge(qd_staged, 8)
                        for b in range(ND):
                            for r in range(2):
                                mm = nc.tensor.matmul(ps[:, 6, b * HEADS + 8 * r:b * HEADS + 8 * r + 8],
                                                      kct[:, b, r, :], qd[:, r, b, :], start=True, stop=True)
                        own = ps[0:ND, 7, 0:P].rearrange("p (b r h) -> p r b h", r=2, h=8)
                        for r in range(2):
                            mm = nc.tensor.matmul(own[:, r], zT[:, 8 + r, NP:N], qd[:, r], start=True, stop=True)
                        mm.then_inc(dec_scores, 1)
                    if c in (5, 6, 7, 8):
                        if c == 5:
                            pe.wait_ge(probs_ready, 2 * turn + 1)
                            if last_turn:
                                pe.wait_ge(dec_scores_out, 2)
                            else:
                                pe.wait_ge(scores_out, 4 * turn + 3)
                            src = s_a[:, :, T0:KEYS_A]
                        if c == 6:
                            pe.wait_ge(scores_out, 4 * turn + 4)
                            src = s_a[:, :, 0:N_META]
                        if c == 7:
                            pe.wait_ge(probs_ready, 2 * turn + 2)
                            pe.wait_ge(probs_t_act, 2 * turn + 1)
                            src = s_b[:, :, 0:P]
                        if c == 8:
                            pe.wait_ge(probs_t_dve, 2 * turn + 1)
                            src = s_b[:, :, P:2 * P]
                        for h in range(GROUP):
                            mm = tr(ps[0:src.shape[2], 6 if c % 2 else 7, h * P:h * P + P], src[:, h])
                        mm.then_inc(probs_t, 1)
                    if last_turn and c == 9:
                        pe.wait_ge(probs_t_act, 2 * turn + 2)
                        nc.tensor.matmul(ps[:, 6, 0:P + 1], table_d[:].rearrange("p b h -> p (b h)"),
                                         onehot_s[:, P - 1:2 * P], start=True, stop=False)
                        nc.tensor.matmul(ps[:, 6, 0:P], sdt[:], ident[:], start=False, stop=True)
                        tr(ps[:, 6, 256:256 + ND], sd_own[:]).then_inc(dec_rows, 1)
                    if c == 10:
                        pe.wait_ge(v_staged, 4 * turn + 4)
                        pe.wait_ge(probs_t_act, 2 * turn + 1)
                        pe.wait_ge(probs_t_dve, 2 * turn + 2)
                        nc.tensor.matmul(ps[:, 7, :], vs[:, 0].rearrange("p a d -> p (a d)"), pt[:, 0, :],
                                         start=True, stop=False)
                        nc.tensor.matmul(ps[:, 7, :], vs[0:N_META, 2].rearrange("p a d -> p (a d)"), pt_m[:],
                                         start=False, stop=True).then_inc(pv_done, 1)
                    if c == 11:
                        pe.wait_ge(probs_t_act, 2 * turn + 2)
                        if last_turn:
                            pe.wait_ge(dec_rows_out, 2)
                        nc.tensor.matmul(ps[:, 6, :], vs[:, 0].rearrange("p a d -> p (a d)"), pt[:, 1, :],
                                         start=True, stop=False)
                        nc.tensor.matmul(ps[:, 6, :], vs[:, 1].rearrange("p a d -> p (a d)"), pt[:, 2, :],
                                         start=False, stop=True).then_inc(pv_done, 1)
                    if last_turn and c == 13:
                        pe.wait_ge(dec_probs, 2)
                        pe.wait_ge(pv_act, 4 * turn + 4)
                        tr(ps[:, 6, 0:P], sd[:, 0:P])
                        tr(ps[0:ND, 6, P:2 * P], sd_own8[:]).then_inc(dec_pt, 1)
                    if last_turn and c == 15:
                        pe.wait_ge(dec_pt_out, 2)
                        pe.wait_ge(vcache_in, 16)
                        pe.wait_ge(kv_out, 4)
                        own = pd_own[:].rearrange("p (b r h) -> p r b h", r=2, h=8)
                        for r in range(2):
                            out = ps[:, 7, HEAD * r:HEAD * r + HEAD]
                            nc.tensor.matmul(out.rearrange("p (b h) -> p b h", h=8), kv_dec[:, 2 * P + r * P:3 * P + r * P],
                                             own[:, r], start=True, stop=False)
                            for b in range(ND):
                                mm = nc.tensor.matmul(out[:, 8 * b:8 * b + 8], vc[:, b, r * P:r * P + P],
                                                      pd[:, b * HEADS + 8 * r:b * HEADS + 8 * r + 8],
                                                      start=False, stop=b == ND - 1)
                        mm.then_inc(dec_pv, 1)

            with pe.Fori(0, CONV_TURNS - 1) as turn:
                conv_turn(turn, False)
            conv_turn(CONV_TURNS - 1, True)

            pe.wait_ge(zb_ready, CT)
            pe.wait_ge(dec_pv_out, 4)
            with pe.Fori(0, 2) as turn:
                for c in range(2 * NC):
                    if c < NC:
                        pe.wait_ge(op_lo_ready, KT + (1 if c < 3 else 2 if c < 7 else 3))
                    project(C_OUT + c, c % NC, c % RING, NB, NB * (c // NC), slice(0, M), WANTED, turn * (2 * NC))

            def token_sums(k, total, last, bank):
                pe.wait_ge(acc_ready, k)
                nc.tensor.matmul(ps[:, bank, 0:M], ones[:], total[:, 0, :], start=True, stop=False)
                for m in range(NB):
                    if m % 2 == 0:
                        pe.wait_ge(sq_ready, 5 * (k - 1) + 4 + m // 2)
                    mm = nc.tensor.matmul(ps[:, bank, 0:M], ones[:], last[:, m, :], start=False, stop=m == NB - 1)
                mm.then_inc(sums_done, 1)

            pe.wait_ge(mix_out, 3)
            token_sums(1, acc4, sq, 2)
            pe.wait_ge(conv_done, CT)
            for j in range(CT):
                mm = tr(ps[0:2 + ND, j // 4, j % 4 * P:j % 4 * P + P], u_out[:, j, :])
            mm.then_inc(crow_done, 1)

            pe.wait_ge(crow_out, 1)
            pe.wait_ge(root_ready, 1)
            pe.wait_ge(mix_out, 4)
            with pe.Fori(0, FF_TURNS) as turn:
                for c in range(2 * NC):
                    if c < NC:
                        pe.wait_ge(op_lo_ready, KT + 3 + 2 * c + 2)
                    project(C_FF + c, c % NC, c % RING, NB, NB * (c // NC), slice(0, M), WANTED, turn * (2 * NC))

            with pe.Fori(0, 2) as turn:
                for c in range(2 * DC):
                    k = c % DC
                    pe.wait_ge(lo_ready, RING + C_DOWN + c + 1 + turn * (2 * DC))
                    if c < DC and k * 2 + 2 > FT - NB:
                        pe.wait_ge(hid_lo, FF_TURNS)
                    elif c == 0:
                        pe.wait_ge(hid_lo, FF_TURNS - 1)
                        pe.wait_ge(up_ready, FF_TURNS)
                    chunk(c % RING, NB, NB * (c // DC), 2 * k, h_hi, h_lo, k == 0, k == DC - 1,
                          slice(0, M), slice(0, M)).then_inc(chunk_used, 1)
            token_sums(2, y_acc, y_sq, 0)
            pe.wait_ge(y_out, 4)
            for q in range(4):
                for b, (t, size) in enumerate(OUT_BLOCKS):
                    i = 3 * q + b
                    if b == 0:
                        pe.wait_ge(y_ready_pool, q + 1)
                        pe.wait_ge(y_ready_dve, 3 * q + 3)
                    if i >= 6:
                        pe.wait_ge((yt_act, yt_dve)[i % 2], (i - 6) // 2 + 1)
                    for m in range(NB):
                        mm = tr(ps[0:size, i % 6, m * P:m * P + P], yT[:, NB * q + m, t:t + size])
                    mm.then_inc(yt_done, 1)

        @block.gpsimd
        def _(pool):
            own = Own(pool, pool_own)
            nc.gpsimd.memset(stat3[:, 6:7], 0.0).then_inc(lo_ready, RING)
            nc.gpsimd.memset(cw[:], 0.0).then_inc(chunk_used, RING)
            own.link(nc.gpsimd.memset(eps[:], EPS))
            nc.gpsimd.memset(stat3[:, 7:8], -0.5).then_inc(filled, 1)
            nc.gpsimd.memset(stat3[:, 0:3], 1.0).then_inc(filled, 1)
            pool.wait_ge(filled, 2)
            nc.gpsimd.memset(table[BUCKETS:BUCKETS + 1, :], 1.0).then_inc(filled, 1)
            pool.wait_ge(filled, 3)
            nc.gpsimd.memset(ones[:], 1.0).then_inc(filled, 1)
            pool.wait_ge(filled, 4)

            pool.wait_ge(rms_ready, 1)
            nc.gpsimd.tensor_tensor(stat3[:, 3:6], stat3[:, 0:3], stat3[:, 7:8].broadcast_to([P, 3]),
                                    ALU.pow).then_inc(inv_ready, 1)

            def stage_k(g):
                nc.gpsimd.tensor_copy(ks[:], at(kd, g)).then_inc(k_staged, 1)

            def stage_v(g):
                for half in range(2):
                    nc.gpsimd.tensor_copy(vs[:, 0:2, half, :], vd[:, 0:2, bass.ds(g * HEAD, HEAD)]).then_inc(v_staged, 1)
                    nc.gpsimd.tensor_copy(vs[0:16, 2, half, :], vd[0:16, 2, bass.ds(g * HEAD, HEAD)]).then_inc(v_staged, 1)

            def tap_of(i):
                return cw[:, i:i + 1].broadcast_to([P, EXT - 2])

            def conv_tile(j, half):
                pool.wait_ge(zb_ready, j + 1)
                g, c, h = (zb[:, half, i, :] for i in range(3))
                dec = u_ext[:, SEQ + 2:EXT].rearrange("p (b t) -> p b t", t=3)
                kept, out = at(u_out, j), at(convT, j)
                taps = vec[:, V_CONV:NVEC].rearrange("p (i j) -> p i j", j=CT)[:, :, bass.ds(j, 1)]
                own.link(nc.gpsimd.tensor_copy(cw[:], taps.rearrange("p i j -> p (i j)")))
                own.link(nc.gpsimd.tensor_copy(dec[:, :, 0:2], at(state_t, j).rearrange("p (b t) -> p b t", t=2)))
                own.link(nc.gpsimd.tensor_tensor(u_ext[:, 0:SEQ + 2], c[:, 0:SEQ + 2], h[:, 0:SEQ + 2], ALU.mult))
                own.link(nc.gpsimd.tensor_tensor(dec[:, :, 2], c[:, SEQ + 2:NU], h[:, SEQ + 2:NU], ALU.mult))
                own.link(nc.gpsimd.tensor_tensor(acc[:], u_ext[:, 0:EXT - 2], tap_of(0), ALU.mult))
                own.link(nc.gpsimd.tensor_tensor(tap[:], u_ext[:, 1:EXT - 1], tap_of(1), ALU.mult))
                own.link(nc.gpsimd.tensor_tensor(acc[:], acc[:], tap[:], ALU.add))
                own.link(nc.gpsimd.tensor_tensor(tap[:], u_ext[:, 2:EXT], tap_of(2), ALU.mult))
                own.link(nc.gpsimd.tensor_tensor(acc[:], acc[:], tap[:], ALU.add))
                nc.gpsimd.tensor_copy(kept[:, 0:2], u_ext[:, SEQ:SEQ + 2])
                nc.gpsimd.tensor_copy(kept[:, 2:2 + ND], dec[:, :, 2])
                nc.gpsimd.tensor_tensor(out[:, 0:SEQ], acc[:, 0:SEQ], g[:, 2:SEQ + 2], ALU.mult)
                nc.gpsimd.tensor_tensor(out[:, SEQ:M], acc[:, SEQ + 2:EXT - 2:3], g[:, SEQ + 2:NU], ALU.mult).then_inc(conv_done, 1)

            CONV_LINKS = 9

            pool.wait_ge(bias_done, HEADS // 2)
            nc.gpsimd.memset(qs[:], 0.0).then_inc(zeroed, 1)
            nc.gpsimd.memset(qd[:], 0.0).then_inc(zeroed, 1)
            pool.wait_ge(zeroed, 2)
            pool.wait_ge(kd_ready, 4)
            stage_k(KVH - 1)
            pool.wait_ge(kv_out, 2)
            stage_v(KVH - 1)
            pool.wait_ge(z_out, 4)
            pool.wait_ge(v_staged, 4)
            for e in range(2):
                for a in range(2):
                    for r in range(2):
                        q = zT[HEAD * e:HEAD * e + HEAD, 4 * r + 2 * a:4 * r + 2 * a + 2, NP:N].rearrange("p i b -> p b i")
                        nc.gpsimd.tensor_scalar(qd[HEAD * a:HEAD * a + HEAD, r, :, 4 * a + e:4 * a + 4:2], q,
                                                HEAD ** -0.5, None, ALU.mult).then_inc(qd_staged, 1)
                        pool.wait_ge(qd_staged, 4 * e + 2 * a + r + 1)
            pool.wait_ge(state_out, 1)
            with pool.Fori(0, CONV_TURNS - 1) as turn:
                own.begin(turn, 2 * CONV_LINKS)
                conv_tile(turn * 2, 0)
                pool.wait_ge(scores_done, 4 * turn + 4)
                stage_k(turn * -1 + (KVH - 2))
                conv_tile(turn * 2 + 1, 1)
                pool.wait_ge(pv_done, 2 * turn + 2)
                stage_v(turn * -1 + (KVH - 2))
                own.end(CONV_TURNS - 1)
            conv_tile(CT - 2, 0)
            conv_tile(CT - 1, 1)

            def square_sums(k, total, scratch):
                base = 5 * (k - 1)
                pool.wait_ge(sq_ready, base + 2)
                nc.gpsimd.tensor_tensor(total[:], total[:], scratch[:], ALU.add).then_inc(pool_sums, 1)
                pool.wait_ge(pool_sums, 2 * k - 1)
                pool.wait_ge(sq_ready, base + 3)
                nc.gpsimd.tensor_tensor(total[:], total[:], scratch[:], ALU.add).then_inc(pool_sums, 1)
                pool.wait_ge(pool_sums, 2 * k)
                own.link(nc.gpsimd.tensor_tensor(total[:, 0:2, :], total[:, 0:2, :], total[:, 2:4, :], ALU.add))
                nc.gpsimd.tensor_tensor(total[:, 0, :], total[:, 0, :], total[:, 1, :], ALU.add).then_inc(acc_ready, 1)

            square_sums(1, acc4, sq)
            for i, k in enumerate(K_ORDER):
                pool.wait_ge(scaled, i + 1)
                nc.gpsimd.tensor_tensor(resid[:, k, WANTED], tmp[:, i % 2, :], resid[:, k, WANTED], ALU.add).then_inc(resid_ready, 1)
                if i:
                    pool.wait_ge(rsq_ready, i)
                    if i == 1:
                        nc.gpsimd.tensor_copy(acc4[:, 0, :], sq[:, 0, :]).then_inc(rsum, 1)
                    else:
                        pool.wait_ge(rsum, i - 1)
                        nc.gpsimd.tensor_tensor(acc4[:, 0, :], acc4[:, 0, :], sq[:, (i - 1) % 2, :], ALU.add).then_inc(rsum, 1)
            pool.wait_ge(rsq_ready, KT)
            pool.wait_ge(rsum, KT - 1)
            nc.gpsimd.tensor_tensor(acc4[:, 0, :], acc4[:, 0, :], sq[:, (KT - 1) % 2, :], ALU.add).then_inc(rsum, 1)
            pool.wait_ge(rsum, KT)
            nc.gpsimd.partition_all_reduce(acc4[:, 1, :], acc4[:, 0, :], P, RADD).then_inc(tot_ready, 1)
            with pool.Fori(0, FF_TURNS) as turn:
                pool.wait_ge(sig_ready, turn + 1)
                nc.gpsimd.tensor_tensor(gate[:], gate[:], up[:], ALU.mult).then_inc(swish_ready, 1)
                pool.wait_ge(swish_ready, turn + 1)
                pool.wait_ge(up_ready, turn + 1)
                nc.gpsimd.tensor_tensor(up[:], up[:], gate[:], ALU.mult).then_inc(hid_ready, 1)
                pool.wait_ge(hid_ready, turn + 1)
                pool.wait_ge(hid_hi, turn + 1)
                nc.gpsimd.tensor_tensor(h_lo[:, bass.ds(turn * NB, NB), :], up[:],
                                        h_hi[:, bass.ds(turn * NB, NB), :].bitcast(F32), ALU.subtract).then_inc(hid_lo, 1)
            square_sums(2, y_acc, y_sq)
            for k in range(0, KT, NB):
                pool.wait_ge(y_scaled, k + 1)
                nc.gpsimd.tensor_tensor(yT[:, k, :], yT[:, k, :], resid[:, k, WANTED], ALU.add).then_inc(y_ready_pool, 1)

        @block.scalar
        def _(act):
            act.dma_start(ident[:], squares[0]).then_inc(const_in, 16)
            act.dma_start(flip[:], squares[1]).then_inc(const_in, 16)
            act.dma_start(masks[:], row_masks).then_inc(const_in, 16)
            for i, gain in enumerate((norm_pre_mix, norm_post_mix, norm_pre_ffn, norm_post_ffn)):
                act.dma_start(vec_rows[KT * i:KT * i + KT, :], gain[0].rearrange("(t p) -> t p", p=P)).then_inc(vec_in, 16)
            act.dma_start(vec_rows[V_CONV:NVEC, :], conv_w[0].rearrange("i (j p) -> (i j) p", p=P)).then_inc(vec_in, 16)
            act.dma_start(onehot_s[:], onehot).then_inc(table_in, 16)
            act.dma_start(table[0:BUCKETS, :], rel_bias).then_inc(table_in, 16)
            act.dma_start(sink[:], attn_sinks[0:1, :].broadcast_to([P, HEADS])).then_inc(sink_in, 16)
            act.dma_start(kc[:], cache_k[0].rearrange("b t h d -> t b (h d)")).then_inc(kcache_in, 16)
            act.dma_start(state_rows[:], state_conv[0].rearrange("b t c -> (b t) c")).then_inc(state_in, 16)
            act.dma_start(vc[:], cache_v[0].rearrange("b t h d -> t b (h d)")).then_inc(vcache_in, 16)

            def split(n, slot, size, loads, turn=0, turn_loads=0):
                act.wait_ge(raw_landed[slot], 16 * loads + turn_loads)
                act.wait_ge(chunk_used, n + 1 + turn)
                nc.scalar.activation(w_hi[:, slot, 0:size].rearrange("p (j n) -> p j n", j=2),
                                     raw[:, slot, :, 0:size // 2], ACT.Copy).then_inc(hi_ready, 1)

            def loads_to(n):
                a, b = C_CONV // RING, C_OUT // RING
                done = n // RING + 1
                return done + min(max(done - a, 0), b - a)

            act.wait_ge(x_in, 80)
            act.wait_ge(filled, 4)
            for b, (_, size) in enumerate(BLOCKS):
                if b:
                    act.wait_ge(x_squared, b)
                nc.scalar.activation(w_hi[0:size, 0:2, :].rearrange("p a n -> p (a n)"), rows_in[0:size, b, :],
                                     ACT.Square, accum_out=stat3[0:size, b:b + 1]).then_inc(x_squared, 1)
            act.wait_ge(vec_out, 1)
            for i, k in enumerate(K_ORDER):
                act.wait_ge(xt_out, i + 1)
                nc.scalar.activation(op_hi[:, k, :], resid[:, k, :], ACT.Copy,
                                     scale=vec[:, V_PRE_MIX + k:V_PRE_MIX + k + 1]).then_inc(op_hi_ready, 1)
            act.wait_ge(x_squared, 3)
            for n in range(RING):
                split(n, n, 768, loads_to(n))

            def stage_q(g):
                for e in range(2):
                    part = slice(HEAD * e, HEAD * e + HEAD)
                    nc.scalar.activation(qs[part, e:GROUP:2, :], zT[part, bass.ds(g * 2, 2), T0:NP], ACT.Copy).then_inc(q_staged, 1)

            for c in range(QKV_TURNS * 2 * NC):
                split(c + RING, c % RING, 768, loads_to(c + RING))
                if 12 <= c < 16:
                    i = c - 12
                    act.wait_ge(kct_done, i + 1)
                    nc.scalar.activation(kct[:, 2 * i:2 * i + 2, :, :].rearrange("p b r k -> p (b r k)"),
                                         ps[:, 6 + i % 2, :], ACT.Copy).then_inc(kct_out, 1)
                if c == 18:
                    act.wait_ge(z_out, 2)
                    for a in range(2):
                        for half in range(2):
                            nc.scalar.activation(kd[HEAD * half:HEAD * half + HEAD, a:KVH:2, :],
                                                 zT[HEAD * a:HEAD * a + HEAD, 8:10, 0:NP], ACT.Copy,
                                                 scale=HEAD ** -0.5).then_inc(kd_ready, 1)
                if c == 24:
                    act.wait_ge(zeroed, 1)
                    stage_q(KVH - 1)

            def conv_turn(turn, g, last_turn):
                for c in range(2 * NC):
                    into_next = (c + RING) // (2 * NC)
                    if last_turn and into_next:
                        split(C_CONV + c + RING, c % RING, 1024, loads_to(C_CONV + 2 * NC * CONV_TURNS + c + RING - 2 * NC), turn * (2 * NC))
                    else:
                        loads = C_CONV // RING + 2 * ((c + RING) // RING + 1)
                        split(C_CONV + c + RING, c % RING, 768, loads, turn * (2 * NC), turn * (16 * 2 * 2 * NC // RING))
                    if c in (1, 3):
                        scores, col = (s_a, 0) if c == 1 else (s_b, 4)
                        act.wait_ge(nmax_ready, 2 * turn + 1 + c // 2)
                        for h in range(GROUP):
                            nc.scalar.activation(scores[:, h], scores[:, h], ACT.Exp, bias=nmax[:, col + h:col + h + 1],
                                                 accum_out=den[:, col + h:col + h + 1])
                        nc.scalar.activation(esk[:, col:col + 4], esk[:, col:col + 4], ACT.Exp).then_inc(exp_done, 1)
                    if c in (5, 7):
                        act.wait_ge(probs_t, 4 * turn + (1 if c == 5 else 3))
                        nc.scalar.activation(pt[:, 0 if c == 5 else 1, :], ps[:, 6, :], ACT.Copy).then_inc(probs_t_act, 1)
                    if last_turn and c == 10:
                        act.wait_ge(dec_nmax, 1)
                        nc.scalar.activation(sd[:], sd[:], ACT.Exp, bias=dstat[:, 0:1], accum_out=dstat[:, 2:3])
                        nc.scalar.activation(dstat[:, 3:4], dstat[:, 1:2], ACT.Exp, bias=dstat[:, 0:1]).then_inc(dec_exp, 1)
                    if c in (10, 11):
                        block_i = c - 10
                        act.wait_ge(pv_done, 2 * turn + 1 + block_i)
                        src = ps[:, 7 - block_i, :].rearrange("p (i e q) -> p i e q", e=2, q=P)
                        for e in range(2):
                            part = slice(HEAD * e, HEAD * e + HEAD)
                            nc.scalar.activation(zT[part, bass.ds(g * 2, 2), T0 + block_i * P:T0 + block_i * P + P],
                                                 src[part, :, e, :], ACT.Copy).then_inc(pv_act, 1)
                    if c == 13 and not last_turn:
                        stage_q(g - 1)
                    if last_turn and c == 12:
                        act.wait_ge(conv_done, CT - 2)
                        act.wait_ge(chunk_used, RING + C_OUT - NC + 3)
                        nc.scalar.activation(op_hi[:, 8:14, WANTED], convT[:, 0:6, :], ACT.Copy).then_inc(op_hi_ready, 1)

            with act.Fori(0, CONV_TURNS - 1) as turn:
                conv_turn(turn, turn * -1 + (KVH - 1), False)
            conv_turn(CONV_TURNS - 1, 0, True)
            act.wait_ge(dec_pv_out, 4)
            act.wait_ge(pv_act, 4 * CONV_TURNS)
            act.wait_ge(chunk_used, RING + C_OUT - 1)
            nc.scalar.activation(op_hi[:, 0:8, WANTED], zT[:, 0:8, WANTED], ACT.Copy).then_inc(op_hi_ready, 1)
            act.wait_ge(conv_done, CT)
            act.wait_ge(chunk_used, RING + C_OUT)
            nc.scalar.activation(op_hi[:, 14:16, WANTED], convT[:, 6:8, :], ACT.Copy).then_inc(op_hi_ready, 1)

            def group_out(k, group, bank, dst, gain, total, scratch, out_ready):
                base = 5 * (k - 1)
                if group == 2:
                    act.wait_ge(pool_sums, 2 * k - 1)
                if group == 3:
                    act.wait_ge(acc_ready, k)
                if group < 3:
                    square = total if group == 0 else scratch
                    nc.scalar.activation(square[:], ps[:, bank:bank + NB, 0:M], ACT.Square).then_inc(sq_ready, 1)
                else:
                    for m in (0, 2):
                        nc.scalar.activation(scratch[:, m:m + 2, :], ps[:, bank + m:bank + m + 2, 0:M], ACT.Square).then_inc(sq_ready, 1)
                for m in range(NB):
                    t = NB * group + m
                    mm = nc.scalar.activation(dst[:, t, :], ps[:, bank + m, 0:M], ACT.Copy,
                                              scale=vec[:, gain + t:gain + t + 1])
                mm.then_inc(out_ready, 1)

            for c in range(4 * NC):
                split(C_OUT + c + RING, c % RING, 1024, loads_to(C_OUT + c + RING))
                if c % NC == NC - 1:
                    group = c // NC
                    act.wait_ge(chunk_used, RING + C_OUT + c + 1)
                    group_out(1, group, NB * (group % 2), mixT, V_POST_MIX, acc4, sq, mix_out)

            def inverse_rms(k, total, dst):
                nc.scalar.activation(dst, total, ACT.Sqrt, bias=eps[:], scale=1.0 / D).then_inc(root_ready, 1)

            act.wait_ge(sums_done, 1)
            inverse_rms(1, ps[:, 2, 0:M], root[:])

            def input_step(i):
                k = K_ORDER[i]
                act.wait_ge(resid_ready, i + 1)
                nc.scalar.activation(op_hi[:, k, WANTED], resid[:, k, WANTED], ACT.Copy,
                                     scale=vec[:, V_PRE_FFN + k:V_PRE_FFN + k + 1]).then_inc(op_hi_ready, 1)
                if i >= 2:
                    act.wait_ge(rsum, i - 1)
                nc.scalar.activation(sq[:, i % 2, :], resid[:, k, WANTED], ACT.Square).then_inc(rsq_ready, 1)

            def ffn_turn(turn, first):
                for c in range(2 * NC):
                    if first:
                        for i in range(LEAD + 2 * c, min(LEAD + 2 * c + 2, KT)):
                            input_step(i)
                    split(C_FF + c + RING, c % RING, 1024, loads_to(C_FF + c + RING), turn * (2 * NC),
                          turn * (16 * 2 * NC // RING))
                    if first and c == LEAD - 2:
                        act.wait_ge(tot_ready, 1)
                        inverse_rms(2, acc4[:, 1, :], acc4[:, 2, :])
                    if c == NC:
                        act.wait_ge(gate_ready, turn + 1)
                        nc.scalar.activation(up[:], gate[:], ACT.Sigmoid).then_inc(sig_ready, 1)
                    if c == 2 * NC - 1:
                        act.wait_ge(hid_ready, turn + 1)
                        nc.scalar.activation(h_hi[:, bass.ds(turn * NB, NB), :], up[:], ACT.Copy).then_inc(hid_hi, 1)

            for i in range(LEAD):
                input_step(i)
            act.wait_ge(crow_done, 1)
            nc.scalar.activation(conv_rows[:], ps[0:2 + ND, 0:2, :].rearrange("p a n -> p (a n)"), ACT.Copy).then_inc(crow_out, 1)
            ffn_turn(0, True)
            with act.Fori(1, FF_TURNS) as turn:
                ffn_turn(turn, False)

            def down_slots(first, count):
                for c in range(first, first + count):
                    split(C_DOWN + c + RING, c % RING, 1024, loads_to(C_DOWN + c + RING))

            def down_turns(first, turns):
                with act.Fori(0, turns) as turn:
                    for c in range(first, first + RING):
                        split(C_DOWN + c + RING, c % RING, 1024, loads_to(C_DOWN + c + RING), turn * RING, turn * 16)

            def down_out(group):
                act.wait_ge(chunk_used, RING + C_DOWN + DC * group + DC)
                group_out(2, group, NB * (group % 2), yT, V_POST_FFN, y_acc, y_sq, y_out)

            whole = DC // RING
            for half in range(2):
                start = 2 * DC * half
                down_turns(start, whole)
                down_slots(start + whole * RING, DC % RING)
                down_out(2 * half)
                down_slots(start + DC, RING - DC % RING)
                down_turns(start + DC + RING - DC % RING, whole - half)
                down_out(2 * half + 1)
            act.wait_ge(sums_done, 2)
            inverse_rms(3, ps[:, 0, 0:M], y_root[:])
            for i in range(0, 12, 2):
                b, q = i % 3, i // 3
                size = OUT_BLOCKS[b][1]
                act.wait_ge(yt_done, i + 1)
                nc.scalar.activation(rows_out[0:size, b, 512 * q:512 * q + 512], ps[0:size, i % 6, :], ACT.Copy).then_inc(yt_act, 1)

        @block.vector
        def _(dve):
            own = Own(dve, dve_own)

            def split(n, slot, size, turn=0):
                dve.wait_ge(hi_ready, n + 1 + turn)
                hi = w_hi[:, slot, 0:size].rearrange("p (j n) -> p j n", j=2)
                lo = w_lo[:, slot, 0:size].rearrange("p (j n) -> p j n", j=2)
                nc.vector.tensor_tensor(lo, raw[:, slot, :, 0:size // 2], hi.bitcast(F32), ALU.subtract).then_inc(lo_ready, 1)

            def low_half(i, k, gain, base, cols):
                dve.wait_ge(op_hi_ready, base + i + 1)
                nc.vector.scalar_tensor_tensor(out=op_lo[:, k, cols], in0=resid[:, k, cols], scalar=vec[:, gain + k:gain + k + 1],
                                               in1=op_hi[:, k, cols].bitcast(F32), op0=ALU.mult, op1=ALU.subtract).then_inc(op_lo_ready, 1)

            def diagonals(scratch):
                dve.wait_ge(inv_ready, 1)
                nc.vector.tensor_tensor(scratch[:], each(ident[:], [P, 3, P]),
                                        stat3[:, 3:6].unsqueeze(2).broadcast_to([P, 3, P]), ALU.mult).then_inc(diag_ready, 1)

            dve.wait_ge(vec_done, 1)
            nc.vector.tensor_copy(vec[:], ps[:, 7, 0:NVEC]).then_inc(vec_out, 1)
            dve.wait_ge(rel_done, 1)
            nc.vector.tensor_copy(bias_sb[:], ps[0:HEADS, 6, 0:BIAS_N]).then_inc(rel_out, 1)
            dve.wait_ge(filled, 4)
            dve.wait_ge(table_in, 32)
            nc.vector.tensor_copy(table_d[:], each(table[:], [BUCKETS + 1, ND, HEADS])).then_inc(table_d_ready, 1)
            for i, k in enumerate(K_ORDER):
                dve.wait_ge(xt_done, i + 1)
                nc.vector.tensor_copy(resid[:, k, :], ps[:, i % 6, 0:N]).then_inc(xt_out, 1)
                if i == 2:
                    dve.wait_ge(x_squared, 3)
                    nc.vector.tensor_scalar(stat3[:, 0:3], stat3[:, 0:3], 1.0 / D, EPS, ALU.mult, ALU.add).then_inc(rms_ready, 1)
                if i:
                    dve.wait_ge(xt_out, i)
                    low_half(i - 1, K_ORDER[i - 1], V_PRE_MIX, 0, ALL)
            dve.wait_ge(xt_out, KT)
            low_half(KT - 1, K_ORDER[-1], V_PRE_MIX, 0, ALL)
            for n in range(RING):
                split(n, n, 768)
            dve.wait_ge(const_in, 48)
            diagonals(x_diag)
            dve.wait_ge(sink_in, 16)
            own.link(nc.vector.tensor_scalar(nsink[:], sink[:], -1.0, None, ALU.mult))

            for c in range(QKV_TURNS * 2 * NC):
                split(c + RING, c % RING, 768)
                if c == 2:
                    dve.wait_ge(bcast_done, 1)
                    nc.vector.tensor_copy(rstd[:], ps[:, 6, 0:N]).then_inc(rstd_ready, 1)
                    dve.wait_ge(rstd_ready, 1)
                if c % NC == NC - 1:
                    group = c // NC
                    dve.wait_ge(chunk_used, RING + c + 1)
                    bank = NA * (group % 2)
                    wanted = ALL if group < 2 else WANTED
                    size = wanted.stop - wanted.start
                    nc.vector.tensor_tensor(zT[:, 9 - 3 * group:12 - 3 * group, wanted], ps[:, bank:bank + NA, wanted],
                                            each(rstd[:, wanted], [P, NA, size]), ALU.mult).then_inc(z_out, 1)
                if 4 <= c < 4 + HEADS // 2:
                    i = c - 4
                    dve.wait_ge(bias_done, i + 1)
                    nc.vector.tensor_copy(bias[:, 2 * i:2 * i + 2, :].rearrange("p a n -> p (a n)"),
                                          ps[:, 6 + i % 2, :]).then_inc(bias_out, 1)
                if c == 14:
                    own.link(nc.vector.tensor_tensor(sinks_m[:], sink[:], masks[:, ND:ND + HEADS], ALU.mult))
                    own.link(nc.vector.tensor_reduce(dstat[:, 1:2], sinks_m[:], AX.X, ALU.add))
                    own.link(nc.vector.tensor_scalar(dstat[:, 6:7], dstat[:, 1:2], -1.0, None, ALU.mult))
                if c == 17:
                    dve.wait_ge(kv_done, 1)
                    nc.vector.tensor_copy(vd[:, 0:2, :].rearrange("p a n -> p (a n)"), ps[:, 6, :]).then_inc(kv_out, 1)
                if c == 18:
                    dve.wait_ge(kv_done, 2)
                    nc.vector.tensor_copy(vd[0:N_META, 2, :], ps[0:N_META, 7, 0:2 * P]).then_inc(kv_out, 1)
                if c == 19:
                    dve.wait_ge(kv_done, 3)
                    nc.vector.tensor_copy(kv_rows[:], ps[:, 6, :]).then_inc(kv_out, 1)
                if c == 20:
                    dve.wait_ge(kv_done, 4)
                    nc.vector.tensor_copy(kv_dec[:], ps[0:ND, 7, :]).then_inc(kv_out, 1)
                if c == 22:
                    dve.wait_ge(state_done, 1)
                    nc.vector.tensor_copy(state_t[:].rearrange("p j r -> p (j r)"), ps[:, 6, 0:P]).then_inc(state_out, 1)

            def minus_max(scores, cols, heads):
                own.link(nc.vector.tensor_reduce(nmax[:, cols], scores, AX.X, ALU.max))
                own.link(nc.vector.scalar_tensor_tensor(out=nmax[:, cols], in0=nmax[:, cols], scalar=-1.0, in1=nsink[:, heads],
                                                        op0=ALU.mult, op1=ALU.min))
                nc.vector.tensor_tensor(esk[:, cols], nmax[:, cols], sink[:, heads], ALU.add).then_inc(nmax_ready, 1)

            def normalise(probs, cols):
                own.link(nc.vector.tensor_tensor(den[:, cols], den[:, cols], esk[:, cols], ALU.add))
                own.link(nc.vector.reciprocal(den[:, cols], den[:, cols]))
                nc.vector.tensor_tensor(probs, probs, den[:, cols].unsqueeze(2).broadcast_to(list(probs.shape)),
                                        ALU.mult).then_inc(probs_ready, 1)

            TURN_LINKS = 8

            def conv_turn(turn, g, last_turn):
                heads = bass.ds(g * GROUP, GROUP)
                for c in range(2 * NC):
                    size = 1024 if last_turn and c + RING >= 2 * NC else 768
                    split(C_CONV + c + RING, c % RING, size, turn * (2 * NC))
                    if c % NC == NC - 1:
                        half = c // NC
                        dve.wait_ge(chunk_used, RING + C_CONV + c + 1 + turn * (2 * NC))
                        nc.vector.tensor_tensor(zb[:, half], ps[:, NA * half:NA * half + NA, 0:NU],
                                                each(rstd[:, U0:N], [P, NA, NU]), ALU.mult).then_inc(zb_ready, 1)
                    if c == 0:
                        dve.wait_ge(scores_done, 4 * turn + 1)
                        nc.vector.tensor_tensor(s_a[:, :, T0:KEYS_A], heads4(ps[:, 6, :]), bias[:, heads, P:2 * P], ALU.add).then_inc(scores_out, 1)
                        dve.wait_ge(scores_done, 4 * turn + 2)
                        nc.vector.tensor_tensor(s_a[:, :, 0:N_META], heads4(ps[:, 7, 0:GROUP * N_META]),
                                                bias[:, heads, P - N_META:P], ALU.add).then_inc(scores_out, 1)
                        dve.wait_ge(scores_out, 4 * turn + 2)
                        minus_max(s_a[:], slice(0, 4), heads)
                    if c in (1, 2):
                        h = 2 * (c - 1)
                        dve.wait_ge(scores_done, 4 * turn + 2 + c)
                        nc.vector.tensor_tensor(s_b[:, h:h + 2], ps[:, 5 + c, :].rearrange("p (h k) -> p h k", h=2),
                                                bias[:, bass.ds(g * GROUP + h, 2), :], ALU.add).then_inc(scores_out, 1)
                    if c == 2:
                        dve.wait_ge(scores_out, 4 * turn + 4)
                        minus_max(s_b[:], slice(4, 8), heads)
                    if c == 3:
                        dve.wait_ge(exp_done, 2 * turn + 1)
                        normalise(s_a[:], slice(0, 4))
                    if last_turn and c == 4:
                        dve.wait_ge(dec_scores, 1)
                        nc.vector.tensor_copy(sdt[:], ps[:, 6, 0:P]).then_inc(dec_scores_out, 1)
                        nc.vector.tensor_copy(sd_own[:], ps[0:ND, 7, 0:P]).then_inc(dec_scores_out, 1)
                    if c == 5:
                        dve.wait_ge(exp_done, 2 * turn + 2)
                        normalise(s_b[:], slice(4, 8))
                    if c == 6:
                        dve.wait_ge(probs_t, 4 * turn + 2)
                        nc.vector.tensor_copy(pt_m[:], ps[0:N_META, 7, :]).then_inc(probs_t_dve, 1)
                    if c == 8:
                        dve.wait_ge(probs_t, 4 * turn + 4)
                        nc.vector.tensor_copy(pt[:, 2, :], ps[:, 7, :]).then_inc(probs_t_dve, 1)
                    if last_turn and c == 9:
                        dve.wait_ge(dec_rows, 1)
                        nc.vector.tensor_copy(sd[:], ps[:, 6, 0:P + 1]).then_inc(dec_rows_out, 1)
                        own.link(nc.vector.tensor_tensor(sd_own8[:], ps[:, 6, 256:256 + ND], masks[:, 0:ND], ALU.mult))
                        own.link(nc.vector.tensor_reduce(dstat[:, 5:6], sd_own8[:], AX.X, ALU.add))
                        nc.vector.tensor_tensor(sd[:, P:P + 1], sd[:, P:P + 1], dstat[:, 5:6], ALU.add).then_inc(dec_rows_out, 1)
                        dve.wait_ge(dec_rows_out, 2)
                        own.link(nc.vector.tensor_reduce(dstat[:, 0:1], sd[:], AX.X, ALU.max))
                        nc.vector.scalar_tensor_tensor(out=dstat[:, 0:1], in0=dstat[:, 0:1], scalar=-1.0, in1=dstat[:, 6:7],
                                                       op0=ALU.mult, op1=ALU.min).then_inc(dec_nmax, 1)
                    if last_turn and c == 11:
                        dve.wait_ge(dec_exp, 1)
                        own.link(nc.vector.tensor_tensor(dstat[:, 4:5], dstat[:, 2:3], dstat[:, 3:4], ALU.add))
                        own.link(nc.vector.reciprocal(dstat[:, 4:5], dstat[:, 4:5]))
                        nc.vector.tensor_scalar(sd[:], sd[:], dstat[:, 4:5], None, ALU.mult).then_inc(dec_probs, 1)
                        dve.wait_ge(dec_probs, 1)
                        nc.vector.tensor_scalar(sd_own8[:], masks[:, 0:ND], sd[:, P:P + 1], None, ALU.mult).then_inc(dec_probs, 1)
                    if last_turn and c == 13:
                        dve.wait_ge(op_hi_ready, KT + 1)
                        nc.vector.tensor_tensor(op_lo[:, 8:14, WANTED], convT[:, 0:6, :], op_hi[:, 8:14, WANTED].bitcast(F32),
                                                ALU.subtract).then_inc(op_lo_ready, 1)
                        dve.wait_ge(dec_pt, 1)
                        nc.vector.tensor_copy(pd[:], ps[:, 6, 0:P]).then_inc(dec_pt_out, 1)
                        nc.vector.tensor_copy(pd_own[:], ps[0:ND, 6, P:2 * P]).then_inc(dec_pt_out, 1)

            with dve.Fori(0, CONV_TURNS - 1) as turn:
                own.begin(turn, TURN_LINKS)
                conv_turn(turn, turn * -1 + (KVH - 1), False)
                own.end(CONV_TURNS - 1)
            conv_turn(CONV_TURNS - 1, 0, True)
            dve.wait_ge(dec_pv, 1)
            for a in range(2):
                for e in range(2):
                    src = ps[HEAD * a:HEAD * a + HEAD, 7, 0:P].rearrange("p (r b h) -> p r h b", r=2, h=8)[:, :, 4 * a + e:4 * a + 4:2, :]
                    dst = zT[HEAD * e:HEAD * e + HEAD, 0:8, NP:N].rearrange("p (r a i) b -> p r a i b", r=2, a=2)[:, :, a]
                    nc.vector.tensor_copy(dst, src).then_inc(dec_pv_out, 1)
            dve.wait_ge(op_hi_ready, KT + 2)
            nc.vector.tensor_tensor(op_lo[:, 0:8, WANTED], zT[:, 0:8, WANTED], op_hi[:, 0:8, WANTED].bitcast(F32), ALU.subtract).then_inc(op_lo_ready, 1)
            dve.wait_ge(op_hi_ready, KT + 3)
            nc.vector.tensor_tensor(op_lo[:, 14:16, WANTED], convT[:, 6:8, :], op_hi[:, 14:16, WANTED].bitcast(F32), ALU.subtract).then_inc(op_lo_ready, 1)

            with dve.Fori(0, 2) as turn:
                for c in range(2 * NC):
                    split(C_OUT + c + RING, c % RING, 1024, turn * (2 * NC))

            def invert(k, src, dst):
                dve.wait_ge(root_ready, k)
                nc.vector.reciprocal(dst, src).then_inc(rms_inverse, 1)
                dve.wait_ge(rms_inverse, k)

            invert(1, root[:], inv[:])
            dve.wait_ge(mix_out, 4)

            def input_step(i):
                if i < KT:
                    k = K_ORDER[i]
                    if i >= 2:
                        dve.wait_ge(resid_ready, i - 1)
                    nc.vector.tensor_tensor(tmp[:, i % 2, :], mixT[:, k, :], inv[:], ALU.mult).then_inc(scaled, 1)
                if i:
                    low_half(i - 1, K_ORDER[i - 1], V_PRE_FFN, KT + 3, WANTED)

            def scale_out(dst, bank, ready, c, turn):
                dve.wait_ge(chunk_used, RING + C_FF + c + 1 + turn * (2 * NC))
                nc.vector.tensor_tensor(dst[:], ps[:, bank:bank + NB, 0:M], each(rstd[:, 0:M], [P, NB, M]), ALU.mult).then_inc(ready, 1)

            def ffn_turn(turn, first):
                for c in range(2 * NC):
                    if first:
                        for i in range(LEAD + 2 * c, min(LEAD + 2 * c + 2, KT + 1)):
                            input_step(i)
                    split(C_FF + c + RING, c % RING, 1024, turn * (2 * NC))
                    if c == NC - 1:
                        if first:
                            invert(2, acc4[:, 2, :], rstd[:, 0:M])
                        else:
                            dve.wait_ge(hid_lo, turn)
                        scale_out(gate, 0, gate_ready, c, turn)
                    if c == 2 * NC - 1:
                        dve.wait_ge(swish_ready, turn + 1)
                        scale_out(up, NB, up_ready, c, turn)

            for i in range(LEAD):
                input_step(i)
            ffn_turn(0, True)
            with dve.Fori(1, FF_TURNS) as turn:
                ffn_turn(turn, False)

            with dve.Fori(0, (4 * DC - RING) // RING) as turn:
                for c in range(RING):
                    split(C_DOWN + c + RING, c, 1024, turn * RING)
            invert(3, y_root[:], rstd[:, 0:M])
            dve.wait_ge(y_out, 4)

            def add_residual(k):
                dve.wait_ge(y_scaled, k + 1)
                nc.vector.tensor_tensor(yT[:, k, :], yT[:, k, :], resid[:, k, WANTED], ALU.add).then_inc(y_ready_dve, 1)

            def rows(q):
                for i in range(3 * q, 3 * q + 3):
                    if i % 2:
                        b = i % 3
                        size = OUT_BLOCKS[b][1]
                        dve.wait_ge(yt_done, i + 1)
                        nc.vector.tensor_copy(rows_out[0:size, b, 512 * q:512 * q + 512], ps[0:size, i % 6, :]).then_inc(yt_dve, 1)

            for q in range(4):
                for k in range(NB * q, NB * q + NB):
                    nc.vector.tensor_tensor(yT[:, k, :], yT[:, k, :], rstd[:, 0:M], ALU.mult).then_inc(y_scaled, 1)
                    if k % NB >= 2:
                        add_residual(k - 1)
                add_residual(NB * q + NB - 1)
                if q:
                    rows(q - 1)
            rows(3)


def shape_constants():
    import math
    import numpy as np
    squares = np.stack([np.eye(P), np.eye(P)[::-1]]).astype(np.float32)
    d = 255 - np.arange(BIAS_N)
    exact = BUCKETS // 2
    ratio = np.maximum(d, 1).astype(np.float32) / np.float32(exact)
    far = exact + (np.log(ratio) / np.float32(math.log(WINDOW / exact)) * np.float32(BUCKETS - exact)).astype(np.int32)
    bucket = np.where(d < exact, d, np.minimum(far, BUCKETS - 1))
    onehot = np.zeros((BUCKETS + 1, BIAS_N), np.float32)
    for n in range(BIAS_N):
        if 0 <= d[n] <= WINDOW:
            onehot[bucket[n], n] = 1.0
        else:
            onehot[BUCKETS, n] = MASKED
    row = np.arange(P)[:, None]
    row_masks = np.concatenate([row // HEADS == np.arange(ND), row % HEADS == np.arange(HEADS)],
                               axis=1).astype(np.float32)
    return dict(squares=squares, onehot=onehot, row_masks=row_masks)


def kernel(x_prompt, x_sample, cache_k, cache_v, state_conv, meta_tokens, rel_bias, w_in, conv_w,
           attn_sinks, w_out, norm_pre_mix, norm_post_mix, norm_pre_ffn, norm_post_ffn, w_gate,
           w_up, w_down):
    import numpy as np
    import concourse.bacc as _bacc
    from concourse.bass_utils import run_bass_kernel_spmd as _run

    inputs = dict(x_prompt=x_prompt, x_sample=x_sample, cache_k=cache_k, cache_v=cache_v,
                  state_conv=state_conv, meta_tokens=meta_tokens, rel_bias=rel_bias, w_in=w_in,
                  conv_w=conv_w, attn_sinks=attn_sinks, w_out=w_out, norm_pre_mix=norm_pre_mix,
                  norm_post_mix=norm_post_mix, norm_pre_ffn=norm_pre_ffn,
                  norm_post_ffn=norm_post_ffn, w_gate=w_gate, w_up=w_up, w_down=w_down)
    inputs.update(shape_constants())
    outputs = dict(y_prompt=(1, SEQ, D), y_sample=(ND, 1, D),
                   k_prompt=(1, 1, WINDOW, KVH, HEAD), v_prompt=(1, 1, WINDOW, KVH, HEAD),
                   conv_prompt=(1, 1, 2, CONV),
                   k_sample=(1, ND, WINDOW, KVH, HEAD), v_sample=(1, ND, WINDOW, KVH, HEAD),
                   conv_sample=(1, ND, 2, CONV))
    nc = _bacc.Bacc("TRN2", target_bir_lowering=False, num_devices=1, dynamic_dma_scratch_size=1024)
    arrays, args = {}, {}
    for name, value in inputs.items():
        arrays[f"in_{name}"] = np.ascontiguousarray(value)
        args[name] = nc.dram_tensor(f"in_{name}", arrays[f"in_{name}"].shape, F32, kind="ExternalInput").ap()
    for name, shape in outputs.items():
        args[name] = nc.dram_tensor(f"out_{name}", shape, F32, kind="ExternalOutput").ap()
    args["bias_rows"] = nc.dram_tensor("bias_rows", (HEADS, BIAS_N), F32, kind="Internal").ap()
    mixer_kernel(nc, **args)
    r = _run(nc, [arrays], core_ids=[0])
    return tuple(r.results[0][f"out_{name}"] for name in outputs)
```

```python
from contextlib import ExitStack

import concourse.bass as bass
from concourse import mybir

F32 = mybir.dt.float32
F32R = mybir.dt.float32r
ALU = mybir.AluOpType
ACT = mybir.ActivationFunctionType
AX = mybir.AxisListType
RADD = bass.bass_isa.ReduceOp.add

P = 128
D = 2048
SEQ = 256
N_META = 16
NP = SEQ + N_META
ND = 8
N = NP + ND
HEAD = 64
HEADS = 16
KVH = 4
GROUP = HEADS // KVH
WINDOW = 128
CONV = 1024
BUCKETS = 32
FF = 5632
IN = 4608
EPS = 1e-6
MASKED = -1e30

T0 = N_META
M = N - T0
U0 = T0 - 2
NU = N - U0
ALL, WANTED = slice(0, N), slice(T0, N)
KEYS_A = T0 + P

KT = D // P
FT = FF // P
CT = CONV // P
RING = 4
NA = 3
NB = 4
ORDER = [4, 5, 6, 0, 1, 2, 3, 7]
NC = len(ORDER)
DC = FT // 2
K_ORDER = [2 * c + j for c in ORDER for j in range(2)]
QKV_TURNS = 2
CONV_TURNS = 4
FF_TURNS = FT // NB
C_QKV = 0
C_CONV = C_QKV + QKV_TURNS * 2 * NC
C_OUT = C_CONV + CONV_TURNS * 2 * NC
C_FF = C_OUT + 4 * NC
C_DOWN = C_FF + FF_TURNS * 2 * NC
BLOCKS = [(0, 128), (128, 128), (256, N - 256)]
V_PRE_MIX, V_POST_MIX, V_PRE_FFN, V_POST_FFN, V_CONV = 0, KT, 2 * KT, 3 * KT, 4 * KT
NVEC = V_CONV + 3 * CT
EXT = SEQ + 2 + 3 * ND
LEAD = 4
X_BANKS = [3, 4, 5, 7]
BIAS_AT, KCT_AT = 10, 18
BIAS_N = 384


def mixer_kernel(nc, x_prompt, x_sample, cache_k, cache_v, state_conv, meta_tokens, rel_bias, w_in,
                 conv_w, attn_sinks, w_out, norm_pre_mix, norm_post_mix, norm_pre_ffn,
                 norm_post_ffn, w_gate, w_up, w_down, squares, onehot, row_masks,
                 y_prompt, y_sample, k_prompt, v_prompt, conv_prompt, k_sample, v_sample,
                 conv_sample, bias_rows):
    with ExitStack() as ctx:
        def sem(name):
            return ctx.enter_context(nc.semaphore(name))

        def place(name, shape, start, dt=F32):
            size = 4
            for s in shape[1:]:
                size *= s
            end = start + -(-size // 32) * 32
            assert end <= nc.sbuf_usable_end, (name, end)
            return nc.alloc_sbuf_tensor_at(name, shape, dt, offset=start), end

        e = -(-nc.sbuf_base // 32) * 32
        ident, e = place("ident", [P, P], e)
        ones, e = place("ones", [P, P], e)
        vec, e = place("vec", [P, NVEC], e)
        rstd, e = place("rstd", [P, N], e)
        eps, e = place("eps", [P, 1], e)
        stat_b, e = place("stat_b", [P, 4], e)
        stat3, e = place("stat3", [P, 8], e)
        resid, operand = place("resid", [P, KT, N], e)
        op_hi, e = place("op_hi", [P, KT, N], operand, F32R)
        op_lo, e = place("op_lo", [P, KT, N], e, F32R)
        raw, e = place("raw", [P, RING, 2, 512], e)
        w_hi, e = place("w_hi", [P, RING, 1024], e, F32R)
        w_lo, area = place("w_lo", [P, RING, 1024], e, F32R)
        h_hi, e = place("h_hi", [P, FT, M], area, F32R)
        h_lo, e = place("h_lo", [P, FT, M], e, F32R)
        gate, e = place("gate", [P, NB, M], e)
        up, keep = place("up", [P, NB, M], e)
        kv_rows, e = place("kv_rows", [P, 4 * P], keep)
        kv_dec, e = place("kv_dec", [ND, 4 * P], e)
        conv_rows, e = place("conv_rows", [2 + ND, CONV], e)
        yT, yT_end = place("yT", [P, KT, M], operand)
        y_sq, e = place("y_sq", [P, NB, M], yT_end)
        y_acc, e = place("y_acc", [P, NB, M], e)
        y_root, e = place("y_root", [P, M], e)
        rows_out, e = place("rows_out", [P, 2, D], area)
        dec_y, e = place("dec_y", [P, KT, ND], e)
        dec_rows_y, e = place("dec_rows_y", [P, P], e)
        zT, conv_area = place("zT", [P, 12, N], area)
        convT, zb_area = place("convT", [P, CT, M], conv_area)
        zb, e = place("zb", [P, 2, NA, NU], zb_area)
        after_zb = e
        bias, e = place("bias", [P, HEADS, 2 * P], e)
        u_ext, e = place("u_ext", [P, EXT], e)
        tap, e = place("tap", [P, EXT - 2], e)
        acc, e = place("acc", [P, EXT - 2], e)
        cw, e = place("cw", [P, 3], e)
        state_t, e = place("state_t", [P, CT, 2 * ND], e)
        u_out, e = place("u_out", [P, CT, 2 + ND], e)
        kd, e = place("kd", [P, KVH, NP], e)
        vd, e = place("vd", [P, 3, 2 * P], e)
        sink, e = place("sink", [P, HEADS], e)
        nsink, e = place("nsink", [P, HEADS], e)
        masks, e = place("masks", [P, ND + HEADS], e)
        vc, e = place("vc", [P, ND, 2 * P], e)
        kct, e = place("kct", [P, ND, 2, P], e)
        onehot_s, e = place("onehot_s", [BUCKETS + 1, BIAS_N], e)
        table, e = place("table", [BUCKETS + 1, HEADS], e)
        table_d, e = place("table_d", [BUCKETS + 1, ND, HEADS], e)
        flip, attn = place("flip", [P, P], e)
        rows_in, _ = place("rows_in", [P, 3, D], attn)
        hankel, e = place("hankel", [P, HEADS, 2 * P], attn)
        qs, e = place("qs", [P, GROUP, 2 * P], attn)
        ks, e = place("ks", [P, NP], e)
        vs, e = place("vs", [P, 3, 2, HEAD], e)
        s_a, e = place("s_a", [P, GROUP, KEYS_A], e)
        s_b, e = place("s_b", [P, GROUP, 2 * P], e)
        nmax, e = place("nmax", [P, 12], e)
        den, e = place("den", [P, 12], e)
        esk, e = place("esk", [P, 12], e)
        pt, e = place("pt", [P, 3, 512], e)
        pt_m, e = place("pt_m", [N_META, 512], e)
        qd, e = place("qd", [P, 2, ND, 2 * GROUP], e)
        sd, e = place("sd", [P, P + 1], e)
        sd_own8, e = place("sd_own8", [P, ND], e)
        sdt, e = place("sdt", [P, P], e)
        sd_own, e = place("sd_own", [ND, P], e)
        pd, e = place("pd", [P, P], e)
        pd_own, e = place("pd_own", [ND, P], e)
        dstat, e = place("dstat", [P, 8], e)
        sinks_m, e = place("sinks_m", [P, HEADS], e)
        assert e <= keep
        x_sq, _ = place("x_sq", [P, D // 2], area)
        kc, _ = place("kc", [P, ND, 2 * P], conv_area)
        vec_rows, e = place("vec_rows", [NVEC, P], zb_area)
        state_rows, e = place("state_rows", [2 * ND, CONV], e)
        bias_sb, e = place("bias_sb", [HEADS, BIAS_N], e)
        assert e <= after_zb
        mixT, e = place("mixT", [P, KT, M], after_zb)
        sq, e = place("sq", [P, NB, M], max(e, attn))
        acc4, e = place("acc4", [P, NB, M], e)
        root, e = place("root", [P, M], e)
        inv, e = place("inv", [P, M], e)
        tmp, e = place("tmp", [P, 2, 2, M], e)
        assert e <= keep
        x_diag, _ = place("x_diag", [P, 3, P], after_zb)

        ps = ctx.enter_context(nc.psum_tensor("ps", [P, 8, 512], F32))

        raw_landed = [sem(f"raw_landed{s}") for s in range(RING)]
        hi_ready = sem("hi_ready")
        lo_ready = sem("lo_ready")
        chunk_used = sem("chunk_used")
        x_in = [[sem(f"x_in{half}_{b}") for b in range(3)] for half in range(2)]
        ident_in, const_in, vec_in, table_in = sem("ident_in"), sem("const_in"), sem("vec_in"), sem("table_in")
        kcache_in, state_in, sink_in, vcache_in = sem("kcache_in"), sem("state_in"), sem("sink_in"), sem("vcache_in")
        filled = sem("filled")
        vec_done, vec_out, table_d_ready = sem("vec_done"), sem("vec_out"), sem("table_d_ready")
        rel_done, rel_out, rel_stored, hankel_in = sem("rel_done"), sem("rel_out"), sem("rel_stored"), [sem(f"hankel_in{part}") for part in range(4)]
        xt_done, xt_out, x_squared = sem("xt_done"), sem("xt_out"), sem("x_squared")
        op_hi_ready, op_lo_ready = sem("op_hi_ready"), sem("op_lo_ready")
        rms_ready, inv_ready, diag_ready, bcast_done = sem("rms_ready"), sem("inv_ready"), sem("diag_ready"), sem("bcast_done")
        rstd_ready = sem("rstd_ready")
        z_out = sem("z_out")
        bias_done, bias_out = sem("bias_done"), sem("bias_out")
        kct_done, kct_out = sem("kct_done"), sem("kct_out")
        kv_done, kv_out, kd_ready = sem("kv_done"), sem("kv_out"), sem("kd_ready")
        state_done, state_out = sem("state_done"), sem("state_out")
        zeroed, q_staged, k_staged, v_staged, qd_staged = (sem("zeroed"), sem("q_staged"), sem("k_staged"),
                                                           sem("v_staged"), sem("qd_staged"))
        scores_done, scores_out = sem("scores_done"), sem("scores_out")
        nmax_ready, exp_done, probs_ready = sem("nmax_ready"), sem("exp_done"), sem("probs_ready")
        probs_t = sem("probs_t")
        probs_t_act, probs_t_dve = sem("probs_t_act"), sem("probs_t_dve")
        pv_done, pv_act = sem("pv_done"), sem("pv_act")
        dec_scores, dec_scores_out, dec_rows, dec_rows_out = (sem("dec_scores"), sem("dec_scores_out"),
                                                              sem("dec_rows"), sem("dec_rows_out"))
        dec_nmax, dec_exp, dec_probs = sem("dec_nmax"), sem("dec_exp"), sem("dec_probs")
        dec_pt, dec_pt_out, dec_pv, dec_pv_out = sem("dec_pt"), sem("dec_pt_out"), sem("dec_pv"), sem("dec_pv_out")
        zb_ready, conv_done = sem("zb_ready"), sem("conv_done")
        mix_out, sq_ready, acc_ready, sums_done = sem("mix_out"), sem("sq_ready"), sem("acc_ready"), sem("sums_done")
        pool_sums = sem("pool_sums")
        scaled, resid_ready, rsq_ready, rsum = sem("scaled"), sem("resid_ready"), sem("rsq_ready"), sem("rsum")
        tot_ready, root_ready, rms_inverse = sem("tot_ready"), sem("root_ready"), sem("rms_inverse")
        crow_done, crow_out = sem("crow_done"), sem("crow_out")
        gate_ready, sig_ready, swish_ready = sem("gate_ready"), sem("sig_ready"), sem("swish_ready")
        up_ready, hid_ready, hid_hi, hid_lo = sem("up_ready"), sem("hid_ready"), sem("hid_hi"), sem("hid_lo")
        y_out, y_scaled, y_ready_pool, y_ready_dve = sem("y_out"), sem("y_scaled"), sem("y_ready_pool"), sem("y_ready_dve")
        dec_y_ready = sem("dec_y_ready")
        yt_done, yt_act, yt_dve = sem("yt_done"), sem("yt_act"), sem("yt_dve")
        stored = sem("stored")
        dve_own, pool_own = sem("dve_own"), sem("pool_own")

        class Own:

            def __init__(self, engine, semaphore):
                self.engine, self.semaphore, self.n, self.turn = engine, semaphore, 0, 0

            def link(self, instruction):
                instruction.then_inc(self.semaphore, 1)
                self.n += 1
                self.engine.wait_ge(self.semaphore, self.n + self.turn)

            def begin(self, turn, per_turn):
                self.turn, self.mark, self.per = turn * per_turn, self.n, per_turn

            def end(self, turns):
                assert self.n - self.mark == self.per, (self.n - self.mark, self.per)
                self.turn, self.n = 0, self.mark + turns * self.per

        def each(ap, shape):
            return ap.unsqueeze(1).broadcast_to(shape)

        def heads4(ap):
            return ap.rearrange("p (h k) -> p h k", h=GROUP)

        def at(ap, i):
            return ap[:, bass.ds(i, 1)].rearrange("p a n -> p (a n)")

        block = ctx.enter_context(nc.Block())

        @block.sync
        def _(sp):
            def load_x(half):
                cols = slice(half * D // 2, (half + 1) * D // 2)
                done = x_in[half]
                sp.dma_start(rows_in[N_META:P, 0, cols], x_prompt[0, 0:P - N_META, cols]).then_inc(done[0], 16)
                sp.dma_start(rows_in[0:N_META, 0, cols], meta_tokens[:, cols]).then_inc(done[0], 16)
                sp.dma_start(rows_in[:, 1, cols], x_prompt[0, P - N_META:2 * P - N_META, cols]).then_inc(done[1], 16)
                sp.dma_start(rows_in[0:N_META, 2, cols], x_prompt[0, SEQ - N_META:SEQ, cols]).then_inc(done[2], 16)
                sp.dma_start(rows_in[N_META:N_META + ND, 2, cols], x_sample[:, 0, cols]).then_inc(done[2], 16)

            load_x(1)

            def load(n, slot, src, dst, turn=0):
                sp.wait_ge(lo_ready, n + 1 + turn)
                sp.dma_start(dst, src).then_inc(raw_landed[slot], 16)

            def rows_of(w, chunk, col, width):
                return w[chunk * 2 * P:(chunk + 1) * 2 * P, bass.ds(col, width)].rearrange(
                    "(j p) n -> p j n", p=P)

            for c in range(QKV_TURNS * 2 * NC):
                if c == 2:
                    load_x(0)
                if c == 2 * RING:
                    sp.wait_ge(rel_out, 1)
                    sp.dma_start(bias_rows, bias_sb[:]).then_inc(rel_stored, 16)
                if c == RING + 2:
                    sp.dma_start(state_rows[:], state_conv[0].rearrange("b t c -> (b t) c")).then_inc(state_in, 16)
                if c == 10:
                    sp.wait_ge(rel_stored, 16)
                    sp.wait_ge(xt_done, KT)
                    sp.wait_ge(x_squared, 6)
                if c in (10, 12, 14, 16):
                    part = (c - 10) // 2
                    sp.dma_start(hankel[:, 4 * part:4 * part + 4, :],
                                 bass.AP(bias_rows.tensor, 4 * part * BIAS_N, [[1, P], [BIAS_N, 4], [1, 2 * P]])
                                 ).then_inc(hankel_in[part], 16)
                if c == 20:
                    sp.dma_start(kc[:], cache_k[0].rearrange("b t h d -> t b (h d)")).then_inc(kcache_in, 16)
                if c == 26:
                    sp.dma_start(vc[:], cache_v[0].rearrange("b t h d -> t b (h d)")).then_inc(vcache_in, 16)
                load(C_QKV + c, c % RING, rows_of(w_in[0], ORDER[c % NC], 1152 - 384 * (c // NC), 384),
                     raw[:, c % RING, :, 0:384])
            parts = w_in[0][:, IN - 3 * CONV:IN].rearrange("k (a n) -> k a n", a=3)
            with sp.Fori(0, CONV_TURNS) as turn:
                for c in range(2 * NC):
                    chunk = ORDER[c % NC]
                    sp.wait_ge(lo_ready, C_CONV + c + 1 + turn * (2 * NC))
                    for j in range(2):
                        k = 2 * chunk + j
                        sp.dma_start(raw[:, c % RING, j, 0:384].rearrange("p (a n) -> p a n", a=3),
                                     parts[k * P:k * P + P, :, bass.ds(turn * (2 * P) + c // NC * P, P)]
                                     ).then_inc(raw_landed[c % RING], 16)

            def column(turn, width, k):
                return (turn + turn) * (width // 2) if k == 0 else turn * width

            with sp.Fori(0, 2) as turn:
                for c in range(2 * NC):
                    load(C_OUT + c, c % RING, rows_of(w_out[0][:, c // NC * 512:], ORDER[c % NC], column(turn, 1024, ORDER[c % NC]), 512),
                         raw[:, c % RING], turn * (2 * NC))
            def ffn_loads(turn):
                for c in range(2 * NC):
                    w = (w_gate, w_up)[c // NC][0]
                    load(C_FF + c, c % RING, rows_of(w, ORDER[c % NC], column(turn, 512, ORDER[c % NC]), 512),
                         raw[:, c % RING], turn * (2 * NC))

            ffn_loads(0)
            sp.wait_ge(kv_out, 4)
            sp.wait_ge(crow_out, 1)
            flat = "t h d -> t (h d)"
            sp.dma_start(k_prompt[0, 0].rearrange(flat), kv_rows[:, 0:2 * P]).then_inc(stored, 16)
            sp.dma_start(v_prompt[0, 0].rearrange(flat), kv_rows[:, 2 * P:4 * P]).then_inc(stored, 16)
            sp.dma_start(k_sample[0, :, WINDOW - 1].rearrange(flat), kv_dec[:, 0:2 * P]).then_inc(stored, 16)
            sp.dma_start(v_sample[0, :, WINDOW - 1].rearrange(flat), kv_dec[:, 2 * P:4 * P]).then_inc(stored, 16)
            sp.dma_start(conv_sample[0, :, 0, :], state_conv[0, :, 1, :]).then_inc(stored, 16)
            sp.dma_start(conv_prompt[0, 0], conv_rows[0:2, :]).then_inc(stored, 16)
            sp.dma_start(conv_sample[0, :, 1, :], conv_rows[2:2 + ND, :]).then_inc(stored, 16)
            with sp.Fori(1, 1 + ND) as turn:
                ffn_loads(turn)
                for cache, out in ((cache_k, k_sample), (cache_v, v_sample)):
                    to, of = (x[0].rearrange("b t h d -> b (t h d)")[bass.ds(turn - 1, 1), start:start + (WINDOW - 1) * 2 * P]
                              .rearrange("b (a n) -> a (b n)", a=16) for x, start in ((out, 0), (cache, 2 * P)))
                    sp.dma_start(to, of).then_inc(stored, 16)
            with sp.Fori(1 + ND, FF_TURNS) as turn:
                ffn_loads(turn)
            with sp.Fori(0, 2) as turn:
                for c in range(2 * DC):
                    load(C_DOWN + c, c % RING, rows_of(w_down[0][:, c // DC * 512:], c % DC, column(turn, 1024, c % DC), 512),
                         raw[:, c % RING], turn * (2 * DC))
            for i in range(8):
                q, t = i // 2, i % 2 * P
                cols = slice(512 * q, 512 * q + 512)
                sp.wait_ge(yt_act, i + 1)
                sp.dma_start(y_prompt[0, t:t + P, cols], rows_out[:, i % 2, cols]).then_inc(stored, 16)
            sp.wait_ge(yt_dve, 1)
            sp.dma_start(y_sample[:, 0, :].rearrange("t (k p) -> k t p", k=KT),
                         dec_rows_y[:]).then_inc(stored, 16)
            sp.wait_ge(stored, 16 * (4 + 2 * ND + 3 + 8 + 1))

        @block.tensor
        def _(pe):
            def tr(out, in_):
                n = in_.shape[0]
                return nc.tensor.transpose(out, in_, ident[0:n, 0:n])

            def chunk(slot, tiles, bank, k0, moving_hi, moving_lo, first, last, out, cols, bank_free=None):
                for m in range(tiles):
                    if bank_free and m == tiles - 1:
                        pe.wait_ge(*bank_free)
                    for j in range(2):
                        col = (j * tiles + m) * P
                        hi, lo = w_hi[:, slot, col:col + P], w_lo[:, slot, col:col + P]
                        for i, (w, x) in enumerate(((hi, moving_hi), (hi, moving_lo), (lo, moving_hi))):
                            mm = nc.tensor.matmul(ps[:, bank + m, out], w, x[:, k0 + j, cols],
                                                  start=first and j == 0 and i == 0,
                                                  stop=last and j == 1 and i == 2)
                return mm

            def project(n, c, slot, tiles, bank, out, cols, turn=0, bank_free=None):
                pe.wait_ge(lo_ready, RING + n + 1 + turn)
                mm = chunk(slot, tiles, bank, 2 * ORDER[c], op_hi, op_lo, c == 0, c == NC - 1, out, cols, bank_free)
                mm.then_inc(chunk_used, 1)

            def spread(scratch, bank):
                pe.wait_ge(diag_ready, 1)
                nc.tensor.matmul(ps[:, bank, 0:2 * P], ones[:], scratch[:, 0:2, :], start=True, stop=True)
                nc.tensor.matmul(ps[:, bank, 2 * P:N], ones[:], scratch[:, 2, 0:N - 2 * P], start=True, stop=True).then_inc(bcast_done, 1)

            pe.wait_ge(ident_in, 16)
            pe.wait_ge(vec_in, 80)
            tr(ps[:, 7, 0:NVEC], vec_rows[:]).then_inc(vec_done, 1)
            def transpose_x(i):
                k = K_ORDER[i]
                if i >= 4:
                    pe.wait_ge(op_lo_ready, i - 3)
                for blk, (t, size) in enumerate(BLOCKS):
                    half = k * P // (D // 2)
                    if i == 0 or half == 0 and K_ORDER[i - 1] * P >= D // 2:
                        pe.wait_ge(x_in[half][blk], 16 if blk == 1 else 32)
                    mm = tr(ps[:, X_BANKS[i % 4], t:t + size], rows_in[0:size, blk, k * P:k * P + P])
                mm.then_inc(xt_done, 1)

            pe.wait_ge(vec_out, 1)
            for i in range(4):
                transpose_x(i)

            for c in range(QKV_TURNS * 2 * NC):
                if c < NC:
                    pe.wait_ge(op_lo_ready, 2 * c + 2)
                wanted = ALL if c < 2 * NC else WANTED
                project(C_QKV + c, c % NC, c % RING, NA, NA * (c // NC % 2), wanted, wanted)
                for i in range(2 * c + 4, min(2 * c + 6, KT)):
                    transpose_x(i)
                if c == 1:
                    pe.wait_ge(table_in, 32)
                    pe.wait_ge(filled, 4)
                    nc.tensor.matmul(ps[0:HEADS, 6, 0:BIAS_N], table[:], onehot_s[:], start=True, stop=True).then_inc(rel_done, 1)
                if c == NC - 1:
                    spread(x_diag, 6)
                if BIAS_AT <= c < BIAS_AT + HEADS // 2:
                    i = c - BIAS_AT
                    if i == 0:
                        pe.wait_ge(const_in, 32)
                        pe.wait_ge(rstd_ready, 1)
                    if i % 2 == 0:
                        pe.wait_ge(hankel_in[i // 2], 16)
                    if i >= 2:
                        pe.wait_ge(bias_out, i - 1)
                    nc.tensor.matmul(ps[:, 6 + i % 2, :], flip[:], hankel[:, 2 * i:2 * i + 2, :],
                                     start=True, stop=True).then_inc(bias_done, 1)
                if KCT_AT <= c < KCT_AT + 4:
                    i = c - KCT_AT
                    if i == 0:
                        pe.wait_ge(kcache_in, 16)
                    if i < 2:
                        pe.wait_ge(bias_out, HEADS // 2 - 1 + i)
                    else:
                        pe.wait_ge(kct_out, i - 1)
                    for m in range(4):
                        b, r = 2 * i + m // 2, m % 2
                        mm = tr(ps[:, 6 + i % 2, m * P:m * P + P], kc[:, b, r * P:r * P + P])
                    mm.then_inc(kct_done, 1)
                if c == 22:
                    pe.wait_ge(z_out, 2)
                    pe.wait_ge(kct_out, 3)
                    for m in range(4):
                        b, r = m // 2, m % 2
                        mm = tr(ps[:, 6, m * P:m * P + P], zT[:, 10 + r, T0 + b * P:T0 + b * P + P])
                    mm.then_inc(kv_done, 1)
                if c == 23:
                    pe.wait_ge(kct_out, 4)
                    for r in range(2):
                        mm = tr(ps[0:N_META, 7, r * P:r * P + P], zT[:, 10 + r, 0:N_META])
                    mm.then_inc(kv_done, 1)
                if c == 24:
                    pe.wait_ge(kv_out, 1)
                    for m in range(4):
                        mm = tr(ps[:, 6, m * P:m * P + P], zT[:, 8 + m, NP - WINDOW:NP])
                    mm.then_inc(kv_done, 1)
                if c == 25:
                    pe.wait_ge(kv_out, 2)
                    for m in range(4):
                        mm = tr(ps[0:ND, 7, m * P:m * P + P], zT[:, 8 + m, NP:N])
                    mm.then_inc(kv_done, 1)
                if c == 27:
                    pe.wait_ge(state_in, 16)
                    pe.wait_ge(kv_out, 3)
                    for j in range(CT):
                        mm = tr(ps[:, 6, j * 2 * ND:(j + 1) * 2 * ND], state_rows[:, j * P:j * P + P])
                    mm.then_inc(state_done, 1)

            def conv_turn(turn, last_turn):
                for c in range(2 * NC):
                    project(C_CONV + c, c % NC, c % RING, NA, NA * (c // NC), slice(0, NU), slice(U0, N), turn * (2 * NC))
                    if c == 0:
                        pe.wait_ge(q_staged, 2 * turn + 2)
                        pe.wait_ge(k_staged, turn + 1)
                        for h in range(GROUP):
                            mm = nc.tensor.matmul(ps[:, 6, h * P:h * P + P], qs[:, h, 0:P], ks[:, T0:KEYS_A],
                                                  start=True, stop=True)
                        mm.then_inc(scores_done, 1)
                        for h in range(GROUP):
                            mm = nc.tensor.matmul(ps[:, 7, h * N_META:(h + 1) * N_META], qs[:, h, 0:P], ks[:, 0:N_META],
                                                  start=True, stop=True)
                        mm.then_inc(scores_done, 1)
                    if c in (1, 2):
                        pe.wait_ge(scores_out, 4 * turn + c)
                        for i in range(2):
                            mm = nc.tensor.matmul(ps[:, 5 + c, i * 256:i * 256 + 256], qs[:, 2 * (c - 1) + i, P:2 * P],
                                                  ks[:, T0:NP], start=True, stop=True)
                        mm.then_inc(scores_done, 1)
                    if last_turn and c in (3, 4):
                        pe.wait_ge(scores_out, 4 * turn + c)
                        pe.wait_ge(qd_staged, 8)
                        for row in range(4 * (c - 3), 4 * (c - 3) + 4):
                            for r in range(2):
                                nc.tensor.matmul(ps[:, 6, row * HEADS + 8 * r:row * HEADS + 8 * r + 8],
                                                 kct[:, row, r, :], qd[:, r, row, :], start=True, stop=True)
                    if last_turn and c == 4:
                        own = ps[0:ND, 7, 0:P].rearrange("p (b r h) -> p r b h", r=2, h=8)
                        for r in range(2):
                            mm = nc.tensor.matmul(own[:, r], zT[:, 8 + r, NP:N], qd[:, r], start=True, stop=True)
                        mm.then_inc(dec_scores, 1)
                    if c in (5, 6, 7, 8):
                        if c == 5:
                            pe.wait_ge(probs_ready, 2 * turn + 1)
                            if last_turn:
                                pe.wait_ge(dec_scores_out, 2)
                            else:
                                pe.wait_ge(scores_out, 4 * turn + 3)
                            src = s_a[:, :, T0:KEYS_A]
                        if c == 6:
                            pe.wait_ge(scores_out, 4 * turn + 4)
                            src = s_a[:, :, 0:N_META]
                        if c == 7:
                            pe.wait_ge(probs_ready, 2 * turn + 2)
                            pe.wait_ge(probs_t_act, 2 * turn + 1)
                            src = s_b[:, :, 0:P]
                        if c == 8:
                            pe.wait_ge(probs_t_dve, 2 * turn + 1)
                            src = s_b[:, :, P:2 * P]
                        for h in range(GROUP):
                            mm = tr(ps[0:src.shape[2], 6 if c % 2 else 7, h * P:h * P + P], src[:, h])
                        mm.then_inc(probs_t, 1)
                    if last_turn and c == 9:
                        pe.wait_ge(probs_t_act, 2 * turn + 2)
                        pe.wait_ge(table_d_ready, 1)
                        nc.tensor.matmul(ps[:, 6, 0:P + 1], table_d[:].rearrange("p b h -> p (b h)"),
                                         onehot_s[:, P - 1:2 * P], start=True, stop=False)
                        nc.tensor.matmul(ps[:, 6, 0:P], sdt[:], ident[:], start=False, stop=True)
                        tr(ps[:, 6, 256:256 + ND], sd_own[:]).then_inc(dec_rows, 1)
                    if c == 10:
                        pe.wait_ge(v_staged, 4 * turn + 4)
                        pe.wait_ge(probs_t_act, 2 * turn + 1)
                        pe.wait_ge(probs_t_dve, 2 * turn + 2)
                        nc.tensor.matmul(ps[:, 7, :], vs[:, 0].rearrange("p a d -> p (a d)"), pt[:, 0, :],
                                         start=True, stop=False)
                        nc.tensor.matmul(ps[:, 7, :], vs[0:N_META, 2].rearrange("p a d -> p (a d)"), pt_m[:],
                                         start=False, stop=True).then_inc(pv_done, 1)
                    if c == 11:
                        pe.wait_ge(probs_t_act, 2 * turn + 2)
                        if last_turn:
                            pe.wait_ge(dec_rows_out, 2)
                        nc.tensor.matmul(ps[:, 6, :], vs[:, 0].rearrange("p a d -> p (a d)"), pt[:, 1, :],
                                         start=True, stop=False)
                        nc.tensor.matmul(ps[:, 6, :], vs[:, 1].rearrange("p a d -> p (a d)"), pt[:, 2, :],
                                         start=False, stop=True).then_inc(pv_done, 1)
                    if last_turn and c == 12:
                        pe.wait_ge(dec_probs, 2)
                        pe.wait_ge(pv_act, 4 * turn + 4)
                        tr(ps[:, 6, 0:P], sd[:, 0:P])
                        tr(ps[0:ND, 6, P:2 * P], sd_own8[:]).then_inc(dec_pt, 1)
                    if last_turn and c >= 14:
                        r = c - 14
                        if r == 0:
                            pe.wait_ge(dec_pt_out, 2)
                            pe.wait_ge(vcache_in, 16)
                            pe.wait_ge(kv_out, 4)
                        own = pd_own[:].rearrange("p (b r h) -> p r b h", r=2, h=8)
                        out = ps[:, 7, HEAD * r:HEAD * r + HEAD]
                        nc.tensor.matmul(out.rearrange("p (b h) -> p b h", h=8), kv_dec[:, 2 * P + r * P:3 * P + r * P],
                                         own[:, r], start=True, stop=False)
                        for row in range(ND):
                            mm = nc.tensor.matmul(out[:, 8 * row:8 * row + 8], vc[:, row, r * P:r * P + P],
                                                  pd[:, row * HEADS + 8 * r:row * HEADS + 8 * r + 8],
                                                  start=False, stop=row == ND - 1)
                        mm.then_inc(dec_pv, 1)

            with pe.Fori(0, CONV_TURNS - 1) as turn:
                conv_turn(turn, False)
            conv_turn(CONV_TURNS - 1, True)

            with pe.Fori(0, 2) as turn:
                for c in range(2 * NC):
                    if c < NC:
                        pe.wait_ge(op_lo_ready, KT + (1 if c < 3 else 2 if c < 7 else 3))
                    if c == NC:
                        pe.wait_ge(dec_pv_out, 4)
                    project(C_OUT + c, c % NC, c % RING, NB, NB * (c // NC), slice(0, M), WANTED, turn * (2 * NC),
                            (zb_ready, CT) if c == 0 else None)

            def token_sums(k, total, last, bank):
                pe.wait_ge(acc_ready, k)
                nc.tensor.matmul(ps[:, bank, 0:M], ones[:], total[:, 0, :], start=True, stop=False)
                for m in range(NB):
                    if m % 2 == 0:
                        pe.wait_ge(sq_ready, 5 * (k - 1) + 4 + m // 2)
                    mm = nc.tensor.matmul(ps[:, bank, 0:M], ones[:], last[:, m, :], start=False, stop=m == NB - 1)
                mm.then_inc(sums_done, 1)

            pe.wait_ge(mix_out, 3)
            token_sums(1, acc4, sq, 2)
            pe.wait_ge(conv_done, CT)
            for j in range(CT):
                mm = tr(ps[0:2 + ND, j // 4, j % 4 * P:j % 4 * P + P], u_out[:, j, :])
            mm.then_inc(crow_done, 1)

            pe.wait_ge(crow_out, 1)
            pe.wait_ge(root_ready, 1)
            pe.wait_ge(mix_out, 4)
            with pe.Fori(0, FF_TURNS) as turn:
                for c in range(2 * NC):
                    if c < NC:
                        pe.wait_ge(op_lo_ready, KT + 3 + 2 * c + 2)
                    project(C_FF + c, c % NC, c % RING, NB, NB * (c // NC), slice(0, M), WANTED, turn * (2 * NC))

            with pe.Fori(0, 2) as turn:
                for c in range(2 * DC):
                    k = c % DC
                    pe.wait_ge(lo_ready, RING + C_DOWN + c + 1 + turn * (2 * DC))
                    if c < DC and k * 2 + 2 > FT - NB:
                        pe.wait_ge(hid_lo, FF_TURNS)
                    elif c == 0:
                        pe.wait_ge(hid_lo, FF_TURNS - 1)
                    elif c == DC:
                        pe.wait_ge(up_ready, FF_TURNS)
                    chunk(c % RING, NB, NB * (c // DC), 2 * k, h_hi, h_lo, k == 0, k == DC - 1,
                          slice(0, M), slice(0, M)).then_inc(chunk_used, 1)
            token_sums(2, y_acc, y_sq, 0)
            pe.wait_ge(y_out, 4)
            for i in range(8):
                q, t = i // 2, i % 2 * P
                if i % 2 == 0:
                    pe.wait_ge(y_ready_pool, q + 1)
                    pe.wait_ge(y_ready_dve, q + 1)
                for m in range(NB):
                    mm = tr(ps[:, i, m * P:m * P + P], yT[:, NB * q + m, t:t + P])
                mm.then_inc(yt_done, 1)
            pe.wait_ge(dec_y_ready, 1)
            pe.wait_ge(yt_act, 1)
            tr(ps[:, 0, 0:P], dec_y[:].rearrange("p k t -> p (k t)")).then_inc(yt_done, 1)

        @block.gpsimd
        def _(pool):
            own = Own(pool, pool_own)
            nc.gpsimd.memset(stat3[:, 6:7], 0.0).then_inc(lo_ready, RING)
            nc.gpsimd.memset(cw[:], 0.0).then_inc(chunk_used, RING)
            own.link(nc.gpsimd.memset(eps[:], EPS))
            own.link(nc.gpsimd.memset(stat_b[:], 0.0))
            nc.gpsimd.memset(stat3[:, 7:8], -0.5).then_inc(filled, 1)
            nc.gpsimd.memset(stat3[:, 0:3], 1.0).then_inc(filled, 1)
            pool.wait_ge(filled, 2)
            nc.gpsimd.memset(table[BUCKETS:BUCKETS + 1, :], 1.0).then_inc(filled, 1)
            pool.wait_ge(filled, 3)
            nc.gpsimd.memset(ones[:], 1.0).then_inc(filled, 1)
            pool.wait_ge(filled, 4)
            pool.dma_start(onehot_s[:], onehot).then_inc(table_in, 16)
            pool.dma_start(table[0:BUCKETS, :], rel_bias).then_inc(table_in, 16)
            pool.dma_start(flip[:], squares[1]).then_inc(const_in, 16)
            pool.dma_start(masks[:], row_masks).then_inc(const_in, 16)
            pool.dma_start(sink[:], attn_sinks[0:1, :].broadcast_to([P, HEADS])).then_inc(sink_in, 16)

            pool.wait_ge(rms_ready, 1)
            nc.gpsimd.tensor_tensor(stat3[:, 3:6], stat3[:, 0:3], stat3[:, 7:8].broadcast_to([P, 3]),
                                    ALU.pow).then_inc(inv_ready, 1)

            def stage_k(g):
                nc.gpsimd.tensor_copy(ks[:], at(kd, g)).then_inc(k_staged, 1)

            def stage_v(g):
                for half in range(2):
                    nc.gpsimd.tensor_copy(vs[:, 0:2, half, :], vd[:, 0:2, bass.ds(g * HEAD, HEAD)]).then_inc(v_staged, 1)
                    nc.gpsimd.tensor_copy(vs[0:16, 2, half, :], vd[0:16, 2, bass.ds(g * HEAD, HEAD)]).then_inc(v_staged, 1)

            def tap_of(i):
                return cw[:, i:i + 1].broadcast_to([P, EXT - 2])

            def conv_tile(j, half):
                pool.wait_ge(zb_ready, j + 1)
                g, c, h = (zb[:, half, i, :] for i in range(3))
                dec = u_ext[:, SEQ + 2:EXT].rearrange("p (b t) -> p b t", t=3)
                kept, out = at(u_out, j), at(convT, j)
                taps = vec[:, V_CONV:NVEC].rearrange("p (i j) -> p i j", j=CT)[:, :, bass.ds(j, 1)]
                own.link(nc.gpsimd.tensor_copy(cw[:], taps.rearrange("p i j -> p (i j)")))
                own.link(nc.gpsimd.tensor_copy(dec[:, :, 0:2], at(state_t, j).rearrange("p (b t) -> p b t", t=2)))
                own.link(nc.gpsimd.tensor_tensor(u_ext[:, 0:SEQ + 2], c[:, 0:SEQ + 2], h[:, 0:SEQ + 2], ALU.mult))
                own.link(nc.gpsimd.tensor_tensor(dec[:, :, 2], c[:, SEQ + 2:NU], h[:, SEQ + 2:NU], ALU.mult))
                own.link(nc.gpsimd.tensor_tensor(acc[:], u_ext[:, 0:EXT - 2], tap_of(0), ALU.mult))
                own.link(nc.gpsimd.tensor_tensor(tap[:], u_ext[:, 1:EXT - 1], tap_of(1), ALU.mult))
                own.link(nc.gpsimd.tensor_tensor(acc[:], acc[:], tap[:], ALU.add))
                own.link(nc.gpsimd.tensor_tensor(tap[:], u_ext[:, 2:EXT], tap_of(2), ALU.mult))
                own.link(nc.gpsimd.tensor_tensor(acc[:], acc[:], tap[:], ALU.add))
                nc.gpsimd.tensor_copy(kept[:, 0:2], u_ext[:, SEQ:SEQ + 2])
                nc.gpsimd.tensor_copy(kept[:, 2:2 + ND], dec[:, :, 2])
                nc.gpsimd.tensor_tensor(out[:, 0:SEQ], acc[:, 0:SEQ], g[:, 2:SEQ + 2], ALU.mult)
                nc.gpsimd.tensor_tensor(out[:, SEQ:M], acc[:, SEQ + 2:EXT - 2:3], g[:, SEQ + 2:NU], ALU.mult).then_inc(conv_done, 1)

            CONV_LINKS = 9

            pool.wait_ge(bias_done, HEADS // 2)
            nc.gpsimd.memset(qs[:], 0.0).then_inc(zeroed, 1)
            nc.gpsimd.memset(qd[:], 0.0).then_inc(zeroed, 1)
            pool.wait_ge(zeroed, 2)
            pool.wait_ge(kd_ready, 4)
            stage_k(KVH - 1)
            pool.wait_ge(kv_out, 2)
            stage_v(KVH - 1)
            pool.wait_ge(z_out, 4)
            pool.wait_ge(v_staged, 4)
            for e in range(2):
                for a in range(2):
                    for r in range(2):
                        q = zT[HEAD * e:HEAD * e + HEAD, 4 * r + 2 * a:4 * r + 2 * a + 2, NP:N].rearrange("p i b -> p b i")
                        nc.gpsimd.tensor_scalar(qd[HEAD * a:HEAD * a + HEAD, r, :, 4 * a + e:4 * a + 4:2], q,
                                                HEAD ** -0.5, None, ALU.mult).then_inc(qd_staged, 1)
                        pool.wait_ge(qd_staged, 4 * e + 2 * a + r + 1)
            pool.wait_ge(state_out, 1)
            with pool.Fori(0, CONV_TURNS - 1) as turn:
                own.begin(turn, 2 * CONV_LINKS)
                conv_tile(turn * 2, 0)
                pool.wait_ge(scores_done, 4 * turn + 4)
                stage_k(turn * -1 + (KVH - 2))
                conv_tile(turn * 2 + 1, 1)
                pool.wait_ge(pv_done, 2 * turn + 2)
                stage_v(turn * -1 + (KVH - 2))
                own.end(CONV_TURNS - 1)
            conv_tile(CT - 2, 0)
            conv_tile(CT - 1, 1)

            def square_sums(k, total, scratch):
                base = 5 * (k - 1)
                pool.wait_ge(sq_ready, base + 2)
                nc.gpsimd.tensor_tensor(total[:], total[:], scratch[:], ALU.add).then_inc(pool_sums, 1)
                pool.wait_ge(pool_sums, 2 * k - 1)
                pool.wait_ge(sq_ready, base + 3)
                nc.gpsimd.tensor_tensor(total[:], total[:], scratch[:], ALU.add).then_inc(pool_sums, 1)
                pool.wait_ge(pool_sums, 2 * k)
                own.link(nc.gpsimd.tensor_tensor(total[:, 0:2, :], total[:, 0:2, :], total[:, 2:4, :], ALU.add))
                nc.gpsimd.tensor_tensor(total[:, 0, :], total[:, 0, :], total[:, 1, :], ALU.add).then_inc(acc_ready, 1)

            square_sums(1, acc4, sq)
            for n in range(NC):
                pool.wait_ge(scaled, n + 1)
                pair = slice(K_ORDER[2 * n], K_ORDER[2 * n] + 2)
                nc.gpsimd.tensor_tensor(resid[:, pair, WANTED], tmp[:, n % 2], resid[:, pair, WANTED], ALU.add).then_inc(resid_ready, 1)
            for i in range(1, 4):
                pool.wait_ge(rsq_ready, 2 * i + 2)
                nc.gpsimd.tensor_tensor(acc4[:], acc4[:], sq[:], ALU.add).then_inc(rsum, 1)
                pool.wait_ge(rsum, i)
            own.link(nc.gpsimd.tensor_tensor(acc4[:, 0:2, :], acc4[:, 0:2, :], acc4[:, 2:4, :], ALU.add))
            own.link(nc.gpsimd.tensor_tensor(acc4[:, 0, :], acc4[:, 0, :], acc4[:, 1, :], ALU.add))
            nc.gpsimd.partition_all_reduce(acc4[:, 1, :], acc4[:, 0, :], P, RADD).then_inc(tot_ready, 1)
            with pool.Fori(0, FF_TURNS) as turn:
                pool.wait_ge(sig_ready, turn + 1)
                nc.gpsimd.tensor_tensor(gate[:], gate[:], up[:], ALU.mult).then_inc(swish_ready, 1)
                pool.wait_ge(swish_ready, turn + 1)
                pool.wait_ge(up_ready, turn + 1)
                nc.gpsimd.tensor_tensor(up[:], up[:], gate[:], ALU.mult).then_inc(hid_ready, 1)
                pool.wait_ge(hid_ready, turn + 1)
                pool.wait_ge(hid_hi, turn + 1)
                nc.gpsimd.tensor_tensor(h_lo[:, bass.ds(turn * NB, NB), :], up[:],
                                        h_hi[:, bass.ds(turn * NB, NB), :].bitcast(F32), ALU.subtract).then_inc(hid_lo, 1)
            square_sums(2, y_acc, y_sq)
            for q in range(4):
                pool.wait_ge(y_scaled, 2 * q + 1)
                pair = slice(NB * q, NB * q + 2)
                nc.gpsimd.tensor_tensor(yT[:, pair, :], yT[:, pair, :], resid[:, pair, WANTED], ALU.add).then_inc(y_ready_pool, 1)

        @block.scalar
        def _(act):
            act.dma_start(ident[:], squares[0]).then_inc(ident_in, 16)
            for i, gain in enumerate((norm_pre_mix, norm_post_mix, norm_pre_ffn, norm_post_ffn)):
                act.dma_start(vec_rows[KT * i:KT * i + KT, :], gain[0].rearrange("(t p) -> t p", p=P)).then_inc(vec_in, 16)
            act.dma_start(vec_rows[V_CONV:NVEC, :], conv_w[0].rearrange("i (j p) -> (i j) p", p=P)).then_inc(vec_in, 16)

            def split(n, slot, size, loads, turn=0, turn_loads=0):
                act.wait_ge(raw_landed[slot], 16 * loads + turn_loads)
                act.wait_ge(chunk_used, n + 1 + turn)
                nc.scalar.activation(w_hi[:, slot, 0:size].rearrange("p (j n) -> p j n", j=2),
                                     raw[:, slot, :, 0:size // 2], ACT.Copy).then_inc(hi_ready, 1)

            def loads_to(n):
                a, b = C_CONV // RING, C_OUT // RING
                done = n // RING + 1
                return done + min(max(done - a, 0), b - a)

            def square_x(half, blk, done):
                size = BLOCKS[blk][1]
                act.wait_ge(x_in[half][blk], 16 if blk == 1 else 32)
                if done:
                    act.wait_ge(x_squared, done)
                total = (stat3, stat_b)[half]
                nc.scalar.activation(x_sq[0:size, :], rows_in[0:size, blk, half * D // 2:(half + 1) * D // 2], ACT.Square,
                                     accum_out=total[0:size, blk:blk + 1]).then_inc(x_squared, 1)

            act.wait_ge(filled, 4)
            nc.scalar.activation(stat3[:, 6:7], ones[:, 0:1], ACT.Square)
            square_x(1, 0, 0)
            act.wait_ge(vec_out, 1)
            for n in range(NC):
                if n:
                    split(n, n % RING, 768, loads_to(n))
                for i in (2 * n, 2 * n + 1):
                    k = K_ORDER[i]
                    act.wait_ge(xt_done, i + 1)
                    nc.scalar.activation(op_hi[:, k, :], ps[:, X_BANKS[i % 4], 0:N], ACT.Copy,
                                         scale=vec[:, V_PRE_MIX + k:V_PRE_MIX + k + 1]).then_inc(op_hi_ready, 1)
                    nc.scalar.activation(resid[:, k, :], ps[:, X_BANKS[i % 4], 0:N], ACT.Copy).then_inc(xt_out, 1)
                if n == 0:
                    split(n, n % RING, 768, loads_to(n))
                if n == 1:
                    square_x(1, 1, 1)
                    square_x(1, 2, 2)
                if 3 <= n < 6:
                    square_x(0, n - 3, n)

            def stage_q(g):
                for e in range(2):
                    part = slice(HEAD * e, HEAD * e + HEAD)
                    nc.scalar.activation(qs[part, e:GROUP:2, :], zT[part, bass.ds(g * 2, 2), T0:NP], ACT.Copy).then_inc(q_staged, 1)

            for c in range(NC - RING, QKV_TURNS * 2 * NC):
                split(c + RING, c % RING, 768, loads_to(c + RING))
                if KCT_AT <= c < KCT_AT + 4:
                    i = c - KCT_AT
                    act.wait_ge(kct_done, i + 1)
                    nc.scalar.activation(kct[:, 2 * i:2 * i + 2, :, :].rearrange("p b r k -> p (b r k)"),
                                         ps[:, 6 + i % 2, :], ACT.Copy).then_inc(kct_out, 1)
                if c == 23:
                    act.wait_ge(z_out, 2)
                    for a in range(2):
                        for half in range(2):
                            nc.scalar.activation(kd[HEAD * half:HEAD * half + HEAD, a:KVH:2, :],
                                                 zT[HEAD * a:HEAD * a + HEAD, 8:10, 0:NP], ACT.Copy,
                                                 scale=HEAD ** -0.5).then_inc(kd_ready, 1)
                if c == 24:
                    act.wait_ge(zeroed, 1)
                    stage_q(KVH - 1)

            def conv_turn(turn, g, last_turn):
                for c in range(2 * NC):
                    into_next = (c + RING) // (2 * NC)
                    if last_turn and into_next:
                        split(C_CONV + c + RING, c % RING, 1024, loads_to(C_CONV + 2 * NC * CONV_TURNS + c + RING - 2 * NC), turn * (2 * NC))
                    else:
                        loads = C_CONV // RING + 2 * ((c + RING) // RING + 1)
                        split(C_CONV + c + RING, c % RING, 768, loads, turn * (2 * NC), turn * (16 * 2 * 2 * NC // RING))
                    if c in (1, 3):
                        scores, col = (s_a, 0) if c == 1 else (s_b, 4)
                        act.wait_ge(nmax_ready, 2 * turn + 1 + c // 2)
                        for h in range(GROUP):
                            nc.scalar.activation(scores[:, h], scores[:, h], ACT.Exp, bias=nmax[:, col + h:col + h + 1],
                                                 accum_out=den[:, col + h:col + h + 1])
                        nc.scalar.activation(esk[:, col:col + 4], esk[:, col:col + 4], ACT.Exp).then_inc(exp_done, 1)
                    if c in (5, 7):
                        act.wait_ge(probs_t, 4 * turn + (1 if c == 5 else 3))
                        nc.scalar.activation(pt[:, 0 if c == 5 else 1, :], ps[:, 6, :], ACT.Copy).then_inc(probs_t_act, 1)
                    if last_turn and c == 10:
                        act.wait_ge(dec_nmax, 1)
                        nc.scalar.activation(sd[:], sd[:], ACT.Exp, bias=dstat[:, 0:1], accum_out=dstat[:, 2:3])
                        nc.scalar.activation(dstat[:, 3:4], dstat[:, 1:2], ACT.Exp, bias=dstat[:, 0:1]).then_inc(dec_exp, 1)
                    if c in (10, 11):
                        block_i = c - 10
                        act.wait_ge(pv_done, 2 * turn + 1 + block_i)
                        src = ps[:, 7 - block_i, :].rearrange("p (i e q) -> p i e q", e=2, q=P)
                        for e in range(2):
                            part = slice(HEAD * e, HEAD * e + HEAD)
                            nc.scalar.activation(zT[part, bass.ds(g * 2, 2), T0 + block_i * P:T0 + block_i * P + P],
                                                 src[part, :, e, :], ACT.Copy).then_inc(pv_act, 1)
                    if c == 13 and not last_turn:
                        stage_q(g - 1)
                    if last_turn and c == 12:
                        act.wait_ge(conv_done, CT - 2)
                        act.wait_ge(chunk_used, RING + C_OUT - NC + 3)
                        nc.scalar.activation(op_hi[:, 8:14, WANTED], convT[:, 0:6, :], ACT.Copy).then_inc(op_hi_ready, 1)

            with act.Fori(0, CONV_TURNS - 1) as turn:
                conv_turn(turn, turn * -1 + (KVH - 1), False)
            conv_turn(CONV_TURNS - 1, 0, True)
            act.wait_ge(dec_pv_out, 4)
            act.wait_ge(pv_act, 4 * CONV_TURNS)
            act.wait_ge(chunk_used, RING + C_OUT - 1)
            nc.scalar.activation(op_hi[:, 0:8, WANTED], zT[:, 0:8, WANTED], ACT.Copy).then_inc(op_hi_ready, 1)

            def group_out(k, group, bank, dst, gain, total, scratch, out_ready):
                base = 5 * (k - 1)
                if group == 2:
                    act.wait_ge(pool_sums, 2 * k - 1)
                if group == 3:
                    act.wait_ge(acc_ready, k)
                if group < 3:
                    square = total if group == 0 else scratch
                    nc.scalar.activation(square[:], ps[:, bank:bank + NB, 0:M], ACT.Square).then_inc(sq_ready, 1)
                else:
                    for m in (0, 2):
                        nc.scalar.activation(scratch[:, m:m + 2, :], ps[:, bank + m:bank + m + 2, 0:M], ACT.Square).then_inc(sq_ready, 1)
                for m in range(NB):
                    t = NB * group + m
                    mm = nc.scalar.activation(dst[:, t, :], ps[:, bank + m, 0:M], ACT.Copy,
                                              scale=vec[:, gain + t:gain + t + 1])
                mm.then_inc(out_ready, 1)

            for c in range(4 * NC):
                if c == 3:
                    act.wait_ge(conv_done, CT)
                    nc.scalar.activation(op_hi[:, 14:16, WANTED], convT[:, 6:8, :], ACT.Copy).then_inc(op_hi_ready, 1)
                    nc.scalar.activation(stat3[:, 6:7], eps[:], ACT.Sqrt)
                if c % NC == NC - 1:
                    group = c // NC
                    act.wait_ge(chunk_used, RING + C_OUT + c + 1)
                    group_out(1, group, NB * (group % 2), mixT, V_POST_MIX, acc4, sq, mix_out)
                if c < 4 * NC - 1:
                    split(C_OUT + c + RING, c % RING, 1024, loads_to(C_OUT + c + RING))

            def inverse_rms(k, total, dst):
                nc.scalar.activation(dst, total, ACT.Sqrt, bias=eps[:], scale=1.0 / D).then_inc(root_ready, 1)

            act.wait_ge(sums_done, 1)
            inverse_rms(1, ps[:, 2, 0:M], root[:])
            act.wait_ge(crow_done, 1)
            nc.scalar.activation(conv_rows[:], ps[0:2 + ND, 0:2, :].rearrange("p a n -> p (a n)"), ACT.Copy).then_inc(crow_out, 1)

            def input_pair(n):
                act.wait_ge(resid_ready, n + 1)
                for i in (2 * n, 2 * n + 1):
                    k = K_ORDER[i]
                    nc.scalar.activation(op_hi[:, k, WANTED], resid[:, k, WANTED], ACT.Copy,
                                         scale=vec[:, V_PRE_FFN + k:V_PRE_FFN + k + 1]).then_inc(op_hi_ready, 1)

            def ffn_turn(turn, first):
                for c in range(2 * NC):
                    if first:
                        if LEAD + c < NC:
                            input_pair(LEAD + c)
                    split(C_FF + c + RING, c % RING, 1024, loads_to(C_FF + c + RING), turn * (2 * NC),
                          turn * (16 * 2 * NC // RING))
                    if first and 2 <= c < 6:
                        i = c - 2
                        act.wait_ge(resid_ready, 2 * i + 2)
                        if i >= 2:
                            act.wait_ge(rsum, i - 1)
                        square = acc4 if i == 0 else sq
                        for m in range(0, 4, 2):
                            k = K_ORDER[4 * i + m]
                            nc.scalar.activation(square[:, m:m + 2, :], resid[:, k:k + 2, WANTED], ACT.Square).then_inc(rsq_ready, 1)
                    if first and c == NC:
                        act.wait_ge(tot_ready, 1)
                        inverse_rms(2, acc4[:, 1, :], acc4[:, 2, :])
                    if c == (NC + 2 if first else NC):
                        act.wait_ge(gate_ready, turn + 1)
                        nc.scalar.activation(up[:], gate[:], ACT.Sigmoid).then_inc(sig_ready, 1)
                    if c == 2 * NC - 1:
                        act.wait_ge(hid_ready, turn + 1)
                        nc.scalar.activation(h_hi[:, bass.ds(turn * NB, NB), :], up[:], ACT.Copy).then_inc(hid_hi, 1)

            split(C_FF + RING - 1, RING - 1, 1024, loads_to(C_FF + RING - 1))
            for n in range(LEAD):
                input_pair(n)
            ffn_turn(0, True)
            with act.Fori(1, FF_TURNS) as turn:
                ffn_turn(turn, False)

            def down_slots(first, count):
                for c in range(first, first + count):
                    split(C_DOWN + c + RING, c % RING, 1024, loads_to(C_DOWN + c + RING))

            def down_turns(first, turns):
                with act.Fori(0, turns) as turn:
                    for c in range(first, first + RING):
                        split(C_DOWN + c + RING, c % RING, 1024, loads_to(C_DOWN + c + RING), turn * RING, turn * 16)

            def down_out(group):
                act.wait_ge(chunk_used, RING + C_DOWN + DC * group + DC)
                group_out(2, group, NB * (group % 2), yT, V_POST_FFN, y_acc, y_sq, y_out)

            whole = DC // RING
            for half in range(2):
                start = 2 * DC * half
                down_turns(start, whole)
                down_slots(start + whole * RING, DC % RING)
                down_out(2 * half)
                down_slots(start + DC, RING - DC % RING)
                down_turns(start + DC + RING - DC % RING, whole - half)
                if half:
                    nc.scalar.activation(stat3[:, 6:7], eps[:], ACT.Sqrt)
                down_out(2 * half + 1)
            act.wait_ge(sums_done, 2)
            inverse_rms(3, ps[:, 0, 0:M], y_root[:])
            for i in range(8):
                q = i // 2
                act.wait_ge(yt_done, i + 1)
                nc.scalar.activation(rows_out[:, i % 2, 512 * q:512 * q + 512], ps[:, i, :], ACT.Copy).then_inc(yt_act, 1)

        @block.vector
        def _(dve):
            own = Own(dve, dve_own)

            def split(n, slot, size, turn=0):
                dve.wait_ge(hi_ready, n + 1 + turn)
                hi = w_hi[:, slot, 0:size].rearrange("p (j n) -> p j n", j=2)
                lo = w_lo[:, slot, 0:size].rearrange("p (j n) -> p j n", j=2)
                nc.vector.tensor_tensor(lo, raw[:, slot, :, 0:size // 2], hi.bitcast(F32), ALU.subtract).then_inc(lo_ready, 1)

            def low_half(i, k):
                dve.wait_ge(op_hi_ready, KT + 3 + i + 1)
                nc.vector.scalar_tensor_tensor(out=op_lo[:, k, WANTED], in0=resid[:, k, WANTED],
                                               scalar=vec[:, V_PRE_FFN + k:V_PRE_FFN + k + 1],
                                               in1=op_hi[:, k, WANTED].bitcast(F32), op0=ALU.mult, op1=ALU.subtract).then_inc(op_lo_ready, 1)

            def diagonals(scratch):
                dve.wait_ge(inv_ready, 1)
                nc.vector.tensor_tensor(scratch[:], each(ident[:], [P, 3, P]),
                                        stat3[:, 3:6].unsqueeze(2).broadcast_to([P, 3, P]), ALU.mult).then_inc(diag_ready, 1)

            dve.wait_ge(vec_done, 1)
            nc.vector.tensor_copy(vec[:], ps[:, 7, 0:NVEC]).then_inc(vec_out, 1)
            for n in range(NC):
                if n:
                    split(n, n % RING, 768)
                for i in (2 * n, 2 * n + 1):
                    k = K_ORDER[i]
                    dve.wait_ge(op_hi_ready, i + 1)
                    dve.wait_ge(xt_out, i + 1)
                    nc.vector.scalar_tensor_tensor(out=op_lo[:, k, :], in0=ps[:, X_BANKS[i % 4], 0:N],
                                                   scalar=vec[:, V_PRE_MIX + k:V_PRE_MIX + k + 1],
                                                   in1=op_hi[:, k, :].bitcast(F32), op0=ALU.mult, op1=ALU.subtract).then_inc(op_lo_ready, 1)
                if n == 0:
                    split(n, n % RING, 768)
                if n == 2:
                    dve.wait_ge(rel_done, 1)
                    nc.vector.tensor_copy(bias_sb[:], ps[0:HEADS, 6, 0:BIAS_N]).then_inc(rel_out, 1)
                    dve.wait_ge(filled, 4)
                    dve.wait_ge(table_in, 32)
                    nc.vector.tensor_copy(table_d[:], each(table[:], [BUCKETS + 1, ND, HEADS])).then_inc(table_d_ready, 1)
                if n == 6:
                    dve.wait_ge(x_squared, 6)
                    own.link(nc.vector.tensor_tensor(stat3[:, 0:3], stat3[:, 0:3], stat_b[:, 0:3], ALU.add))
                    nc.vector.tensor_scalar(stat3[:, 0:3], stat3[:, 0:3], 1.0 / D, EPS, ALU.mult, ALU.add).then_inc(rms_ready, 1)
            diagonals(x_diag)
            dve.wait_ge(const_in, 32)
            dve.wait_ge(sink_in, 16)
            own.link(nc.vector.tensor_scalar(nsink[:], sink[:], -1.0, None, ALU.mult))

            for c in range(NC - RING, QKV_TURNS * 2 * NC):
                split(c + RING, c % RING, 768)
                if c == NC - 1:
                    dve.wait_ge(bcast_done, 1)
                    nc.vector.tensor_copy(rstd[:], ps[:, 6, 0:N]).then_inc(rstd_ready, 1)
                    dve.wait_ge(rstd_ready, 1)
                if c % NC == NC - 1:
                    group = c // NC
                    dve.wait_ge(chunk_used, RING + c + 1)
                    bank = NA * (group % 2)
                    wanted = ALL if group < 2 else WANTED
                    size = wanted.stop - wanted.start
                    nc.vector.tensor_tensor(zT[:, 9 - 3 * group:12 - 3 * group, wanted], ps[:, bank:bank + NA, wanted],
                                            each(rstd[:, wanted], [P, NA, size]), ALU.mult).then_inc(z_out, 1)
                if BIAS_AT <= c < BIAS_AT + HEADS // 2:
                    i = c - BIAS_AT
                    dve.wait_ge(bias_done, i + 1)
                    nc.vector.tensor_copy(bias[:, 2 * i:2 * i + 2, :].rearrange("p a n -> p (a n)"),
                                          ps[:, 6 + i % 2, :]).then_inc(bias_out, 1)
                if c == BIAS_AT + HEADS // 2:
                    own.link(nc.vector.tensor_tensor(sinks_m[:], sink[:], masks[:, ND:ND + HEADS], ALU.mult))
                    own.link(nc.vector.tensor_reduce(dstat[:, 1:2], sinks_m[:], AX.X, ALU.add))
                    own.link(nc.vector.tensor_scalar(dstat[:, 6:7], dstat[:, 1:2], -1.0, None, ALU.mult))
                if c == 22:
                    dve.wait_ge(kv_done, 1)
                    nc.vector.tensor_copy(vd[:, 0:2, :].rearrange("p a n -> p (a n)"), ps[:, 6, :]).then_inc(kv_out, 1)
                if c == 23:
                    dve.wait_ge(kv_done, 2)
                    nc.vector.tensor_copy(vd[0:N_META, 2, :], ps[0:N_META, 7, 0:2 * P]).then_inc(kv_out, 1)
                if c == 24:
                    dve.wait_ge(kv_done, 3)
                    nc.vector.tensor_copy(kv_rows[:], ps[:, 6, :]).then_inc(kv_out, 1)
                if c == 25:
                    dve.wait_ge(kv_done, 4)
                    nc.vector.tensor_copy(kv_dec[:], ps[0:ND, 7, :]).then_inc(kv_out, 1)
                if c == 27:
                    dve.wait_ge(state_done, 1)
                    nc.vector.tensor_copy(state_t[:].rearrange("p j r -> p (j r)"), ps[:, 6, 0:P]).then_inc(state_out, 1)

            def minus_max(scores, cols, heads):
                own.link(nc.vector.tensor_reduce(nmax[:, cols], scores, AX.X, ALU.max))
                own.link(nc.vector.scalar_tensor_tensor(out=nmax[:, cols], in0=nmax[:, cols], scalar=-1.0, in1=nsink[:, heads],
                                                        op0=ALU.mult, op1=ALU.min))
                nc.vector.tensor_tensor(esk[:, cols], nmax[:, cols], sink[:, heads], ALU.add).then_inc(nmax_ready, 1)

            def normalise(probs, cols):
                own.link(nc.vector.tensor_tensor(den[:, cols], den[:, cols], esk[:, cols], ALU.add))
                own.link(nc.vector.reciprocal(den[:, cols], den[:, cols]))
                nc.vector.tensor_tensor(probs, probs, den[:, cols].unsqueeze(2).broadcast_to(list(probs.shape)),
                                        ALU.mult).then_inc(probs_ready, 1)

            TURN_LINKS = 8

            def conv_turn(turn, g, last_turn):
                heads = bass.ds(g * GROUP, GROUP)
                for c in range(2 * NC):
                    size = 1024 if last_turn and c + RING >= 2 * NC else 768
                    split(C_CONV + c + RING, c % RING, size, turn * (2 * NC))
                    if c % NC == NC - 1:
                        half = c // NC
                        dve.wait_ge(chunk_used, RING + C_CONV + c + 1 + turn * (2 * NC))
                        nc.vector.tensor_tensor(zb[:, half], ps[:, NA * half:NA * half + NA, 0:NU],
                                                each(rstd[:, U0:N], [P, NA, NU]), ALU.mult).then_inc(zb_ready, 1)
                    if c == 0:
                        dve.wait_ge(scores_done, 4 * turn + 1)
                        nc.vector.tensor_tensor(s_a[:, :, T0:KEYS_A], heads4(ps[:, 6, :]), bias[:, heads, P:2 * P], ALU.add).then_inc(scores_out, 1)
                        dve.wait_ge(scores_done, 4 * turn + 2)
                        nc.vector.tensor_tensor(s_a[:, :, 0:N_META], heads4(ps[:, 7, 0:GROUP * N_META]),
                                                bias[:, heads, P - N_META:P], ALU.add).then_inc(scores_out, 1)
                        dve.wait_ge(scores_out, 4 * turn + 2)
                        minus_max(s_a[:], slice(0, 4), heads)
                    if c in (1, 2):
                        h = 2 * (c - 1)
                        dve.wait_ge(scores_done, 4 * turn + 2 + c)
                        nc.vector.tensor_tensor(s_b[:, h:h + 2], ps[:, 5 + c, :].rearrange("p (h k) -> p h k", h=2),
                                                bias[:, bass.ds(g * GROUP + h, 2), :], ALU.add).then_inc(scores_out, 1)
                    if c == 2:
                        dve.wait_ge(scores_out, 4 * turn + 4)
                        minus_max(s_b[:], slice(4, 8), heads)
                    if c == 3:
                        dve.wait_ge(exp_done, 2 * turn + 1)
                        normalise(s_a[:], slice(0, 4))
                    if last_turn and c == 4:
                        dve.wait_ge(dec_scores, 1)
                        nc.vector.tensor_copy(sdt[:], ps[:, 6, 0:P]).then_inc(dec_scores_out, 1)
                        nc.vector.tensor_copy(sd_own[:], ps[0:ND, 7, 0:P]).then_inc(dec_scores_out, 1)
                    if c == 5:
                        dve.wait_ge(exp_done, 2 * turn + 2)
                        normalise(s_b[:], slice(4, 8))
                    if c == 6:
                        dve.wait_ge(probs_t, 4 * turn + 2)
                        nc.vector.tensor_copy(pt_m[:], ps[0:N_META, 7, :]).then_inc(probs_t_dve, 1)
                    if c == 8:
                        dve.wait_ge(probs_t, 4 * turn + 4)
                        nc.vector.tensor_copy(pt[:, 2, :], ps[:, 7, :]).then_inc(probs_t_dve, 1)
                    if last_turn and c == 9:
                        dve.wait_ge(dec_rows, 1)
                        nc.vector.tensor_copy(sd[:], ps[:, 6, 0:P + 1]).then_inc(dec_rows_out, 1)
                        own.link(nc.vector.tensor_tensor(sd_own8[:], ps[:, 6, 256:256 + ND], masks[:, 0:ND], ALU.mult))
                        own.link(nc.vector.tensor_reduce(dstat[:, 5:6], sd_own8[:], AX.X, ALU.add))
                        nc.vector.tensor_tensor(sd[:, P:P + 1], sd[:, P:P + 1], dstat[:, 5:6], ALU.add).then_inc(dec_rows_out, 1)
                        dve.wait_ge(dec_rows_out, 2)
                        own.link(nc.vector.tensor_reduce(dstat[:, 0:1], sd[:], AX.X, ALU.max))
                        nc.vector.scalar_tensor_tensor(out=dstat[:, 0:1], in0=dstat[:, 0:1], scalar=-1.0, in1=dstat[:, 6:7],
                                                       op0=ALU.mult, op1=ALU.min).then_inc(dec_nmax, 1)
                    if last_turn and c == 11:
                        dve.wait_ge(dec_exp, 1)
                        own.link(nc.vector.tensor_tensor(dstat[:, 4:5], dstat[:, 2:3], dstat[:, 3:4], ALU.add))
                        own.link(nc.vector.reciprocal(dstat[:, 4:5], dstat[:, 4:5]))
                        nc.vector.tensor_scalar(sd[:], sd[:], dstat[:, 4:5], None, ALU.mult).then_inc(dec_probs, 1)
                        dve.wait_ge(dec_probs, 1)
                        nc.vector.tensor_scalar(sd_own8[:], masks[:, 0:ND], sd[:, P:P + 1], None, ALU.mult).then_inc(dec_probs, 1)
                    if last_turn and c == 12:
                        dve.wait_ge(dec_pt, 1)
                        nc.vector.tensor_copy(pd[:], ps[:, 6, 0:P]).then_inc(dec_pt_out, 1)
                        nc.vector.tensor_copy(pd_own[:], ps[0:ND, 6, P:2 * P]).then_inc(dec_pt_out, 1)
                    if last_turn and c == 13:
                        dve.wait_ge(op_hi_ready, KT + 1)
                        nc.vector.tensor_tensor(op_lo[:, 8:14, WANTED], convT[:, 0:6, :], op_hi[:, 8:14, WANTED].bitcast(F32),
                                                ALU.subtract).then_inc(op_lo_ready, 1)

            with dve.Fori(0, CONV_TURNS - 1) as turn:
                own.begin(turn, TURN_LINKS)
                conv_turn(turn, turn * -1 + (KVH - 1), False)
                own.end(CONV_TURNS - 1)
            conv_turn(CONV_TURNS - 1, 0, True)
            dve.wait_ge(dec_pv, 2)
            for a in range(2):
                for e in range(2):
                    src = ps[HEAD * a:HEAD * a + HEAD, 7, 0:P].rearrange("p (r b h) -> p r h b", r=2, h=8)[:, :, 4 * a + e:4 * a + 4:2, :]
                    dst = zT[HEAD * e:HEAD * e + HEAD, 0:8, NP:N].rearrange("p (r a i) b -> p r a i b", r=2, a=2)[:, :, a]
                    nc.vector.tensor_copy(dst, src).then_inc(dec_pv_out, 1)
            dve.wait_ge(op_hi_ready, KT + 2)
            nc.vector.tensor_tensor(op_lo[:, 0:8, WANTED], zT[:, 0:8, WANTED], op_hi[:, 0:8, WANTED].bitcast(F32), ALU.subtract).then_inc(op_lo_ready, 1)

            for c in range(4 * NC - 1):
                if c == 3:
                    dve.wait_ge(op_hi_ready, KT + 3)
                    nc.vector.tensor_tensor(op_lo[:, 14:16, WANTED], convT[:, 6:8, :], op_hi[:, 14:16, WANTED].bitcast(F32),
                                            ALU.subtract).then_inc(op_lo_ready, 1)
                split(C_OUT + c + RING, c % RING, 1024)

            def invert(k, src, dst):
                dve.wait_ge(root_ready, k)
                nc.vector.reciprocal(dst, src).then_inc(rms_inverse, 1)
                dve.wait_ge(rms_inverse, k)

            invert(1, root[:], inv[:])
            dve.wait_ge(mix_out, 4)

            def scale_pair(n):
                if n < NC:
                    k = K_ORDER[2 * n]
                    if n >= 2:
                        dve.wait_ge(resid_ready, n - 1)
                    nc.vector.tensor_tensor(tmp[:, n % 2], mixT[:, k:k + 2, :], each(inv[:], [P, 2, M]), ALU.mult).then_inc(scaled, 1)

            def low_pair(n):
                for i in (2 * n, 2 * n + 1):
                    low_half(i, K_ORDER[i])

            def scale_out(dst, bank, ready, c, turn):
                dve.wait_ge(chunk_used, RING + C_FF + c + 1 + turn * (2 * NC))
                nc.vector.tensor_tensor(dst[:], ps[:, bank:bank + NB, 0:M], each(rstd[:, 0:M], [P, NB, M]), ALU.mult).then_inc(ready, 1)

            def ffn_turn(turn, first):
                for c in range(2 * NC):
                    if first and LEAD + c <= NC:
                        low_pair(LEAD + c - 1)
                        scale_pair(LEAD + c + 1)
                    split(C_FF + c + RING, c % RING, 1024, turn * (2 * NC))
                    if c == (NC + 1 if first else NC - 1):
                        if first:
                            invert(2, acc4[:, 2, :], rstd[:, 0:M])
                        else:
                            dve.wait_ge(hid_lo, turn)
                        scale_out(gate, 0, gate_ready, NC - 1, turn)
                    if c == 2 * NC - 1:
                        dve.wait_ge(swish_ready, turn + 1)
                        scale_out(up, NB, up_ready, c, turn)

            scale_pair(0)
            scale_pair(1)
            split(C_FF + RING - 1, RING - 1, 1024)
            low_pair(0)
            for n in range(2, LEAD):
                scale_pair(n)
                low_pair(n - 1)
            scale_pair(LEAD)
            ffn_turn(0, True)
            with dve.Fori(1, FF_TURNS) as turn:
                ffn_turn(turn, False)

            with dve.Fori(0, (4 * DC - RING) // RING) as turn:
                for c in range(RING):
                    split(C_DOWN + c + RING, c, 1024, turn * RING)
            invert(3, y_root[:], rstd[:, 0:M])
            dve.wait_ge(y_out, 4)

            for q in range(4):
                for half in range(2):
                    pair = slice(NB * q + 2 * half, NB * q + 2 * half + 2)
                    nc.vector.tensor_tensor(yT[:, pair, :], yT[:, pair, :], each(rstd[:, 0:M], [P, 2, M]), ALU.mult).then_inc(y_scaled, 1)
                dve.wait_ge(y_scaled, 2 * q + 2)
                nc.vector.tensor_tensor(yT[:, pair, :], yT[:, pair, :], resid[:, pair, WANTED], ALU.add).then_inc(y_ready_dve, 1)
            dve.wait_ge(y_ready_pool, 4)
            dve.wait_ge(y_ready_dve, 4)
            nc.vector.tensor_copy(dec_y[:], yT[:, :, SEQ:M]).then_inc(dec_y_ready, 1)
            dve.wait_ge(yt_done, 9)
            nc.vector.tensor_copy(dec_rows_y[:], ps[:, 0, 0:P]).then_inc(yt_dve, 1)


def shape_constants():
    import math
    import numpy as np
    squares = np.stack([np.eye(P), np.eye(P)[::-1]]).astype(np.float32)
    d = 255 - np.arange(BIAS_N)
    exact = BUCKETS // 2
    ratio = np.maximum(d, 1).astype(np.float32) / np.float32(exact)
    far = exact + (np.log(ratio) / np.float32(math.log(WINDOW / exact)) * np.float32(BUCKETS - exact)).astype(np.int32)
    bucket = np.where(d < exact, d, np.minimum(far, BUCKETS - 1))
    onehot = np.zeros((BUCKETS + 1, BIAS_N), np.float32)
    for n in range(BIAS_N):
        if 0 <= d[n] <= WINDOW:
            onehot[bucket[n], n] = 1.0
        else:
            onehot[BUCKETS, n] = MASKED
    row = np.arange(P)[:, None]
    row_masks = np.concatenate([row // HEADS == np.arange(ND), row % HEADS == np.arange(HEADS)],
                               axis=1).astype(np.float32)
    return dict(squares=squares, onehot=onehot, row_masks=row_masks)


def kernel(x_prompt, x_sample, cache_k, cache_v, state_conv, meta_tokens, rel_bias, w_in, conv_w,
           attn_sinks, w_out, norm_pre_mix, norm_post_mix, norm_pre_ffn, norm_post_ffn, w_gate,
           w_up, w_down):
    import numpy as np
    import concourse.bacc as _bacc
    from concourse.bass_utils import run_bass_kernel_spmd as _run

    inputs = dict(x_prompt=x_prompt, x_sample=x_sample, cache_k=cache_k, cache_v=cache_v,
                  state_conv=state_conv, meta_tokens=meta_tokens, rel_bias=rel_bias, w_in=w_in,
                  conv_w=conv_w, attn_sinks=attn_sinks, w_out=w_out, norm_pre_mix=norm_pre_mix,
                  norm_post_mix=norm_post_mix, norm_pre_ffn=norm_pre_ffn,
                  norm_post_ffn=norm_post_ffn, w_gate=w_gate, w_up=w_up, w_down=w_down)
    inputs.update(shape_constants())
    outputs = dict(y_prompt=(1, SEQ, D), y_sample=(ND, 1, D),
                   k_prompt=(1, 1, WINDOW, KVH, HEAD), v_prompt=(1, 1, WINDOW, KVH, HEAD),
                   conv_prompt=(1, 1, 2, CONV),
                   k_sample=(1, ND, WINDOW, KVH, HEAD), v_sample=(1, ND, WINDOW, KVH, HEAD),
                   conv_sample=(1, ND, 2, CONV))
    nc = _bacc.Bacc("TRN2", target_bir_lowering=False, num_devices=1, dynamic_dma_scratch_size=1024)
    arrays, args = {}, {}
    for name, value in inputs.items():
        arrays[f"in_{name}"] = np.ascontiguousarray(value)
        args[name] = nc.dram_tensor(f"in_{name}", arrays[f"in_{name}"].shape, F32, kind="ExternalInput").ap()
    for name, shape in outputs.items():
        args[name] = nc.dram_tensor(f"out_{name}", shape, F32, kind="ExternalOutput").ap()
    args["bias_rows"] = nc.dram_tensor("bias_rows", (HEADS, BIAS_N), F32, kind="Internal").ap()
    mixer_kernel(nc, **args)
    r = _run(nc, [arrays], core_ids=[0])
    return tuple(r.results[0][f"out_{name}"] for name in outputs)
```
